# Optimizing a Trainium2 kernel written in Bass

```python
import math
import jax, jax.numpy as jnp
from jax import lax
import numpy as np

D_MODEL = 1024
BATCH = 1
SEQ = 512
DEPTH = 2

PLE_DIM = 256
Q_BLOCK = 128
RNN_WIDTH = 512
RNN_BLOCKS = 8
CONV_WIDTH = 4
LRU_C = 8.0
DSA_HEADS = 8
DSA_HEAD_DIM = 64
IDX_HEADS = 4
IDX_DIM = 64
DSA_TOPK_MAX = 256
MLA_HEADS = 16
MLA_Q_LORA = 512
MLA_KV_LORA = 256
MLA_NOPE = 64
MLA_ROPE = 32
MLA_V = 64
ROPE_BASE = 10000.0
D_FF = 4 * D_MODEL
DN_ALPHA = (2 * DEPTH) ** 0.25
DN_BETA = (8 * DEPTH) ** -0.25
LN_EPS = 1e-5
RMS_EPS = 1e-6
N_EVEN = (DEPTH + 1) // 2
N_ODD = DEPTH // 2
EVEN_SPLITS = (RNN_WIDTH, RNN_WIDTH, DSA_HEADS * DSA_HEAD_DIM, DSA_HEAD_DIM, DSA_HEAD_DIM,
               IDX_HEADS * IDX_DIM, IDX_DIM, IDX_HEADS)
EVEN_IN = sum(EVEN_SPLITS)
EVEN_MIX = RNN_WIDTH + DSA_HEADS * DSA_HEAD_DIM
MLA_DOWN = MLA_Q_LORA + MLA_KV_LORA + MLA_ROPE
MLA_MIX = MLA_HEADS * MLA_V


def layer_norm(x, g, b):
    xf = x.astype(jnp.float32)
    mu = jnp.mean(xf, axis=-1, keepdims=True)
    var = jnp.mean(jnp.square(xf - mu), axis=-1, keepdims=True)
    y = (xf - mu) * lax.rsqrt(var + LN_EPS) * g.astype(jnp.float32) + b.astype(jnp.float32)
    return y.astype(x.dtype)

def rms_norm(x, g):
    xf = x.astype(jnp.float32)
    y = xf * lax.rsqrt(jnp.mean(jnp.square(xf), axis=-1, keepdims=True) + RMS_EPS)
    return (y * g.astype(jnp.float32)).astype(x.dtype)

def causal_depthwise_conv(x, w, b):
    c = x.shape[-1]
    y = lax.conv_general_dilated(x, w[:, None, :], window_strides=(1,), padding=[(CONV_WIDTH - 1, 0)],
                                 dimension_numbers=("NWC", "WIO", "NWC"), feature_group_count=c)
    return y + b

def rg_lru(x, w_a, b_a, w_x, b_x, lam):
    bsz, s, c = x.shape
    xb = x.reshape(bsz, s, RNN_BLOCKS, c // RNN_BLOCKS)
    r = jax.nn.sigmoid(jnp.einsum("bsnc,ncd->bsnd", xb, w_a).reshape(bsz, s, c) + b_a)
    i = jax.nn.sigmoid(jnp.einsum("bsnc,ncd->bsnd", xb, w_x).reshape(bsz, s, c) + b_x)
    log_a = -LRU_C * r.astype(jnp.float32) * jax.nn.softplus(-lam.astype(jnp.float32))
    a = jnp.exp(log_a)
    u = jnp.sqrt(-jnp.expm1(2.0 * log_a)) * (i * x).astype(jnp.float32)

    def combine(left, right):
        a1, b1 = left
        a2, b2 = right
        return a1 * a2, a2 * b1 + b2

    _, h = lax.associative_scan(combine, (a, u), axis=1)
    return h.astype(x.dtype)

def alibi_slopes(n):
    return jnp.exp2(-8.0 * (jnp.arange(n, dtype=jnp.float32) + 1.0) / n)

def rope(x, cos, sin):
    half = x.shape[-1] // 2
    x1, x2 = x[..., :half], x[..., half:]
    return jnp.concatenate([x1 * cos - x2 * sin, x2 * cos + x1 * sin], axis=-1)

def to_blocks(a, nb):
    a = a.reshape((a.shape[0], nb, Q_BLOCK) + a.shape[2:])
    return jnp.moveaxis(a, 1, 0)

def from_blocks(o):
    o = jnp.moveaxis(o, 0, 1)
    return o.reshape((o.shape[0], o.shape[1] * o.shape[2]) + o.shape[3:])

def gather_rows(src, idx):
    return jax.vmap(lambda sb, ib: sb[ib])(src, idx)

def dsa_attention(q, k, v, iq, ik, iw):
    bsz, s = q.shape[:2]
    nb = s // Q_BLOCK
    topk = min(DSA_TOPK_MAX, s // 4)
    slopes = alibi_slopes(DSA_HEADS)
    key_pos = jnp.arange(s, dtype=jnp.int32)
    iw = iw.astype(jnp.float32) * (IDX_HEADS ** -0.5 * IDX_DIM ** -0.5)

    def block(args):
        qb, iqb, iwb, t0 = args
        qpos = t0 + jnp.arange(Q_BLOCK, dtype=jnp.int32)
        dots = jnp.einsum("bthd,bsd->bths", iqb, ik).astype(jnp.float32)
        isc = jnp.einsum("bths,bth->bts", jax.nn.relu(dots), iwb)
        causal = key_pos[None, :] <= qpos[:, None]
        isc = jnp.where(causal[None], isc, -jnp.inf)
        _, idx = lax.top_k(isc, topk)
        ksel = gather_rows(k, idx)
        vsel = gather_rows(v, idx)
        logits = jnp.einsum("bthd,btkd->bthk", qb, ksel).astype(jnp.float32) * (DSA_HEAD_DIM ** -0.5)
        dist = qpos[None, :, None] - idx
        logits = logits - slopes[None, None, :, None] * dist.astype(jnp.float32)[:, :, None, :]
        logits = jnp.where((dist >= 0)[:, :, None, :], logits, -jnp.inf)
        probs = jax.nn.softmax(logits, axis=-1).astype(v.dtype)
        return jnp.einsum("bthk,btkd->bthd", probs, vsel)

    starts = jnp.arange(nb, dtype=jnp.int32) * Q_BLOCK
    out = lax.map(block, (to_blocks(q, nb), to_blocks(iq, nb), to_blocks(iw, nb), starts))
    return from_blocks(out)

def mla_attention(q, k, v):
    bsz, s = q.shape[:2]
    nb = s // Q_BLOCK
    scale = q.shape[-1] ** -0.5
    key_pos = jnp.arange(s, dtype=jnp.int32)

    def block(args):
        qb, t0 = args
        qpos = t0 + jnp.arange(Q_BLOCK, dtype=jnp.int32)
        logits = jnp.einsum("bthd,bshd->bhts", qb, k).astype(jnp.float32) * scale
        causal = key_pos[None, :] <= qpos[:, None]
        logits = jnp.where(causal[None, None], logits, -jnp.inf)
        probs = jax.nn.softmax(logits, axis=-1).astype(v.dtype)
        return jnp.einsum("bhts,bshd->bthd", probs, v)

    starts = jnp.arange(nb, dtype=jnp.int32) * Q_BLOCK
    out = lax.map(block, (to_blocks(q, nb), starts))
    return from_blocks(out)

def hybrid_mixer(x, w_in, conv_w, conv_b, ga_w, ga_b, gx_w, gx_b, lam, w_out):
    bsz, s, _ = x.shape
    proj = x @ w_in
    split_points = np.cumsum(EVEN_SPLITS)[:-1].tolist()
    xr, yr, q, k, v, iq, ik, iw = jnp.split(proj, split_points, axis=-1)
    xr = causal_depthwise_conv(xr, conv_w, conv_b)
    rec = rg_lru(xr, ga_w, ga_b, gx_w, gx_b, lam) * jax.nn.gelu(yr)
    att = dsa_attention(q.reshape(bsz, s, DSA_HEADS, DSA_HEAD_DIM), k, v,
                        iq.reshape(bsz, s, IDX_HEADS, IDX_DIM), ik, iw)
    mixed = jnp.concatenate([rec, att.reshape(bsz, s, DSA_HEADS * DSA_HEAD_DIM)], axis=-1)
    return mixed @ w_out

def mla_mixer(x, w_down, q_norm, kv_norm, w_uq, w_ukv, w_out):
    bsz, s, _ = x.shape
    down = x @ w_down
    cq, ckv, kr = jnp.split(down, [MLA_Q_LORA, MLA_Q_LORA + MLA_KV_LORA], axis=-1)
    q = (rms_norm(cq, q_norm) @ w_uq).reshape(bsz, s, MLA_HEADS, MLA_NOPE + MLA_ROPE)
    kv = (rms_norm(ckv, kv_norm) @ w_ukv).reshape(bsz, s, MLA_HEADS, MLA_NOPE + MLA_V)
    q_nope, q_rope = q[..., :MLA_NOPE], q[..., MLA_NOPE:]
    k_nope, v = kv[..., :MLA_NOPE], kv[..., MLA_NOPE:]
    pos = jnp.arange(s, dtype=jnp.float32)
    freq = ROPE_BASE ** (-jnp.arange(0, MLA_ROPE, 2, dtype=jnp.float32) / MLA_ROPE)
    ang = pos[:, None] * freq[None, :]
    cos = jnp.cos(ang).astype(x.dtype)
    sin = jnp.sin(ang).astype(x.dtype)
    q_rope = rope(q_rope, cos[:, None, :], sin[:, None, :])
    k_rope = rope(kr, cos, sin)
    qf = jnp.concatenate([q_nope, q_rope], axis=-1)
    kf = jnp.concatenate([k_nope, jnp.broadcast_to(k_rope[:, :, None, :], (bsz, s, MLA_HEADS, MLA_ROPE))], axis=-1)
    o = mla_attention(qf, kf, v)
    return o.reshape(bsz, s, MLA_MIX) @ w_out

def first_inputs(seed: int = 0) -> dict:
    key = jax.random.key(seed)
    ks = jax.random.split(key, 32)

    def nrm(k, shape, scale):
        return jax.random.normal(k, shape, jnp.float32) * scale

    u = jax.random.uniform(ks[12], (N_EVEN, RNN_WIDTH), jnp.float32, 0.9, 0.999)
    sig = u ** (1.0 / LRU_C)
    lam = jnp.log(sig) - jnp.log1p(-sig)
    bw = RNN_WIDTH // RNN_BLOCKS
    return {
        "x": nrm(ks[0], (BATCH, SEQ, D_MODEL), 1.0),
        "p": nrm(ks[1], (DEPTH, BATCH, SEQ, PLE_DIM), 1.0),
        "ln1_g": 1.0 + nrm(ks[2], (DEPTH, D_MODEL), 0.02),
        "ln1_b": nrm(ks[3], (DEPTH, D_MODEL), 0.02),
        "ln2_g": 1.0 + nrm(ks[4], (DEPTH, D_MODEL), 0.02),
        "ln2_b": nrm(ks[5], (DEPTH, D_MODEL), 0.02),
        "mlp_w1": nrm(ks[6], (DEPTH, D_MODEL, D_FF), D_MODEL ** -0.5),
        "mlp_w2": nrm(ks[7], (DEPTH, D_FF, D_MODEL), DN_BETA * D_FF ** -0.5),
        "ple_w_proj": nrm(ks[8], (DEPTH, PLE_DIM, D_MODEL), DN_BETA * PLE_DIM ** -0.5),
        "ple_w_gate": nrm(ks[9], (DEPTH, D_MODEL, D_MODEL), D_MODEL ** -0.5),
        "hy_w_in": nrm(ks[10], (N_EVEN, D_MODEL, EVEN_IN), D_MODEL ** -0.5),
        "hy_conv_w": nrm(ks[11], (N_EVEN, CONV_WIDTH, RNN_WIDTH), CONV_WIDTH ** -0.5),
        "hy_conv_b": nrm(ks[13], (N_EVEN, RNN_WIDTH), 0.01),
        "hy_ga_w": nrm(ks[14], (N_EVEN, RNN_BLOCKS, bw, bw), bw ** -0.5),
        "hy_ga_b": nrm(ks[15], (N_EVEN, RNN_WIDTH), 0.01),
        "hy_gx_w": nrm(ks[16], (N_EVEN, RNN_BLOCKS, bw, bw), bw ** -0.5),
        "hy_gx_b": nrm(ks[17], (N_EVEN, RNN_WIDTH), 0.01),
        "hy_lambda": lam,
        "hy_w_out": nrm(ks[18], (N_EVEN, EVEN_MIX, D_MODEL), DN_BETA * EVEN_MIX ** -0.5),
        "mla_w_down": nrm(ks[19], (N_ODD, D_MODEL, MLA_DOWN), D_MODEL ** -0.5),
        "mla_q_norm": 1.0 + nrm(ks[20], (N_ODD, MLA_Q_LORA), 0.02),
        "mla_kv_norm": 1.0 + nrm(ks[21], (N_ODD, MLA_KV_LORA), 0.02),
        "mla_w_uq": nrm(ks[22], (N_ODD, MLA_Q_LORA, MLA_HEADS * (MLA_NOPE + MLA_ROPE)), MLA_Q_LORA ** -0.5),
        "mla_w_ukv": nrm(ks[23], (N_ODD, MLA_KV_LORA, MLA_HEADS * (MLA_NOPE + MLA_V)), MLA_KV_LORA ** -0.5),
        "mla_w_out": nrm(ks[24], (N_ODD, MLA_MIX, D_MODEL), DN_BETA * MLA_MIX ** -0.5),
    }

def first_block(x, p, ln1_g, ln1_b, ln2_g, ln2_b, mlp_w1, mlp_w2, ple_w_proj, ple_w_gate,
              hy_w_in, hy_conv_w, hy_conv_b, hy_ga_w, hy_ga_b, hy_gx_w, hy_gx_b, hy_lambda, hy_w_out,
              mla_w_down, mla_q_norm, mla_kv_norm, mla_w_uq, mla_w_ukv, mla_w_out):
    for i in range(DEPTH):
        j = i // 2
        if i % 2 == 0:
            m = hybrid_mixer(x, hy_w_in[j], hy_conv_w[j], hy_conv_b[j], hy_ga_w[j], hy_ga_b[j],
                             hy_gx_w[j], hy_gx_b[j], hy_lambda[j], hy_w_out[j])
        else:
            m = mla_mixer(x, mla_w_down[j], mla_q_norm[j], mla_kv_norm[j], mla_w_uq[j],
                          mla_w_ukv[j], mla_w_out[j])
        h = layer_norm(DN_ALPHA * x + m, ln1_g[i], ln1_b[i])
        f = jnp.square(jax.nn.relu(h @ mlp_w1[i])) @ mlp_w2[i]
        e = jax.nn.sigmoid(h @ ple_w_gate[i]) * (p[i] @ ple_w_proj[i])
        x = layer_norm(DN_ALPHA * h + f + e, ln2_g[i], ln2_b[i])
    return x


CTX_LEN = 256
GRID_W = 64
BLOCK = 128
WINDOW = 128
EPS = 1e-6
N_MOD = 6
D_FF_2 = 4 * D_MODEL

A_HEADS = 4
A_HEAD_DIM = D_MODEL // 8
A_WIDTH = A_HEADS * A_HEAD_DIM
A_GATES = 4 * A_HEADS
B_HEADS = 8
B_KV_HEADS = 2
B_HEAD_DIM = D_MODEL // 16
B_WIDTH = B_HEADS * B_HEAD_DIM
B_KV_WIDTH = B_KV_HEADS * B_HEAD_DIM
AB_IN = 4 * A_WIDTH + A_GATES + B_WIDTH + 2 * B_KV_WIDTH
AB_OUT = A_WIDTH + B_WIDTH
C_HEADS = 8
C_KV_HEADS = 2
C_HEAD_DIM = D_MODEL // 8
C_WIDTH = C_HEADS * C_HEAD_DIM
C_KV_WIDTH = C_KV_HEADS * C_HEAD_DIM
C_IN = C_WIDTH + 2 * C_KV_WIDTH


def rms_norm_2(x, g):
    xf = x.astype(jnp.float32)
    y = xf * lax.rsqrt(jnp.mean(xf * xf, axis=-1, keepdims=True) + EPS)
    return (y * g.astype(jnp.float32)).astype(x.dtype)

def modulate(x, g, mod, i):
    return rms_norm_2(x, g) * (1 + mod[:, :, i + 1]) + mod[:, :, i]

def sq_relu_mlp(h, w1, w2):
    return jnp.square(jax.nn.relu(h @ w1)) @ w2

def axial_rope_tables(n_tokens, head_dim):
    rows = n_tokens // GRID_W
    row = jnp.broadcast_to(jnp.arange(rows)[:, None], (rows, GRID_W)).reshape(n_tokens).astype(jnp.float32)
    col = jnp.broadcast_to(jnp.arange(GRID_W)[None, :], (rows, GRID_W)).reshape(n_tokens).astype(jnp.float32)
    pairs_per_axis = head_dim // 4
    inv_freq = ROPE_BASE ** (-jnp.arange(pairs_per_axis, dtype=jnp.float32) / pairs_per_axis)
    ang = jnp.concatenate([row[:, None] * inv_freq, col[:, None] * inv_freq], axis=-1)
    return jnp.cos(ang), jnp.sin(ang)

def apply_rope(x, cos, sin):
    half = x.shape[-1] // 2
    xf = x.astype(jnp.float32)
    x1, x2 = xf[..., :half], xf[..., half:]
    cs, sn = cos[:, None, :], sin[:, None, :]
    return jnp.concatenate([x1 * cs - x2 * sn, x2 * cs + x1 * sn], axis=-1).astype(x.dtype)

def gqa_attend(q, k, v, sink=None):
    b, tq, hq, d = q.shape
    hkv = k.shape[2]
    g = hq // hkv
    s = jnp.einsum('bqhgd,bkhd->bhgqk', q.reshape(b, tq, hkv, g, d), k).astype(jnp.float32) * d ** -0.5
    if sink is None:
        p = jax.nn.softmax(s, axis=-1)
    else:
        s_sink = jnp.broadcast_to(sink.astype(jnp.float32).reshape(1, hkv, g, 1, 1), s.shape[:-1] + (1,))
        p = jax.nn.softmax(jnp.concatenate([s, s_sink], axis=-1), axis=-1)[..., :-1]
    o = jnp.einsum('bhgqk,bkhd->bqhgd', p.astype(v.dtype), v)
    return o.reshape(b, tq, hq * d)

def banded_window_attention(q, k, v, k_ctx, v_ctx, sink):
    b, t, hq, d = q.shape
    hkv = k.shape[2]
    g = hq // hkv
    nb = t // BLOCK
    n_ctx = k_ctx.shape[1]
    nw = 3 * BLOCK
    scale = d ** -0.5
    qb = jnp.moveaxis(q.reshape(b, nb, BLOCK, hkv, g, d), 1, 0)

    def band(a):
        a = jnp.pad(a, ((0, 0), (BLOCK, BLOCK), (0, 0), (0, 0))).reshape(b, nb + 2, BLOCK, hkv, d)
        a = jnp.concatenate([a[:, :-2], a[:, 1:-1], a[:, 2:]], axis=2)
        return jnp.moveaxis(a, 1, 0)

    kw, vw = band(k), band(v)
    qpos = jnp.arange(nb)[:, None, None] * BLOCK + jnp.arange(BLOCK)[None, :, None]
    kpos = (jnp.arange(nb)[:, None, None] - 1) * BLOCK + jnp.arange(nw)[None, None, :]
    valid = (jnp.abs(kpos - qpos) <= WINDOW) & (kpos >= 0) & (kpos < t)
    sink_l = sink.astype(jnp.float32).reshape(1, hkv, g, 1, 1)

    def one_block(args):
        qn, kn, vn, valid_n = args
        s_win = jnp.einsum('bqhgd,bkhd->bhgqk', qn, kn).astype(jnp.float32) * scale
        s_win = jnp.where(valid_n, s_win, -jnp.inf)
        s_ctx = jnp.einsum('bqhgd,bchd->bhgqc', qn, k_ctx).astype(jnp.float32) * scale
        s_sink = jnp.broadcast_to(sink_l, s_win.shape[:-1] + (1,))
        p = jax.nn.softmax(jnp.concatenate([s_win, s_ctx, s_sink], axis=-1), axis=-1).astype(v.dtype)
        o = (jnp.einsum('bhgqk,bkhd->bqhgd', p[..., :nw], vn)
             + jnp.einsum('bhgqc,bchd->bqhgd', p[..., nw:nw + n_ctx], v_ctx))
        return o.reshape(b, BLOCK, hq * d)

    o = lax.map(one_block, (qb, kw, vw, valid))
    return jnp.moveaxis(o, 0, 1).reshape(b, t, hq * d)

def mlstm_dir(q, k, v, log_i, log_f, state):
    n_chunks = q.shape[2] // BLOCK

    def to_chunks(a):
        a = a.reshape(a.shape[:2] + (n_chunks, BLOCK) + a.shape[3:])
        return jnp.moveaxis(a, 2, 0)

    lower = jnp.tril(jnp.ones((BLOCK, BLOCK), dtype=bool))

    def step(carry, inp):
        c_mat, n_vec, m = carry
        qc, kc, vc, ic, fc = inp
        bcum = jnp.cumsum(fc, axis=-1)
        d_log = jnp.where(lower, bcum[..., :, None] - bcum[..., None, :] + ic[..., None, :], -jnp.inf)
        inter_log = bcum + m[..., None]
        m_t = jnp.maximum(inter_log, jnp.max(d_log, axis=-1))
        inter_w = jnp.exp(inter_log - m_t)
        s = jnp.einsum('bhtd,bhsd->bhts', qc, kc) * jnp.exp(d_log - m_t[..., None])
        num = inter_w[..., None] * jnp.einsum('bhtd,bhde->bhte', qc, c_mat) + jnp.einsum('bhts,bhse->bhte', s, vc)
        den = inter_w * jnp.einsum('bhtd,bhd->bht', qc, n_vec) + jnp.sum(s, axis=-1)
        h = num / jnp.maximum(jnp.abs(den), jnp.exp(-m_t))[..., None]
        b_last = bcum[..., -1]
        w_log = b_last[..., None] - bcum + ic
        m_new = jnp.maximum(b_last + m, jnp.max(w_log, axis=-1))
        carry_w = jnp.exp(b_last + m - m_new)
        w = jnp.exp(w_log - m_new[..., None])
        c_new = carry_w[..., None, None] * c_mat + jnp.einsum('bhs,bhsd,bhse->bhde', w, kc, vc)
        n_new = carry_w[..., None] * n_vec + jnp.einsum('bhs,bhsd->bhd', w, kc)
        return (c_new, n_new, m_new), h

    state, h = lax.scan(step, state, (to_chunks(q), to_chunks(k), to_chunks(v), to_chunks(log_i), to_chunks(log_f)))
    h = jnp.moveaxis(h, 0, 2)
    return h.reshape(h.shape[:2] + (-1, h.shape[-1])), state

def mlstm_bidir(q, k, v, gates, state_f, state_b):
    li_f, lf_f, li_b, lf_b = gates
    h_f, st_f = mlstm_dir(q, k, v, li_f, lf_f, state_f)
    flip = lambda a: jnp.flip(a, axis=2)
    h_b, st_b = mlstm_dir(flip(q), flip(k), flip(v), flip(li_b), flip(lf_b), state_b)
    return h_f + flip(h_b), st_f, st_b

def ab_mixer(h_ctx, h_lat, w_in, gate_b, a_norm_g, q_norm_g, k_norm_g, sink, w_out, need_ctx):
    batch = h_lat.shape[0]
    sizes = [A_WIDTH] * 4 + [A_GATES, B_WIDTH, B_KV_WIDTH]
    bounds = [int(s) for s in np.cumsum(sizes)]

    def project(h):
        t = h.shape[1]
        qa, ka, va, oa, ga, qb, kb, vb = jnp.split(h @ w_in, bounds, axis=-1)
        heads_a = lambda a: a.reshape(batch, t, A_HEADS, A_HEAD_DIM).transpose(0, 2, 1, 3).astype(jnp.float32)
        qa, ka, va = heads_a(qa), heads_a(ka) * A_HEAD_DIM ** -0.5, heads_a(va)
        g = (ga + gate_b).astype(jnp.float32).reshape(batch, t, 4, A_HEADS).transpose(2, 0, 3, 1)
        gates = (g[0], jax.nn.log_sigmoid(g[1]), g[2], jax.nn.log_sigmoid(g[3]))
        qb = rms_norm_2(qb.reshape(batch, t, B_HEADS, B_HEAD_DIM), q_norm_g)
        kb = rms_norm_2(kb.reshape(batch, t, B_KV_HEADS, B_HEAD_DIM), k_norm_g)
        vb = vb.reshape(batch, t, B_KV_HEADS, B_HEAD_DIM)
        return (qa, ka, va, gates), oa, (qb, kb, vb)

    def mlstm_out(h, oa):
        h = rms_norm_2(h.transpose(0, 2, 1, 3), a_norm_g.reshape(A_HEADS, A_HEAD_DIM))
        return (h.reshape(h.shape[0], h.shape[1], A_WIDTH) * jax.nn.sigmoid(oa)).astype(oa.dtype)

    a_c, oa_c, (qb_c, kb_c, vb_c) = project(h_ctx)
    a_l, oa_l, (qb_l, kb_l, vb_l) = project(h_lat)
    zero = (jnp.zeros((batch, A_HEADS, A_HEAD_DIM, A_HEAD_DIM), jnp.float32),
            jnp.zeros((batch, A_HEADS, A_HEAD_DIM), jnp.float32),
            jnp.zeros((batch, A_HEADS), jnp.float32))
    ha_c, st_f, st_b = mlstm_bidir(*a_c, zero, zero)
    ha_l, _, _ = mlstm_bidir(*a_l, st_f, st_b)
    cos, sin = axial_rope_tables(h_lat.shape[1], B_HEAD_DIM)
    qb_l, kb_l = apply_rope(qb_l, cos, sin), apply_rope(kb_l, cos, sin)
    ob_l = banded_window_attention(qb_l, kb_l, vb_l, kb_c, vb_c, sink)
    y_lat = jnp.concatenate([mlstm_out(ha_l, oa_l), ob_l.astype(oa_l.dtype)], axis=-1) @ w_out
    y_ctx = None
    if need_ctx:
        ob_c = gqa_attend(qb_c, kb_c, vb_c, sink)
        y_ctx = jnp.concatenate([mlstm_out(ha_c, oa_c), ob_c.astype(oa_c.dtype)], axis=-1) @ w_out
    return y_ctx, y_lat

def c_mixer(h_ctx, h_lat, w_in, q_norm_g, k_norm_g, w_out, need_ctx):
    def project(h):
        b, t, _ = h.shape
        q, k, v = jnp.split(h @ w_in, [C_WIDTH, C_WIDTH + C_KV_WIDTH], axis=-1)
        q = rms_norm_2(q.reshape(b, t, C_HEADS, C_HEAD_DIM), q_norm_g)
        k = rms_norm_2(k.reshape(b, t, C_KV_HEADS, C_HEAD_DIM), k_norm_g)
        return q, k, v.reshape(b, t, C_KV_HEADS, C_HEAD_DIM)

    q_c, k_c, v_c = project(h_ctx)
    q_l, k_l, v_l = project(h_lat)
    b, t = h_lat.shape[:2]
    cos, sin = axial_rope_tables(t, C_HEAD_DIM)
    q_l, k_l = apply_rope(q_l, cos, sin), apply_rope(k_l, cos, sin)
    k_all = jnp.concatenate([k_c, k_l], axis=1)
    v_all = jnp.concatenate([v_c, v_l], axis=1)
    q_blocks = jnp.moveaxis(q_l.reshape(b, t // BLOCK, BLOCK, C_HEADS, C_HEAD_DIM), 1, 0)
    o = lax.map(lambda qb: gqa_attend(qb, k_all, v_all), q_blocks)
    y_lat = jnp.moveaxis(o, 0, 1).reshape(b, t, C_WIDTH) @ w_out
    y_ctx = gqa_attend(q_c, k_c, v_c) @ w_out if need_ctx else None
    return y_ctx, y_lat

def second_inputs(seed: int = 0) -> dict:
    key = jax.random.key(seed)
    ks = jax.random.split(key, 24)
    n_even = (DEPTH + 1) // 2
    n_odd = DEPTH // 2
    f32 = jnp.float32
    nrm = lambda k, shape, scale: jax.random.normal(k, shape, f32) * scale
    gain = lambda k, shape: 1.0 + 0.05 * jax.random.normal(k, shape, f32)
    gate_b = jnp.concatenate([
        nrm(ks[9], (n_even, A_HEADS), 0.1),
        jax.random.uniform(ks[10], (n_even, A_HEADS), f32, 3.0, 6.0),
        nrm(ks[11], (n_even, A_HEADS), 0.1),
        jax.random.uniform(ks[12], (n_even, A_HEADS), f32, 3.0, 6.0)], axis=-1)
    return {
        'x': nrm(ks[0], (BATCH, SEQ, D_MODEL), 1.0),
        'c': nrm(ks[1], (BATCH, D_MODEL), 1.0),
        'ctx': nrm(ks[2], (BATCH, CTX_LEN, D_MODEL), 1.0),
        'c_ctx': nrm(ks[3], (D_MODEL,), 1.0),
        'ada_w': nrm(ks[4], (DEPTH, D_MODEL, N_MOD * D_MODEL), 0.5 * D_MODEL ** -0.5),
        'ada_b': nrm(ks[5], (DEPTH, N_MOD * D_MODEL), 0.02),
        'norm1_g': gain(ks[6], (DEPTH, D_MODEL)),
        'norm2_g': gain(ks[7], (DEPTH, D_MODEL)),
        'ab_w_in': nrm(ks[8], (n_even, D_MODEL, AB_IN), D_MODEL ** -0.5),
        'ab_gate_b': gate_b,
        'mlstm_norm_g': gain(ks[13], (n_even, A_WIDTH)),
        'swa_q_norm_g': gain(ks[14], (n_even, B_HEAD_DIM)),
        'swa_k_norm_g': gain(ks[15], (n_even, B_HEAD_DIM)),
        'swa_sink': nrm(ks[16], (n_even, B_HEADS), 0.5),
        'ab_w_out': nrm(ks[17], (n_even, AB_OUT, D_MODEL), AB_OUT ** -0.5),
        'c_w_in': nrm(ks[18], (n_odd, D_MODEL, C_IN), D_MODEL ** -0.5),
        'c_q_norm_g': gain(ks[19], (n_odd, C_HEAD_DIM)),
        'c_k_norm_g': gain(ks[20], (n_odd, C_HEAD_DIM)),
        'c_w_out': nrm(ks[21], (n_odd, C_WIDTH, D_MODEL), C_WIDTH ** -0.5),
        'mlp_w1': nrm(ks[22], (DEPTH, D_MODEL, D_FF_2), D_MODEL ** -0.5),
        'mlp_w2': nrm(ks[23], (DEPTH, D_FF_2, D_MODEL), D_FF_2 ** -0.5),
    }

def second_block(x, c, ctx, c_ctx, ada_w, ada_b, norm1_g, norm2_g, ab_w_in, ab_gate_b, mlstm_norm_g,
              swa_q_norm_g, swa_k_norm_g, swa_sink, ab_w_out, c_w_in, c_q_norm_g, c_k_norm_g, c_w_out,
              mlp_w1, mlp_w2):
    batch = x.shape[0]
    for layer in range(DEPTH):
        last = layer == DEPTH - 1
        mod_l = (jax.nn.silu(c) @ ada_w[layer] + ada_b[layer]).reshape(batch, 1, N_MOD, D_MODEL)
        mod_c = (jax.nn.silu(c_ctx) @ ada_w[layer] + ada_b[layer]).reshape(1, 1, N_MOD, D_MODEL)
        h_l = modulate(x, norm1_g[layer], mod_l, 0)
        h_c = modulate(ctx, norm1_g[layer], mod_c, 0)
        j = layer // 2
        if layer % 2 == 0:
            y_c, y_l = ab_mixer(h_c, h_l, ab_w_in[j], ab_gate_b[j], mlstm_norm_g[j], swa_q_norm_g[j],
                                swa_k_norm_g[j], swa_sink[j], ab_w_out[j], not last)
        else:
            y_c, y_l = c_mixer(h_c, h_l, c_w_in[j], c_q_norm_g[j], c_k_norm_g[j], c_w_out[j], not last)
        x = x + mod_l[:, :, 2] * y_l
        x = x + mod_l[:, :, 5] * sq_relu_mlp(modulate(x, norm2_g[layer], mod_l, 3), mlp_w1[layer], mlp_w2[layer])
        if not last:
            ctx = ctx + mod_c[:, :, 2] * y_c
            ctx = ctx + mod_c[:, :, 5] * sq_relu_mlp(modulate(ctx, norm2_g[layer], mod_c, 3), mlp_w1[layer], mlp_w2[layer])
    return x


def setup_inputs(seed=0):
    out = dict(first_inputs(seed))
    for name, value in second_inputs(seed + 1).items():
        if name != "x":
            out[name + "_2"] = value
    return out


def reference(
    x, p, ln1_g, ln1_b, ln2_g, ln2_b, mlp_w1, mlp_w2, ple_w_proj, ple_w_gate, hy_w_in,
    hy_conv_w, hy_conv_b, hy_ga_w, hy_ga_b, hy_gx_w, hy_gx_b, hy_lambda, hy_w_out, mla_w_down,
    mla_q_norm, mla_kv_norm, mla_w_uq, mla_w_ukv, mla_w_out, c_2, ctx_2, c_ctx_2, ada_w_2,
    ada_b_2, norm1_g_2, norm2_g_2, ab_w_in_2, ab_gate_b_2, mlstm_norm_g_2, swa_q_norm_g_2,
    swa_k_norm_g_2, swa_sink_2, ab_w_out_2, c_w_in_2, c_q_norm_g_2, c_k_norm_g_2, c_w_out_2,
    mlp_w1_2, mlp_w2_2,
):
    x = first_block(
        x, p, ln1_g, ln1_b, ln2_g, ln2_b, mlp_w1, mlp_w2, ple_w_proj, ple_w_gate, hy_w_in,
        hy_conv_w, hy_conv_b, hy_ga_w, hy_ga_b, hy_gx_w, hy_gx_b, hy_lambda, hy_w_out,
        mla_w_down, mla_q_norm, mla_kv_norm, mla_w_uq, mla_w_ukv, mla_w_out,
    )
    return second_block(
        x, c_2, ctx_2, c_ctx_2, ada_w_2, ada_b_2, norm1_g_2, norm2_g_2, ab_w_in_2, ab_gate_b_2,
        mlstm_norm_g_2, swa_q_norm_g_2, swa_k_norm_g_2, swa_sink_2, ab_w_out_2, c_w_in_2,
        c_q_norm_g_2, c_k_norm_g_2, c_w_out_2, mlp_w1_2, mlp_w2_2,
    )


_drawn_inputs = setup_inputs


def setup_inputs(seed=0):
    import zlib

    import numpy as np

    out = dict(_drawn_inputs(seed))
    spreads = {}
    factors = {'hy_conv_b': 6.707,
     'hy_ga_b': 8.0,
     'hy_gx_b': 8.0,
     'mla_q_norm': 8.0,
     'mla_kv_norm': 8.0,
     'norm1_g_2': 3.348,
     'mlstm_norm_g_2': 8.0,
     'swa_q_norm_g_2': 8.0,
     'swa_k_norm_g_2': 8.0,
     'swa_sink_2': 8.0,
     'c_q_norm_g_2': 8.0,
     'c_k_norm_g_2': 8.0}
    for name, (base, spread) in spreads.items():
        noise = np.random.default_rng([zlib.crc32(name.encode()), seed]).standard_normal(out[name].shape)
        drawn = base * np.exp(spread * noise) if base else spread * noise
        out[name] = __import__('jax').numpy.asarray(drawn.astype(out[name].dtype))
    for name, factor in factors.items():
        out[name] = (out[name] * factor).astype(out[name].dtype)
    return out
```

```python
from contextlib import ExitStack

import concourse.bass as bass
from concourse import mybir

F32 = mybir.dt.float32
ALU = mybir.AluOpType
ACT = mybir.ActivationFunctionType
AX = mybir.AxisListType

P = 128
D = 1024
KD = D // P
LAT, CTX = 512, 256
TOK = LAT + CTX
LT, CT = LAT // P, CTX // P
ALPHA = (2 * 2) ** 0.25
LN_EPS, RMS_EPS = 1e-5, 1e-6
NEG = -1e30
TAKEN = -3e38

RNN = 512
RC = RNN // P
DSA_H, DSA_D, TOPK = 8, 64, 128
IDX_H, IDX_D = 4, 64
MLA_H, NOPE, ROPE, MLA_V = 16, 64, 32, 64
QL, KVL = 512, 256
A_H = 4
B_H, B_KV, B_D = 8, 2, 64
C_H, C_KV = 8, 2
N_MOD = 6
FF = 4 * D
GROUPS = 4
CW = 512
NW = 2
WORK = 30200

CONST_SIZES = [("ident", P), ("ones", P), ("ones64", P), ("rot64", P), ("rot128", P), ("after", P), ("before", P),
               ("dist", LAT), ("pick", 4 * P), ("cosB", LAT), ("sinB", LAT), ("cosC", LAT), ("sinC", LAT),
               ("cosM", LAT), ("sinM", LAT), ("eps", 2)]
CONST = {}
_at = 0
for _name, _n in CONST_SIZES:
    CONST[_name] = (_at, _at + _n)
    _at += _n
NCONST = _at

ROW_SIZES = [("ln1_g", 16), ("ln1_b", 16), ("ln2_g", 16), ("ln2_b", 16), ("conv_w", 16), ("conv_b", 4), ("ga_b", 4),
             ("gx_b", 4), ("lam", 4), ("q_norm", 4), ("kv_norm", 2), ("c", 8), ("c_ctx", 8), ("a_norm", 4),
             ("cq", 1), ("ck", 1), ("bq", 1), ("bk", 1), ("pad", 2),
             ("norm1", 16), ("norm2", 16), ("ada_b", 96)]
ROW = {}
_at = 0
for _name, _n in ROW_SIZES:
    ROW[_name] = _at
    _at += _n
NROW = _at
assert ROW["norm1"] == P and NROW == 2 * P

PLAN_A = [("hy_xr", 4), ("hy_yr", 4), ("hy_q", 4), ("hy_ki", 4), ("hy_v", 1), ("hy_gate", 8), ("idx", 6),
          ("dsa", 4 * DSA_H), ("hy_out", 8), ("ln_m0", 1), ("ln_v0", 1), ("ple_g0", 8), ("ple_p0", 8), ("mlp0", 64),
          ("ln_m1", 1), ("ln_v1", 1),
          ("mla_cq", 4), ("mla_kv", 2), ("mla_kr", 1), ("mla_s", 2), ("uq", 12), ("ukv", 16),
          ("mla", 4 * MLA_H), ("mla_out", 8), ("ln_m2", 1), ("ln_v2", 1), ("ple_g1", 8), ("ple_p1", 8),
          ("mlp1", 64), ("ln_m3", 1), ("ln_v3", 1),
          ("ada", 24),
          ("rms0", 1), ("ab_q", 4), ("ab_k", 4), ("ab_v", 6), ("ab_o", 4), ("ab_qb", 4), ("ab_kb", 2), ("ab_vb", 1),
          ("ab_g", 4), ("ab_n", 6), ("ab_r", 6), ("carry", 1), ("lstm", 48), ("swa", LT * B_H), ("swc", CT * B_H),
          ("ab_out", 8), ("rms1", 1), ("mlp2", 64),
          ("rms2", 1), ("c_q", 8), ("c_k", 2), ("c_v", 2), ("c_n", 10), ("c_r", 10), ("cat", LT * C_H), ("c_out", 8),
          ("rms3", 1), ("mlp3", 64)]
PLAN_B = [("load", 17), ("dsa", 4 * DSA_H), ("dsa_o", 4), ("mla", 4 * MLA_H), ("mla_o", 8), ("ka", 6), ("cols", 1),
          ("lstm", 48), ("hs", 8), ("swa", 6 * B_H), ("swa_o", 4), ("swc", CT * B_H), ("swc_o", 4),
          ("cat", 2 * LT * C_H), ("cat_o", 8), ("out", 8)]


def bases(plan):
    at, base = 0, {}
    for name, n in plan:
        base[name] = at
        at += n
    return base


BASE_A, BASE_B = bases(PLAN_A), bases(PLAN_B)


def build(nc, d, consts, out):
    with ExitStack() as ctx:
        def sb(name, shape):
            return ctx.enter_context(nc.sbuf_tensor(name, shape, F32))

        def sem(name):
            return ctx.enter_context(nc.semaphore(name))

        const = sb("const", [P, NCONST])
        vecT = sb("vecT", [P, NROW])
        small = sb("small", [P, 660])
        xT = sb("xT", [P, KD, TOK])
        pT = sb("pT", [P, 2, 2, LAT])
        mod = sb("mod", [P, 2, N_MOD * KD, 2])
        wbuf = sb("wbuf", [P, NW, 8, CW])
        work = sb("work", [P, WORK])
        psA = ctx.enter_context(nc.psum_tensor("psA", [P, 2, 1024], F32))
        psB = ctx.enter_context(nc.psum_tensor("psB", [P, 2, 512], F32))
        psO = ctx.enter_context(nc.psum_tensor("psO", [P, 1024], F32))

        C = {name: const[:, a:b] for name, (a, b) in CONST.items()}
        ident, ones = C["ident"], C["ones"]
        eps_ln, eps_rms = C["eps"][:, 0:1], C["eps"][:, 1:2]

        def vec(name, j):
            return vecT[:, ROW[name] + j:ROW[name] + j + 1]

        cursor = [0]

        def area(*shape, at=None):
            if at is not None:
                cursor[0] = at
            n = 1
            for s in shape:
                n *= s
            v = work[:, cursor[0]:cursor[0] + n]
            cursor[0] += n
            assert cursor[0] <= WORK, cursor[0]
            if len(shape) == 2:
                return v.rearrange("p (a b) -> p a b", b=shape[1])
            if len(shape) == 3:
                return v.rearrange("p (a b c) -> p a b c", b=shape[1], c=shape[2])
            if len(shape) == 4:
                return v.rearrange("p (a b c e) -> p a b c e", b=shape[1], c=shape[2], e=shape[3])
            return v

        xn, cn, pn, rows = area(LT, D, at=0), area(CT, D), area(2, LT, 256), area(2, P)
        hT, acc, gT = area(KD, TOK, at=0), area(KD, TOK), area(KD, TOK)
        nrm, rstd = area(TOK), area(TOK)
        xpad = area(RC, LAT + 3, at=0)
        xc, yg, qT = area(RC, LAT), area(RC, LAT), area(RC, LAT)
        kT, iqT, ikT, vN, iw = area(LAT), area(2, LAT), area(LAT), area(LT, DSA_D), area(LT, IDX_H)
        gr, gi, t2, mixT0 = area(RC, LAT), area(RC, LAT), area(RC, LAT), area(KD, LAT)
        isc, relu, pens = area(LAT), area(2, LAT), area(4, LAT)
        prob0, turn0, biasb = area(2, LAT), area(LAT), area(2, LAT)
        gw = area(2, RC, P)
        on0 = gr
        lru = area(RC, LAT, at=0)
        qf, kf, vM = area(MLA_H, LAT, at=0), area(MLA_H, LAT), area(LT, MLA_H * MLA_V)
        cqT, ckvT, sq1, rs1 = area(4, LAT), area(2, LAT), area(4, LAT), area(2, LAT)
        rt, krt = area(2, LAT), area(2, LAT)
        on1 = area(LT, D, at=2 * MLA_H * LAT + LT * D)
        prob1, turn1 = area(2, LAT), area(LAT)
        mixT1 = area(KD, LAT, at=0)
        mixT2 = area(KD, TOK, at=0)
        qkb = area(6, TOK)
        vb = area(6, P)
        stage2 = cursor[0]
        qaT, kaT, kaN = area(A_H, TOK), area(A_H, TOK), area(6, A_H * P)
        vaN, oaT = area(6, A_H, P + 1), area(A_H, TOK)
        late = cursor[0]
        gI, gF = area(2, TOK), area(2, TOK)
        hs = area(6, A_H, P, at=late)
        R0, R1, R2, R3 = area(2, TOK, at=0), area(2, TOK), area(2, TOK), area(2, TOK)
        sqb, rsb, rtb = area(TOK, at=0), area(TOK), area(LAT)
        Cn = area(2, A_H, P + 1, at=0)
        lw = area(2, 4, P + 1)
        row_out = [R1, gF, R2, R0, R3]
        prob2, turn2 = area(2, 640, at=stage2), area(2, 512)
        on2 = area(LT, 512)
        mixT3 = area(KD, LAT, at=0)
        qC = area(KD, LAT, at=KD * TOK)
        kC, vC = area(C_KV, TOK), area(6, 256)
        sqc, rsc, rtc = area(TOK), area(TOK), area(LAT)
        prob3, turn3, on3 = area(2, TOK), area(2, 512), area(LT, D)

        const_in, rows_in, x_in, p_in, bias_in = (sem(n) for n in
                                                 ("const_in", "rows_in", "x_in", "p_in", "bias_in"))
        gates_in = sem("gates_in")
        a_ready, a_free = [sem(f"a_ready{i}") for i in range(2)], [sem(f"a_free{i}") for i in range(2)]
        b_ready, b_free = [sem(f"b_ready{i}") for i in range(2)], [sem(f"b_free{i}") for i in range(2)]
        w_landed = [sem(f"w_landed{i}") for i in range(NW)]
        o_ready, o_free = sem("o_ready"), sem("o_free")
        stage_over = sem("stage_over")
        out_set, out_stored = sem("out_set"), sem("out_stored")
        S = {n: sem(n) for n in (
            "centered", "squared", "hidden_set", "relu_used", "conv_set", "sqrt_set", "lam_exp", "lam_set",
            "bias_set", "bias_used", "dsa_max", "mla_max", "swa_max", "swc_max", "cat_max", "rope_raw", "head_sq",
            "onat_set", "kr_set", "rot_set", "rot_used", "abs_exp", "row_arg", "exp_arg", "lstm_d",
            "score_set", "kw_set", "state_set", "hs_sq")}

        def A(stage, j):
            n = BASE_A[stage] + j
            return n % 2, n // 2

        def B(stage, j):
            n = BASE_B[stage] + j
            return n % 2, n // 2

        def get_a(eng, stage, j, more=0):
            s, c = A(stage, j)
            eng.wait_ge(a_ready[s], more + (c + 1))
            return psA[:, s, :], a_free[s]

        def get_b(eng, stage, j):
            s, c = B(stage, j)
            eng.wait_ge(b_ready[s], c + 1)
            return psB[:, s, :], b_free[s]

        def emptied(eng, stage, j):
            s, c = A(stage, j)
            eng.wait_ge(a_free[s], c + 1)

        def turned(eng, stage, j):
            s, c = B(stage, j)
            eng.wait_ge(b_free[s], c + 1)

        met = {}

        def meet(eng):
            met[eng.engine] = met.get(eng.engine, 0) + 1
            eng.drain().then_inc(stage_over, 1)
            eng.wait_ge(stage_over, 4 * met[eng.engine])

        def tile_cols(w, a, b, kt=KD):
            return w[:, a:b].rearrange("(k p) c -> p k c", p=P), kt, b - a

        chunks = []

        def chunk(stage, last, *copies):
            slot, pairs = wbuf[:, len(chunks) % NW], []
            for col, src, kt, cols, *pitch in copies:
                if isinstance(cols, int):
                    pairs.append((slot[:, 0:kt, col:col + cols], src))
                else:
                    pitch = pitch[0] if pitch else cols[1]
                    for k in range(kt):
                        dst = slot[:, k, :].rearrange("p (h c) -> p h c", c=pitch)
                        h0, c0 = col // pitch, col % pitch
                        pairs.append((dst[:, h0:h0 + cols[0], c0:c0 + cols[1]], src[:, k]))
            chunks.append((stage, last, pairs))

        def mlp_chunks(name):
            for n in range(4 * GROUPS):
                chunks.append((name, (name, 16 * (n // 4) + 4 * (n % 4) + 3), None))

        w = d["hy_w_in"][0]
        chunk("hy", ("hy_xr", 3), (0, *tile_cols(w, 0, 512)))
        chunk("hy", ("hy_yr", 3), (0, *tile_cols(w, 512, 1024)))
        chunk("hy", ("hy_q", 3), (0, *tile_cols(w, 1024, 1536)))
        chunk("hy", ("hy_ki", 3), (0, *tile_cols(w, 1536, 1600)), (64, *tile_cols(w, 1536, 1600)),
              (128, *tile_cols(w, 1664, 1920)), (384, *tile_cols(w, 1920, 1984)), (448, *tile_cols(w, 1920, 1984)))
        chunk("hy", ("hy_v", 0), (0, *tile_cols(w, 1600, 1664)), (64, *tile_cols(w, 1984, 1988)))

        def out_chunks(stage, w):
            for c in range(2):
                chunk(stage, (stage, 4 * c + 3), (0, *tile_cols(w, c * 512, c * 512 + 512)))

        def ple_chunks(l):
            for c in range(2):
                chunk(f"ple{l}", (f"ple_g{l}", 4 * c + 3), (0, *tile_cols(d["ple_w_gate"][l], c * 512, c * 512 + 512)))
            for c in range(2):
                chunk(f"ple{l}", (f"ple_p{l}", 4 * c + 3),
                      (0, *tile_cols(d["ple_w_proj"][l], c * 512, c * 512 + 512, 2)))

        out_chunks("hy_out", d["hy_w_out"][0])
        ple_chunks(0)
        mlp_chunks("mlp0")
        w = d["mla_w_down"][0]
        chunk("mla", ("mla_cq", 3), (0, *tile_cols(w, 0, 512)))
        chunk("mla", ("mla_kr", 0), (0, *tile_cols(w, 512, 800)), (288, *tile_cols(w, 784, 800)),
              (304, *tile_cols(w, 768, 784)))
        w = d["mla_w_uq"][0]
        def head_cols(w, kt, h0, width, a, b):
            v = w.rearrange("(k p) (h c) -> p k h c", p=P, c=width)[:, :, h0:h0 + 4, a:b]
            return v, kt, (4, b - a)

        for c in range(4):
            chunk("uq", ("uq", 3 * c + 2), (0, *head_cols(w, 4, 4 * c, 96, 0, 64)),
                  (256, *head_cols(w, 4, 4 * c, 96, 64, 96)), (384, *head_cols(w, 4, 4 * c, 96, 80, 96), 32),
                  (400, *head_cols(w, 4, 4 * c, 96, 64, 80), 32))
        w = d["mla_w_ukv"][0]
        for c in range(4):
            chunk("ukv", ("ukv", 4 * c + 3), (0, *head_cols(w, 2, 4 * c, 128, 0, 64)),
                  (256, *head_cols(w, 2, 4 * c, 128, 64, 128)))
        out_chunks("mla_out", d["mla_w_out"][0])
        ple_chunks(1)
        mlp_chunks("mlp1")
        for l in range(2):
            for c in range(12):
                chunk("ada", ("ada", 12 * l + c), (0, *tile_cols(d["ada_w_2"][l], c * 512, c * 512 + 512)))
        w = d["ab_w_in_2"][0]
        for c, name in enumerate(("ab_q", "ab_k", "ab_v", "ab_o")):
            chunk("ab", (name, 5 if name == "ab_v" else 3), (0, *tile_cols(w, c * 512, c * 512 + 512)))
        chunk("ab", ("ab_qb", 3), (0, *tile_cols(w, 2064, 2576)))
        chunk("ab", ("ab_g", 3), (0, *tile_cols(w, 2576, 2640)), (64, *tile_cols(w, 2576, 2640)),
              (128, *tile_cols(w, 2640, 2704)), (192, *tile_cols(w, 2640, 2704)),
              (256, *tile_cols(w, 2704, 2832)), (384, *tile_cols(w, 2048, 2064)))
        out_chunks("ab_out", d["ab_w_out_2"][0])
        mlp_chunks("mlp2")
        w = d["c_w_in_2"][0]
        chunk("cin", ("c_q", 3), (0, *tile_cols(w, 0, 512)))
        chunk("cin", ("c_q", 7), (0, *tile_cols(w, 512, 1024)))
        chunk("cin", ("c_v", 1), (0, *tile_cols(w, 1024, 1536)))
        out_chunks("c_out", d["c_w_out_2"][0])
        mlp_chunks("mlp3")

        first_chunk, landed = {}, []
        count = [0] * NW
        for n, (stage, _, copies) in enumerate(chunks):
            first_chunk.setdefault(stage, n)
            count[n % NW] += 16 * (1 if copies is None else len(copies))
            landed.append(count[n % NW])
        MLP = {"mlp0": (d["mlp_w1"][0], d["mlp_w2"][0]), "mlp1": (d["mlp_w1"][1], d["mlp_w2"][1]),
               "mlp2": (d["mlp_w1_2"][0], d["mlp_w2_2"][0]), "mlp3": (d["mlp_w1_2"][1], d["mlp_w2_2"][1])}

        def weights(pe, stage, j, more=0):
            n = first_chunk[stage] + j
            pe.wait_ge(w_landed[n % NW], more + landed[n])
            return wbuf[:, n % NW]

        def dsa_logits(qt, h):
            r = slice(64 * (h % 2), 64 * (h % 2) + 64)
            return [(0, (qt + 1) * P, [(qT[r, h // 2, qt * P:qt * P + P], kT[r, 0:(qt + 1) * P])])]

        def mla_logits(qt, h):
            r = slice(0, NOPE + ROPE)
            return [(0, (qt + 1) * P, [(qf[r, h, qt * P:qt * P + P], kf[r, h, 0:(qt + 1) * P])])]

        def window(qt):
            return list(range(max(qt - 1, 0), min(qt + 2, LT)))

        def swa_logits(qt, h, lat=True):
            r = slice(64 * (h % 2), 64 * (h % 2) + 64)
            kv = 4 + h // (B_H // B_KV)
            q = qkb[r, h // 2, (0 if lat else LAT) + qt * P:(0 if lat else LAT) + qt * P + P]
            parts = [(0, CTX, [(q, qkb[r, kv, LAT:TOK])])]
            if lat:
                for i, b in enumerate(window(qt)):
                    parts.append((CTX + i * P, CTX + i * P + P, [(q, qkb[r, kv, b * P:b * P + P])]))
            return parts

        def swa_masks(qt, h):
            m = []
            for i, b in enumerate(window(qt)):
                if b != qt:
                    m.append((CTX + i * P, CTX + i * P + P, C["after"] if b < qt else C["before"]))
            return m

        def cat_logits(qt, h):
            q, kv = qC[:, h, qt * P:qt * P + P], h // (C_H // C_KV)
            return [(0, LAT, [(q, kC[:, kv, 0:LAT])]), (LAT, TOK, [(q, kC[:, kv, LAT:TOK])])]

        def swa_v(lat):
            def v(qt, kb, h):
                t = LT + kb if kb < CT else window(qt)[kb - CT]
                kv = h // (B_H // B_KV)
                return vb[:, t, kv * B_D:kv * B_D + B_D]
            return v

        diag = C["before"]
        ATT = {
            "dsa": dict(H=DSA_H, QT=LT, dv=DSA_D, nkb=lambda qt: qt + 1, logits=dsa_logits,
                        masks=lambda qt, h: [(0, (qt + 1) * P, biasb[:, h % 2, 0:(qt + 1) * P])],
                        v=lambda qt, kb, h: vN[:, kb, :], prob=prob0, turn=turn0, onat=on0, sink=False),
            "mla": dict(H=MLA_H, QT=LT, dv=MLA_V, nkb=lambda qt: qt + 1, logits=mla_logits,
                        masks=lambda qt, h: [(qt * P, qt * P + P, diag)],
                        v=lambda qt, kb, h: vM[:, kb, h * MLA_V:h * MLA_V + MLA_V], prob=prob1, turn=turn1, onat=on1,
                        sink=False),
            "swa": dict(H=B_H, QT=LT, dv=B_D, nkb=lambda qt: CT + len(window(qt)), logits=swa_logits, masks=swa_masks,
                        v=swa_v(True), prob=prob2, turn=turn2.rearrange("p a b -> p (a b)"), onat=on2, sink=True),
            "swc": dict(H=B_H, QT=CT, dv=B_D, nkb=lambda qt: CT, logits=lambda qt, h: swa_logits(qt, h, False),
                        masks=lambda qt, h: [], v=swa_v(False), prob=prob2,
                        turn=turn2.rearrange("p a b -> p (a b)"), onat=on2, sink=True),
            "cat": dict(H=C_H, QT=LT, dv=P, nkb=lambda qt: 6, logits=cat_logits, masks=lambda qt, h: [],
                        v=lambda qt, kb, h: vC[:, kb, (h // 4) * P:(h // 4) * P + P], prob=prob3,
                        turn=turn3.rearrange("p a b -> p (a b)"), onat=on3, sink=False),
        }
        n_o = {"dsa": 0, "mla": 4, "swa": 8, "swc": 12, "cat": 14}
        nmax, rsum, rinv, sink, sarg = small[:, 0:64], small[:, 64:128], small[:, 128:192], small[:, 192:200], small[:, 200:232]
        sp4, lz, ls, ls2, lacc = (small[:, 232 + 4 * i:236 + 4 * i] for i in range(5))
        m8 = small[:, 252:260]
        silu = small[:, 260:276]
        aff = small[:, 276:308].rearrange("p (a b) -> p a b", b=2)
        gcol = small[:, 308:500].rearrange("p (a b c) -> p a b c", b=12, c=4)
        carry = small[:, 500:548].rearrange("p (a b) -> p a b", b=12)
        hss, hrs = small[:, 548:572], small[:, 572:596]
        bI, bF = small[0:4, 596:598], small[0:4, 598:600]
        mrow = small[0:4, 600:614].rearrange("p (a b) -> p a b", b=7)
        crow = small[0:4, 614:626].rearrange("p (a b) -> p a b", b=6)
        den = small[:, 626:628]
        nsink = small[:, 630:638]
        bq8, cq8 = small[:, 638:639], small[:, 639:640]
        ln_squares = [KD * i for i in range(4)]
        rms_squares = [4 * KD + KD * i for i in range(4)]

        def turned_groups(name, qt):
            n = ATT[name]["nkb"](qt)
            return [range(g, min(g + 4, n)) for g in range(0, n, 4)]

        def units(name):
            s, at, r = ATT[name], 0, []
            for qt in range(s["QT"]):
                for h in range(s["H"]):
                    r.append((len(r), qt, h, at))
                    at += len(turned_groups(name, qt))
            return r

        def rows_of(ap):
            return ap.rearrange("(c p) -> c p", p=P)

        ROW_SRC = [("ln1_g", 0, rows_of(d["ln1_g"][0])), ("ln1_g", 8, rows_of(d["ln1_g"][1])),
                   ("ln1_b", 0, rows_of(d["ln1_b"][0])), ("ln1_b", 8, rows_of(d["ln1_b"][1])),
                   ("ln2_g", 0, rows_of(d["ln2_g"][0])), ("ln2_g", 8, rows_of(d["ln2_g"][1])),
                   ("ln2_b", 0, rows_of(d["ln2_b"][0])), ("ln2_b", 8, rows_of(d["ln2_b"][1])),
                   ("conv_w", 0, d["hy_conv_w"][0].rearrange("w (c p) -> (w c) p", p=P)),
                   ("conv_b", 0, rows_of(d["hy_conv_b"][0])), ("ga_b", 0, rows_of(d["hy_ga_b"][0])),
                   ("gx_b", 0, rows_of(d["hy_gx_b"][0])), ("lam", 0, rows_of(d["hy_lambda"][0])),
                   ("q_norm", 0, rows_of(d["mla_q_norm"][0])), ("kv_norm", 0, rows_of(d["mla_kv_norm"][0])),
                   ("c", 0, rows_of(d["c_2"][0])), ("c_ctx", 0, rows_of(d["c_ctx_2"])),
                   ("a_norm", 0, rows_of(d["mlstm_norm_g_2"][0])),
                   ("cq", 0, d["c_q_norm_g_2"]), ("ck", 0, d["c_k_norm_g_2"]), ("pad", 0, rows_of(d["c_ctx_2"])[0:2]),
                   ("norm1", 0, rows_of(d["norm1_g_2"][0])), ("norm1", 8, rows_of(d["norm1_g_2"][1])),
                   ("norm2", 0, rows_of(d["norm2_g_2"][0])), ("norm2", 8, rows_of(d["norm2_g_2"][1])),
                   ("ada_b", 0, rows_of(d["ada_b_2"][0])), ("ada_b", 48, rows_of(d["ada_b_2"][1]))]
        ROWS_IN = 16 * (len(ROW_SRC) + 4)
        GATES_IN = 16 * 4
        BIAS_IN = 16 * 5

        LSTM_ORDER = [[4, 5, 0, 1, 2, 3], [5, 4, 3, 2, 1, 0]]
        lstm_units = [(j, dr, h) for j in range(6) for dr in range(2) for h in range(A_H)]

        block = ctx.enter_context(nc.Block())

        @block.sync
        def _(sp):
            def used(n, more=0):
                if n >= NW:
                    s, c = A(*chunks[n - NW][1])
                    sp.wait_ge(a_ready[s], more + (c + 1))

            n = 0
            while n < len(chunks):
                stage, last, copies = chunks[n]
                if copies is not None:
                    used(n)
                    for dst, src in copies:
                        sp.dma_start(dst, src).then_inc(w_landed[n % NW], 16)
                    n += 1
                    continue
                w1, w2 = MLP[stage]
                w1 = w1.rearrange("(k p) f -> p k f", p=P)

                def group(i, n0, more):
                    for c in range(4):
                        if c < 2:
                            src = w1[:, :, bass.ds(i * 1024 + c * CW, CW)]
                        else:
                            src = w2[bass.ds(i * 1024, 1024), (c - 2) * CW:(c - 1) * CW].rearrange("(k p) c -> p k c", p=P)
                        used(n0 + c, more)
                        sp.dma_start(wbuf[:, (n0 + c) % NW, :, :], src).then_inc(w_landed[(n0 + c) % NW], 16)

                group(0, n, 0)
                with sp.Fori(1, GROUPS) as i:
                    group(i, n + 4, (i - 1) * 8)
                n += 4 * GROUPS
            sp.wait_ge(out_set, 1)
            sp.dma_start(out[0].rearrange("(a p) d -> p a d", p=P), xn).then_inc(out_stored, 16)
            sp.wait_ge(out_stored, 16)

        @block.tensor
        def _(pe):
            def product(stage, j, parts, more=0):
                s, c = A(stage, j)
                if c > 0:
                    pe.wait_ge(a_free[s], more + c)
                for a, b, pairs in parts:
                    m = 1
                    for e in pairs[0][0].shape[1:]:
                        m *= e
                    for i, (l, r) in enumerate(pairs):
                        ins = pe.matmul(psA[0:m, s, a:b], l, r, start=(i == 0), stop=(i == len(pairs) - 1))
                ins.then_inc(a_ready[s], 1)

            def turn(stage, j, parts):
                s, c = B(stage, j)
                if c > 0:
                    pe.wait_ge(b_free[s], c)
                for col, src in parts:
                    k, m = src.shape[0], src.shape[1]
                    ins = pe.transpose(psB[0:m, s, col:col + k], src, ident[0:k, 0:k])
                ins.then_inc(b_ready[s], 1)

            def features(w, col, rhs, n, kt=KD, m=P):
                return [(a, b, [(w[:, k, col:col + m], rhs[:, k, a:b]) for k in range(kt)])
                        for a, b in ((0, min(n, 512)), (512, n)) if b > a]

            def tokens(w, a, b, lhs, t, at, kt=KD):
                return (at, at + b - a, [(lhs[:, k, t * P:t * P + P], w[:, k, a:b]) for k in range(kt)])

            def linear(stage, chunk_stage, c0, rhs, n, nchunks=2, kt=KD):
                for c in range(nchunks):
                    w = weights(pe, chunk_stage, c0 + c)
                    for m in range(4):
                        product(stage, 4 * c + m, features(w, m * P, rhs, n, kt))

            def attention(name):
                s = ATT[name]
                us = units(name)

                def tail(u, qt, h, b0):
                    emptied(pe, name, u)
                    for g, kbs in enumerate(turned_groups(name, qt)):
                        turn(name, b0 + g, [((kb - kbs[0]) * P, s["prob"][:, u % 2, kb * P:kb * P + P]) for kb in kbs])
                    for g in range(len(turned_groups(name, qt))):
                        turned(pe, name, b0 + g)
                    n = n_o[name] + qt
                    if h == 0 and n > 0:
                        pe.wait_ge(o_free, n)
                    nkb = s["nkb"](qt)
                    for kb in range(nkb):
                        ins = pe.matmul(psO[:, h * s["dv"]:(h + 1) * s["dv"]], s["turn"][:, kb * P:kb * P + P],
                                        s["v"](qt, kb, h), start=(kb == 0), stop=(kb == nkb - 1))
                    if h == s["H"] - 1:
                        ins.then_inc(o_ready, 1)

                for u, qt, h, b0 in us:
                    product(name, u, s["logits"](qt, h))
                    if u >= 1:
                        tail(*us[u - 1])
                tail(*us[-1])
                pe.wait_ge(S["onat_set"], n_o[name] + s["QT"])
                width = s["H"] * s["dv"] // P
                for t in range(width):
                    turn(name + "_o", t, [(qt * P, s["onat"][:, qt, t * P:t * P + P]) for qt in range(s["QT"])])

            def layer_norm(i, x, n=LAT):
                product(f"ln_m{i}", 0, [(0, n, [(ones, x[:, k, 0:n]) for k in range(KD)])])
                pe.wait_ge(S["squared"], ln_squares[i] + KD)
                product(f"ln_v{i}", 0, [(0, n, [(ones, gT[:, k, 0:n]) for k in range(KD)])])

            def rms(i, n):
                pe.wait_ge(S["squared"], rms_squares[i] + KD)
                product(f"rms{i}", 0, [(a, b, [(ones, gT[:, k, a:b]) for k in range(KD)])
                                       for a, b in ((0, 512), (512, n)) if b > a])

            def mlp(name, index, n):
                with pe.Fori(0, GROUPS) as i:
                    for c in range(2):
                        w = weights(pe, name, c, i * 32)
                        for m in range(4):
                            product(name, 4 * c + m, features(w, m * P, hT, n), i * 8)
                    pe.wait_ge(S["hidden_set"], i * 8 + (32 * index + 8))
                    for c in range(2):
                        w = weights(pe, name, 2 + c, i * 32)
                        for m in range(4):
                            product(name, 8 + 4 * c + m, features(w, m * P, gT, n), i * 8)

            def ple(l):
                linear(f"ple_g{l}", f"ple{l}", 0, hT, LAT)
                linear(f"ple_p{l}", f"ple{l}", 2, pT[:, l], LAT, kt=2)

            pe.wait_ge(const_in, 16)
            pe.wait_ge(x_in, 32)
            for k in range(KD):
                turn("load", k, [(t * P, xn[:, t, k * P:k * P + P]) for t in range(LT)])
            for k in range(0, KD, 2):
                turn("load", 8 + k // 2, [(2 * P * e + t * P, cn[:, t, (k + e) * P:(k + e) * P + P])
                                          for e in range(2) for t in range(CT)])
            pe.wait_ge(p_in, 32)
            for l in range(2):
                for k in range(2):
                    turn("load", 12 + 2 * l + k, [(t * P, pn[:, l, t, k * P:k * P + P]) for t in range(LT)])
            pe.wait_ge(rows_in, ROWS_IN)
            turn("load", 16, [(0, rows[:, 0, :]), (P, rows[:, 1, :])])
            meet(pe)

            linear("hy_xr", "hy", 0, xT, LAT, 1)
            linear("hy_yr", "hy", 1, xT, LAT, 1)
            linear("hy_q", "hy", 2, xT, LAT, 1)
            linear("hy_ki", "hy", 3, xT, LAT, 1)
            w = weights(pe, "hy", 4)
            product("hy_v", 0, [tokens(w, 0, 68, xT, t, 68 * t) for t in range(LT)])
            meet(pe)
            pe.wait_ge(gates_in, GATES_IN)
            pe.wait_ge(S["conv_set"], 1)
            for c in range(RC):
                product("hy_gate", 2 * c, [(0, LAT, [(gw[:, 0, c, :], xc[:, c, :])])])
                product("hy_gate", 2 * c + 1, [(0, LAT, [(gw[:, 1, c, :], xc[:, c, :])])])
            for qt in range(1, LT):
                for hp in range(2):
                    product("idx", 2 * (qt - 1) + hp, [
                        (512 * e, 512 * e + (qt + 1) * P,
                         [(iqT[64 * e:64 * e + 64, hp, qt * P:qt * P + P], ikT[64 * e:64 * e + 64, 0:(qt + 1) * P])])
                        for e in range(2)])
            meet(pe)
            attention("dsa")
            meet(pe)
            linear("hy_out", "hy_out", 0, mixT0, LAT)
            meet(pe)
            layer_norm(0, xT)
            meet(pe)
            ple(0)
            meet(pe)
            mlp("mlp0", 0, LAT)
            meet(pe)
            layer_norm(1, acc)
            meet(pe)

            linear("mla_cq", "mla", 0, xT, LAT, 1)
            w = weights(pe, "mla", 1)
            for m in range(2):
                product("mla_kv", m, features(w, m * P, xT, LAT))
            product("mla_kr", 0, [(0, LAT, [(w[:, k, 256:288], xT[:, k, 0:LAT]) for k in range(KD)]),
                                  (512, 512 + LAT, [(w[:, k, 288:320], xT[:, k, 0:LAT]) for k in range(KD)])])
            emptied(pe, "mla_cq", 3)
            product("mla_s", 0, [(0, LAT, [(ones, sq1[:, k, :]) for k in range(4)])])
            emptied(pe, "mla_kv", 1)
            product("mla_s", 1, [(0, LAT, [(ones, rt[:, k, :]) for k in range(2)])])
            meet(pe)
            for c in range(4):
                w = weights(pe, "uq", c)
                for m in range(2):
                    product("uq", 3 * c + m, features(w, m * P, cqT, LAT, 4))
                product("uq", 3 * c + 2, [(0, LAT, [(w[:, k, 256:384], cqT[:, k, :]) for k in range(4)]),
                                          (512, 512 + LAT, [(w[:, k, 384:512], cqT[:, k, :]) for k in range(4)])])
            for c in range(4):
                w = weights(pe, "ukv", c)
                for m in range(2):
                    product("ukv", 4 * c + m, features(w, m * P, ckvT, LAT, 2))
                for m in range(2):
                    product("ukv", 4 * c + 2 + m, [
                        (256 * e, 256 * e + 256,
                         [(ckvT[:, k, (2 * m + e) * P:(2 * m + e) * P + P],
                           w[:, k, 256:512]) for k in range(2)])
                        for e in range(2)])
            meet(pe)
            attention("mla")
            meet(pe)
            linear("mla_out", "mla_out", 0, mixT1, LAT)
            meet(pe)
            layer_norm(2, xT)
            meet(pe)
            ple(1)
            meet(pe)
            mlp("mlp1", 1, LAT)
            meet(pe)
            layer_norm(3, acc)
            meet(pe)

            for l in range(2):
                for c in range(12):
                    w = weights(pe, "ada", 12 * l + c)
                    product("ada", 12 * l + c, [
                        (2 * m, 2 * m + 2, [(w[:, k, m * P:m * P + P], silu[:, 2 * k:2 * k + 2]) for k in range(KD)])
                        for m in range(4)])
            meet(pe)

            rms(0, TOK)
            meet(pe)
            linear("ab_q", "ab", 0, hT, TOK, 1)
            linear("ab_k", "ab", 1, hT, TOK, 1)
            w = weights(pe, "ab", 2)
            for t in range(6):
                product("ab_v", t, [tokens(w, 0, 512, hT, t, 0)])
            linear("ab_o", "ab", 3, hT, TOK, 1)
            linear("ab_qb", "ab", 4, hT, TOK, 1)
            w = weights(pe, "ab", 5)
            for m in range(2):
                product("ab_kb", m, features(w, m * P, hT, TOK))
            product("ab_vb", 0, [tokens(w, 256, 384, hT, t, P * t) for t in range(6)])
            for g, col in enumerate((0, 8, 4, 12)):
                product("ab_g", g, features(w, 384 + col, hT, TOK, m=4))
            meet(pe)
            for h in range(0, 6):
                turn("ka", h, [(P * hh, kaT[:, hh, h * P:h * P + P]) for hh in range(A_H)])
            for m in range(6):
                pe.wait_ge(S["head_sq"], m + 1)
                product("ab_n", m, [(a, b, [(C["ones64"], sqb[:, a:b])]) for a, b in ((0, 512), (512, TOK))])
            for m in range(6):
                pe.wait_ge(S["rope_raw"], m + 1)
                product("ab_r", m, [(0, LAT, [(C["rot64"], qkb[:, m, 0:LAT])])])
            meet(pe)
            meet(pe)
            turn("cols", 0, [(4 * (12 * q + 6 * dr + t), src[0:4, dr, t * P:t * P + P])
                             for q, src in enumerate(row_out[0:4]) for dr in range(2) for t in range(6)])
            product("carry", 0, [(12 * h, 12 * h + 12, [(C["pick"][0:4, h * P:h * P + P],
                                                        small[0:4, 614:626])]) for h in range(A_H)])
            meet(pe)

            def lstm_out(u):
                j, dr, h = lstm_units[u]
                t = LSTM_ORDER[dr][j]
                pe.wait_ge(S["score_set"], u + 1)
                pe.wait_ge(S["kw_set"], u + 1)
                s, c = B("lstm", u)
                pe.wait_ge(b_free[s], c)
                pe.matmul(psB[:, s, 0:P + 1], lw[:, u % 2, 1, 0:P], vaN[:, t, h, :], start=True, stop=True)
                pe.matmul(psB[:, s, 256:256 + P + 1], lw[:, u % 2, 2, 0:P], vaN[:, t, h, :],
                          start=True, stop=True).then_inc(b_ready[s], 1)

            for u, (j, dr, h) in enumerate(lstm_units):
                t = LSTM_ORDER[dr][j]
                cols = slice(t * P, t * P + P)
                pe.wait_ge(S["state_set"], 1 + max(u - 8 + 1, 0))
                product("lstm", u, [(0, P, [(kaT[:, h, cols], qaT[:, h, cols])]),
                                    (P, 2 * P, [(C["pick"][0:4, h * P:h * P + P], row_out[4][0:4, dr, cols])]),
                                    (512, 512 + P + 1, [(qaT[:, h, cols], Cn[:, dr, h, :])])])
                if u >= 1:
                    lstm_out(u - 1)
            lstm_out(47)
            meet(pe)
            meet(pe)
            for h in range(A_H):
                turn("hs", 2 * h, [(t * P, hs[:, t, h, :]) for t in range(LT)])
                turn("hs", 2 * h + 1, [(t * P, hs[:, LT + t, h, :]) for t in range(CT)])
            meet(pe)
            attention("swa")
            meet(pe)
            attention("swc")
            meet(pe)
            linear("ab_out", "ab_out", 0, mixT2, TOK)
            meet(pe)
            rms(1, TOK)
            meet(pe)
            mlp("mlp2", 2, TOK)
            meet(pe)

            rms(2, TOK)
            meet(pe)
            linear("c_q", "cin", 0, hT, LAT)
            w = weights(pe, "cin", 2)
            for m in range(2):
                product("c_k", m, features(w, m * P, hT, TOK))
            for g in range(2):
                product("c_v", g, [tokens(w, 256, 512, hT, t, 256 * (t - 4 * g)) for t in range(4 * g, min(4 * g + 4, 6))])
            meet(pe)
            for m in range(10):
                n = LAT if m < 8 else TOK
                pe.wait_ge(S["head_sq"], 6 + m + 1)
                product("c_n", m, [(a, b, [(ones, sqc[:, a:b])]) for a, b in ((0, 512), (512, n)) if b > a])
            for m in range(10):
                pe.wait_ge(S["rope_raw"], 6 + m + 1)
                product("c_r", m, [(0, LAT, [(C["rot128"], (qC[:, m, :] if m < 8 else kC[:, m - 8, 0:LAT]))])])
            meet(pe)
            attention("cat")
            meet(pe)
            linear("c_out", "c_out", 0, mixT3, LAT)
            meet(pe)
            rms(3, LAT)
            meet(pe)
            mlp("mlp3", 3, LAT)
            meet(pe)
            for t in range(LT):
                for e in range(2):
                    turn("out", 2 * t + e, [((k - 4 * e) * P, xT[:, k, t * P:t * P + P]) for k in range(4 * e, 4 * e + 4)])
            meet(pe)

        @block.scalar
        def _(act):
            def f(out, in_, func, **kw):
                return nc.scalar.activation(out, in_, func, **kw)

            act.dma_start(const[:, :], consts).then_inc(const_in, 16)
            act.dma_start(xn, d["x"][0].rearrange("(a p) d -> p a d", p=P)).then_inc(x_in, 16)
            act.dma_start(cn, d["ctx_2"][0].rearrange("(a p) d -> p a d", p=P)).then_inc(x_in, 16)
            for l in range(2):
                act.dma_start(pn[:, l], d["p"][l, 0].rearrange("(a p) d -> p a d", p=P)).then_inc(p_in, 16)
            for name, at, src in ROW_SRC:
                r = ROW[name] + at
                n = src.shape[0]
                act.dma_start(rows[r % P:r % P + n, r // P, :], src).then_inc(rows_in, 16)
            for name, src in (("bq", d["swa_q_norm_g_2"]), ("bk", d["swa_k_norm_g_2"])):
                for e in range(2):
                    act.dma_start(rows[ROW[name]:ROW[name] + 1, 0, 64 * e:64 * e + 64], src).then_inc(rows_in, 16)
            gb = d["ab_gate_b_2"].rearrange("a (g h) -> g h a", h=A_H)
            for dst, g in ((bI[:, 0:1], 0), (bI[:, 1:2], 2), (bF[:, 0:1], 1), (bF[:, 1:2], 3)):
                act.dma_start(dst, gb[g]).then_inc(bias_in, 16)
            act.dma_start(sink, d["swa_sink_2"][0:1, :].to_broadcast([P, B_H])).then_inc(bias_in, 16)
            meet(act)

            def attention(name, dst):
                s = ATT[name]
                us = units(name)

                def evacuate(u, qt, h, b0):
                    for g, kbs in enumerate(turned_groups(name, qt)):
                        ps, free = get_b(act, name, b0 + g)
                        f(s["turn"][:, kbs[0] * P:(kbs[-1] + 1) * P], ps[:, 0:len(kbs) * P], ACT.Copy).then_inc(free, 1)

                for u, qt, h, b0 in us:
                    c, n = qt * s["H"] + h, s["nkb"](qt) * P
                    act.wait_ge(S[name + "_max"], u + 1)
                    if s["sink"]:
                        f(sarg[:, c:c + 1], sink[:, h:h + 1], ACT.Exp, bias=nmax[:, c:c + 1])
                    slot, _ = A(name, u)
                    f(s["prob"][:, u % 2, 0:n], psA[:, slot, 0:n], ACT.Exp, bias=nmax[:, c:c + 1],
                      accum_out=rsum[:, c:c + 1]).then_inc(a_free[slot], 1)
                    if u >= 1:
                        evacuate(*us[u - 1])
                evacuate(*us[-1])
                for t in range(s["H"] * s["dv"] // P):
                    ps, free = get_b(act, name + "_o", t)
                    f(dst(t), ps[:, 0:s["QT"] * P], ACT.Copy).then_inc(free, 1)

            def root(stage, j, dst, n, width, eps, cols=None):
                ps, free = get_a(act, stage, j)
                f(dst, ps[:, 0:n], ACT.Sqrt, scale=1.0 / width, bias=eps).then_inc(free, 1)

            def layer_norm(i, x, n=LAT):
                for k in range(KD):
                    act.wait_ge(S["centered"], KD * i + k + 1)
                    f(gT[:, k, 0:n], x[:, k, 0:n], ACT.Square).then_inc(S["squared"], 1)
                root(f"ln_v{i}", 0, rstd[:, 0:n], n, D, eps_ln)

            def rms(i, n):
                for k in range(KD):
                    f(gT[:, k, 0:n], xT[:, k, 0:n], ACT.Square).then_inc(S["squared"], 1)
                root(f"rms{i}", 0, rstd[:, 0:n], n, D, eps_rms)

            def ple(l):
                for j in range(KD):
                    ps, free = get_a(act, f"ple_g{l}", j)
                    f(gT[:, j, 0:LAT], ps[:, 0:LAT], ACT.Sigmoid).then_inc(free, 1)

            def mlp(name, n):
                with act.Fori(0, GROUPS) as i:
                    for j in range(8):
                        ps, free = get_a(act, name, j, i * 8)
                        f(gT[:, j, 0:n], ps[:, 0:n], ACT.Relu).then_inc(free, 1)
                        act.drain()
                        f(gT[:, j, 0:n], gT[:, j, 0:n], ACT.Square).then_inc(S["hidden_set"], 1)

            f(lz, vecT[:, ROW["lam"]:ROW["lam"] + 4], ACT.Abs)
            act.drain()
            f(lz, lz, ACT.Exp, scale=-1.0).then_inc(S["lam_exp"], 1)
            for m in range(4):
                ps, free = get_a(act, "hy_xr", m)
                f(xpad[:, m, 3:3 + LAT], ps[:, 0:LAT], ACT.Copy).then_inc(free, 1)
            for m in range(4):
                ps, free = get_a(act, "hy_yr", m)
                f(yg[:, m, :], ps[:, 0:LAT], ACT.Gelu_apprx_tanh).then_inc(free, 1)
            for m in range(4):
                ps, free = get_a(act, "hy_q", m)
                f(qT[:, m, :], ps[:, 0:LAT], ACT.Copy, scale=DSA_D ** -0.5).then_inc(free, 1)
            for v, name in enumerate(("c", "c_ctx")):
                f(silu.rearrange("p (k v) -> p k v", v=2)[:, :, v], vecT[:, ROW[name]:ROW[name] + KD], ACT.Sigmoid)
            meet(act)
            for c in range(RC):
                for g, dst, name in ((0, gr, "ga_b"), (1, gi, "gx_b")):
                    ps, free = get_a(act, "hy_gate", 2 * c + g)
                    f(dst[:, c, :], ps[:, 0:LAT], ACT.Sigmoid, bias=vec(name, c)).then_inc(free, 1)
            act.drain()
            act.wait_ge(S["lam_set"], 1)
            for c in range(RC):
                f(t2[:, c, :], gr[:, c, :], ACT.Tanh, scale=sp4[:, c:c + 1])
            act.drain()
            f(gr, t2, ACT.Sqrt).then_inc(S["sqrt_set"], 1)
            for n in range(6):
                ps, free = get_a(act, "idx", n)
                nk = (n // 2 + 2) * P
                if n >= 1:
                    act.wait_ge(S["relu_used"], n)
                f(relu[:, :, 0:nk], ps.rearrange("p (e c) -> p e c", e=2)[:, :, 0:nk], ACT.Relu).then_inc(free, 1)
            meet(act)
            attention("dsa", lambda t: mixT0[:, RC + t, :])
            meet(act)
            meet(act)
            layer_norm(0, xT)
            meet(act)
            ple(0)
            meet(act)
            mlp("mlp0", LAT)
            meet(act)
            layer_norm(1, acc)
            meet(act)

            for m in range(4):
                ps, free = get_a(act, "mla_cq", m)
                f(cqT[:, m, :], ps[:, 0:LAT], ACT.Copy)
                f(sq1[:, m, :], ps[:, 0:LAT], ACT.Square).then_inc(free, 1)
            for m in range(2):
                ps, free = get_a(act, "mla_kv", m)
                f(ckvT[:, m, :], ps[:, 0:LAT], ACT.Copy)
                f(rt[:, m, :], ps[:, 0:LAT], ACT.Square).then_inc(free, 1)
            root("mla_s", 0, rs1[:, 0, :], LAT, QL, eps_rms)
            root("mla_s", 1, rs1[:, 1, :], LAT, KVL, eps_rms)
            act.wait_ge(S["kr_set"], 1)
            for h in range(MLA_H):
                f(kf[64:96, h, :], krt[0:32, 0, :], ACT.Copy)
            meet(act)
            scale = (NOPE + ROPE) ** -0.5
            for c in range(4):
                for m in range(2):
                    ps, free = get_a(act, "uq", 3 * c + m)
                    h = 4 * c + 2 * m
                    f(qf[0:64, h, :], ps[0:64, 0:LAT], ACT.Copy, scale=scale)
                    f(qf[0:64, h + 1, :], ps[64:128, 0:LAT], ACT.Copy, scale=scale).then_inc(free, 1)
                act.wait_ge(S["rot_set"], c + 1)
                for e in range(4):
                    ins = f(qf[64:96, 4 * c + e, :], rt[32 * e:32 * e + 32, 0, :], ACT.Copy, scale=scale)
                ins.then_inc(S["rot_used"], 1)
            for c in range(4):
                for m in range(2):
                    ps, free = get_a(act, "ukv", 4 * c + m)
                    h = 4 * c + 2 * m
                    f(kf[0:64, h, :], ps[0:64, 0:LAT], ACT.Copy)
                    f(kf[0:64, h + 1, :], ps[64:128, 0:LAT], ACT.Copy).then_inc(free, 1)
            meet(act)
            attention("mla", lambda t: mixT1[:, t, :])
            meet(act)
            meet(act)
            layer_norm(2, xT)
            meet(act)
            ple(1)
            meet(act)
            mlp("mlp1", LAT)
            meet(act)
            layer_norm(3, acc)
            meet(act)
            meet(act)

            rms(0, TOK)
            meet(act)
            for m in range(4):
                ps, free = get_a(act, "ab_q", m)
                f(qaT[:, m, :], ps[:, 0:TOK], ACT.Copy).then_inc(free, 1)
            for m in range(4):
                ps, free = get_a(act, "ab_k", m)
                f(kaT[:, m, :], ps[:, 0:TOK], ACT.Copy, scale=P ** -0.5).then_inc(free, 1)
            for m in range(4):
                ps, free = get_a(act, "ab_o", m)
                f(oaT[:, m, :], ps[:, 0:TOK], ACT.Sigmoid).then_inc(free, 1)
            act.wait_ge(bias_in, BIAS_IN)
            for g in range(4):
                ps, free = get_a(act, "ab_g", g)
                dr, dst, b = g % 2, (gI, gF)[g // 2], (bI, bF)[g // 2]
                lat, cx = ps[0:4, 0:LAT], ps[0:4, LAT:TOK]
                if dr:
                    lat, cx = lat[:, ::-1], cx[:, ::-1]
                f(dst[0:4, dr, CTX:TOK], lat, ACT.Identity, bias=b[:, dr:dr + 1])
                f(dst[0:4, dr, 0:CTX], cx, ACT.Identity, bias=b[:, dr:dr + 1]).then_inc(free, 1)
            meet(act)
            for t in range(6):
                ps, free = get_b(act, "ka", t)
                f(kaN[:, t, :], ps[:, 0:512], ACT.Copy).then_inc(free, 1)

            def head_norms(stage, first, n, tile, sq, rs, width, cols):
                for m in range(n):
                    if m >= 1:
                        act.wait_ge(S["rope_raw"], first + m)
                    f(sq[:, 0:cols(m)], tile(m), ACT.Square).then_inc(S["head_sq"], 1)
                    root(stage, m, rs[:, 0:cols(m)], cols(m), width, eps_rms)

            head_norms("ab_n", 0, 6, lambda m: qkb[:, m, :], sqb, rsb, B_D, lambda m: TOK)
            meet(act)
            f(R0[0:4], gF[0:4], ACT.Abs)
            act.drain()
            f(R0[0:4], R0[0:4], ACT.Exp, scale=-1.0).then_inc(S["abs_exp"], 1)
            act.wait_ge(S["row_arg"], 1)
            f(crow, crow, ACT.Exp)
            for src, dst, func in ((R3, R1, ACT.Exp), (R2, R3, ACT.Copy), (gF, R2, ACT.Exp), (R0, gF, ACT.Exp),
                                   (gI, R0, ACT.Copy)):
                for dr in range(2):
                    lat, cx = src[0:4, dr, CTX:TOK], src[0:4, dr, 0:CTX]
                    if dr:
                        lat, cx = lat[:, ::-1], cx[:, ::-1]
                    f(dst[0:4, dr, 0:LAT], lat, func)
                    f(dst[0:4, dr, LAT:TOK], cx, func)
                act.drain()
            meet(act)
            ps, free = get_b(act, "cols", 0)
            f(small[:, 308:500], ps[:, 0:192], ACT.Copy).then_inc(free, 1)
            ps, free = get_a(act, "carry", 0)
            f(small[:, 500:548], ps[:, 0:48], ACT.Copy).then_inc(free, 1)
            meet(act)
            for u, (j, dr, h) in enumerate(lstm_units):
                t = LSTM_ORDER[dr][j]
                act.wait_ge(S["lstm_d"], u + 1)
                f(lw[:, u % 2, 0, 0:P], lw[:, u % 2, 0, 0:P], ACT.Exp,
                  bias=gcol[:, 3, 6 * dr + t, h:h + 1]).then_inc(S["exp_arg"], 1)
            meet(act)
            for t in range(6):
                for h in range(A_H):
                    f(qaT[:, h, t * P:t * P + P], hs[:, t, h, :], ACT.Square, accum_out=hss[:, 4 * t + h:4 * t + h + 1])
            act.drain()
            f(hrs, hss, ACT.Sqrt, scale=1.0 / P, bias=eps_rms).then_inc(S["hs_sq"], 1)
            meet(act)
            meet(act)
            attention("swa", lambda t: mixT2[:, 4 + t, 0:LAT])
            meet(act)
            attention("swc", lambda t: mixT2[:, 4 + t, LAT:TOK])
            meet(act)
            meet(act)
            rms(1, TOK)
            meet(act)
            mlp("mlp2", TOK)
            meet(act)

            rms(2, TOK)
            meet(act)
            for m in range(8):
                ps, free = get_a(act, "c_q", m)
                f(qC[:, m, :], ps[:, 0:LAT], ACT.Copy).then_inc(free, 1)
            for m in range(2):
                ps, free = get_a(act, "c_k", m)
                f(kC[:, m, :], ps[:, 0:TOK], ACT.Copy).then_inc(free, 1)
            meet(act)
            head_norms("c_n", 6, 10, lambda m: qC[:, m, :] if m < 8 else kC[:, m - 8, :], sqc, rsc, P,
                       lambda m: LAT if m < 8 else TOK)
            meet(act)
            attention("cat", lambda t: mixT3[:, t, :])
            meet(act)
            meet(act)
            rms(3, LAT)
            meet(act)
            mlp("mlp3", LAT)
            meet(act)
            meet(act)

        @block.gpsimd
        def _(pool):
            nc.gpsimd.memset(gw, 0.0)
            pool.drain()
            for g, name in enumerate(("hy_ga_w", "hy_gx_w")):
                for e in range(2):
                    src = d[name][0].rearrange("(c e) i o -> e i c o", e=2)[e]
                    pool.dma_start(gw[64 * e:64 * e + 64, g, :, 64 * e:64 * e + 64], src).then_inc(gates_in, 16)
            for _ in range(3):
                meet(pool)
            for u, qt, h, _ in units("dsa"):
                n = (qt + 1) * P
                if u >= 2:
                    pool.wait_ge(S["bias_used"], u - 1)
                b = biasb[:, u % 2, 0:n]
                slope = 2.0 ** (-8.0 * (h + 1) / DSA_H)
                nc.gpsimd.tensor_scalar(b, C["dist"][:, LAT - n:LAT], -slope, None, ALU.mult)
                pool.drain()
                pen = C["before"] if qt == 0 else pens[:, qt, 0:n]
                nc.gpsimd.tensor_tensor(b, b, pen, ALU.add).then_inc(S["bias_set"], 1)
            for _ in range(PRE_LSTM):
                meet(pool)
            for u, (j, dr, h) in enumerate(lstm_units):
                t = LSTM_ORDER[dr][j]
                if u >= 2:
                    s, c = B("lstm", u - 2)
                    pool.wait_ge(b_ready[s], c + 1)
                nc.gpsimd.tensor_scalar(lw[:, u % 2, 2, 0:P], kaN[:, t, h * P:h * P + P],
                                        gcol[:, 2, 6 * dr + t, h:h + 1], None, ALU.mult).then_inc(S["kw_set"], 1)
            for _ in range(POST_LSTM):
                meet(pool)

        @block.vector
        def _(v):
            ts, tt, stt = nc.vector.tensor_scalar, nc.vector.tensor_tensor, nc.vector.scalar_tensor_tensor

            def log1p(z, s, s2, r):
                ts(s, z, 2.0, None, ALU.add)
                v.drain()
                nc.vector.reciprocal(s, s)
                v.drain()
                tt(s, s, z, ALU.mult)
                v.drain()
                tt(s2, s, s, ALU.mult)
                v.drain()
                ts(r, s2, 1.0 / 15, None, ALU.mult)
                for n in (13, 11, 9, 7, 5, 3):
                    v.drain()
                    stt(r, r, 1.0 / n, s2, ALU.add, ALU.mult)
                v.drain()
                stt(r, r, 1.0, s, ALU.add, ALU.mult)
                v.drain()

            def attention(name):
                s = ATT[name]

                def finish(qt):
                    n = n_o[name] + qt
                    H, dv = s["H"], s["dv"]
                    c = slice(qt * H, qt * H + H)
                    v.wait_ge(o_ready, n + 1)
                    if s["sink"]:
                        tt(rsum[:, c], rsum[:, c], sarg[:, c], ALU.add)
                        v.drain()
                    nc.vector.reciprocal(rinv[:, c], rsum[:, c])
                    v.drain()
                    for h in range(H):
                        ins = ts(s["onat"][:, qt, h * dv:h * dv + dv], psO[:, h * dv:h * dv + dv],
                                 rinv[:, qt * H + h:qt * H + h + 1], None, ALU.mult)
                    ins.then_inc(o_free, 1)
                    v.drain().then_inc(S["onat_set"], 1)

                for u, qt, h, _ in units(name):
                    c, n = qt * s["H"] + h, s["nkb"](qt) * P
                    ps, _ = get_a(v, name, u)
                    if name == "dsa":
                        v.wait_ge(S["bias_set"], u + 1)
                    ins = None
                    for a, b, m in s["masks"](qt, h):
                        ins = tt(ps[:, a:b], ps[:, a:b], m, ALU.add)
                    if ins is not None:
                        if name == "dsa":
                            ins.then_inc(S["bias_used"], 1)
                        v.drain()
                    ins = nc.vector.tensor_reduce(nmax[:, c:c + 1], ps[:, 0:n], AX.X, ALU.max, negate=True)
                    if s["sink"]:
                        v.drain()
                        ins = tt(nmax[:, c:c + 1], nmax[:, c:c + 1], nsink[:, h:h + 1], ALU.min)
                    ins.then_inc(S[name + "_max"], 1)
                    if h == 0 and qt > 0:
                        finish(qt - 1)
                finish(s["QT"] - 1)

            def layer_norm(i, x, gain, bias, j0, dst, n=LAT):
                ps, free = get_a(v, f"ln_m{i}", 0)
                ts(nrm[:, 0:n], ps[:, 0:n], 1.0 / D, None, ALU.mult).then_inc(free, 1)
                v.drain()
                for k in range(KD):
                    tt(x[:, k, 0:n], x[:, k, 0:n], nrm[:, 0:n], ALU.subtract).then_inc(S["centered"], 1)
                emptied(v, f"ln_v{i}", 0)
                nc.vector.reciprocal(rstd[:, 0:n], rstd[:, 0:n])
                v.drain()
                for k in range(KD):
                    stt(dst[:, k, 0:n], x[:, k, 0:n], vec(gain, j0 + k), rstd[:, 0:n], ALU.mult, ALU.mult)
                v.drain()
                for k in range(KD):
                    ts(dst[:, k, 0:n], dst[:, k, 0:n], vec(bias, j0 + k), None, ALU.add)

            def rms(i, layer, norm, first, n):
                for k in range(KD):
                    ts(aff[:, k, :], mod[:, layer, (first + 1) * KD + k, :], 1.0, vec(norm, 8 * layer + k),
                       ALU.add, ALU.mult)
                emptied(v, f"rms{i}", 0)
                nc.vector.reciprocal(rstd[:, 0:n], rstd[:, 0:n])
                v.drain()
                spans = [(0, LAT, 0)] + ([(LAT, n, 1)] if n > LAT else [])
                for k in range(KD):
                    for a, b, e in spans:
                        stt(hT[:, k, a:b], xT[:, k, a:b], aff[:, k, e:e + 1], rstd[:, a:b], ALU.mult, ALU.mult)
                v.drain()
                for k in range(KD):
                    for a, b, e in spans:
                        ts(hT[:, k, a:b], hT[:, k, a:b], mod[:, layer, first * KD + k, e:e + 1], None, ALU.add)

            def residual(stage):
                for m in range(KD):
                    ps, free = get_a(v, stage, m)
                    stt(xT[:, m, 0:LAT], xT[:, m, 0:LAT], ALPHA, ps[:, 0:LAT], ALU.mult, ALU.add).then_inc(free, 1)

            def gated(stage, layer, n):
                spans = [(0, LAT, 0)] + ([(LAT, n, 1)] if n > LAT else [])
                for m in range(KD):
                    ps, free = get_a(v, stage, m)
                    for a, b, e in spans:
                        ins = stt(xT[:, m, a:b], ps[:, a:b], mod[:, layer, 2 * KD + m, e:e + 1], xT[:, m, a:b],
                                  ALU.mult, ALU.add)
                    ins.then_inc(free, 1)

            def ple(l):
                emptied(v, f"ple_g{l}", 7)
                for j in range(KD):
                    ps, free = get_a(v, f"ple_p{l}", j)
                    tt(acc[:, j, 0:LAT], gT[:, j, 0:LAT], ps[:, 0:LAT], ALU.mult).then_inc(free, 1)
                v.drain()
                for j in range(KD):
                    stt(acc[:, j, 0:LAT], hT[:, j, 0:LAT], ALPHA, acc[:, j, 0:LAT], ALU.mult, ALU.add)

            def mlp(name, n):
                with v.Fori(0, GROUPS) as i:
                    for j in range(8):
                        ps, free = get_a(v, name, 8 + j, i * 8)
                        tt(acc[:, j, 0:n], acc[:, j, 0:n], ps[:, 0:n], ALU.add).then_inc(free, 1)
                    v.drain()

            def mlp_residual(layer, n):
                v.drain()
                for k in range(KD):
                    for a, b, e in [(0, LAT, 0)] + ([(LAT, n, 1)] if n > LAT else []):
                        stt(xT[:, k, a:b], acc[:, k, a:b], mod[:, layer, 5 * KD + k, e:e + 1], xT[:, k, a:b],
                            ALU.mult, ALU.add)

            for k in range(KD):
                ps, free = get_b(v, "load", k)
                nc.vector.tensor_copy(xT[:, k, 0:LAT], ps).then_inc(free, 1)
            for k in range(0, KD, 2):
                ps, free = get_b(v, "load", 8 + k // 2)
                nc.vector.tensor_copy(xT[:, k:k + 2, LAT:TOK], ps.rearrange("p (a b) -> p a b", a=2)).then_inc(free, 1)
            for l in range(2):
                for k in range(2):
                    ps, free = get_b(v, "load", 12 + 2 * l + k)
                    nc.vector.tensor_copy(pT[:, l, k, :], ps).then_inc(free, 1)
            ps, free = get_b(v, "load", 16)
            nc.vector.tensor_copy(vecT[:, :], ps[:, 0:NROW]).then_inc(free, 1)
            meet(v)

            v.wait_ge(bias_in, BIAS_IN)
            ts(nsink, sink, -1.0, None, ALU.mult)
            ts(bq8, vec("bq", 0), B_D ** -0.5, None, ALU.mult)
            ts(cq8, vec("cq", 0), P ** -0.5, None, ALU.mult)
            nc.vector.memset(xpad[:, :, 0:3], 0.0)
            v.wait_ge(S["lam_exp"], 1)
            log1p(lz, ls, ls2, lacc)
            ts(ls, vecT[:, ROW["lam"]:ROW["lam"] + 4], -1.0, 0.0, ALU.mult, ALU.max)
            v.drain()
            stt(sp4, lacc, 2.0, ls, ALU.mult, ALU.add)
            v.drain()
            ts(sp4, sp4, LRU_HALF, None, ALU.mult).then_inc(S["lam_set"], 1)
            for m in range(3):
                ps, free = get_a(v, "hy_ki", m)
                nc.vector.tensor_copy(kT if m == 0 else iqT[:, m - 1, :], ps[:, 0:LAT]).then_inc(free, 1)
            ps, free = get_a(v, "hy_ki", 3)
            nc.vector.tensor_copy(ikT, ps[:, 0:LAT]).then_inc(free, 1)
            ps, free = get_a(v, "hy_v", 0)
            ps = ps[:, 0:4 * 68].rearrange("p (t c) -> p t c", c=68)
            nc.vector.tensor_copy(vN, ps[:, :, 0:64])
            ts(iw, ps[:, :, 64:68], IDX_H ** -0.5 * IDX_D ** -0.5, None, ALU.mult).then_inc(free, 1)
            meet(v)
            s16 = silu.rearrange("p (k v) -> p k v", v=2)
            for e, name in enumerate(("c", "c_ctx")):
                tt(s16[:, :, e], s16[:, :, e], vecT[:, ROW[name]:ROW[name] + KD], ALU.mult)
            for c in range(RC):
                ts(xc[:, c, :], xpad[:, c, 0:LAT], vec("conv_w", c), vec("conv_b", c), ALU.mult, ALU.add)
            for i in range(1, 4):
                v.drain()
                for c in range(RC):
                    stt(xc[:, c, :], xpad[:, c, i:i + LAT], vec("conv_w", RC * i + c), xc[:, c, :], ALU.mult, ALU.add)
            v.drain().then_inc(S["conv_set"], 1)
            v.wait_ge(S["sqrt_set"], 1)
            ts(lru, t2, 1.0, None, ALU.add)
            v.drain()
            nc.vector.reciprocal(lru, lru)
            tt(gi, gi, xc, ALU.mult)
            v.drain()
            tt(gr, gr, lru, ALU.mult)
            ts(t2, t2, -1.0, 1.0, ALU.mult, ALU.add)
            v.drain()
            stt(gi, gi, 2.0, gr, ALU.mult, ALU.mult)
            tt(t2, t2, lru, ALU.mult)
            v.drain()
            for c in range(RC):
                nc.vector.tensor_tensor_scan(xc[:, c, :], t2[:, c, :], gi[:, c, :], 0.0, ALU.mult, ALU.add)
            v.drain()
            tt(mixT0[:, 0:RC, :], xc, yg, ALU.mult)
            for qt in range(1, LT):
                nk = (qt + 1) * P
                s = isc[:, 0:nk]
                for hp in range(2):
                    n = 2 * (qt - 1) + hp
                    emptied(v, "idx", n)
                    for e in range(2):
                        h = 2 * hp + e
                        if h == 0:
                            ts(s, relu[:, 0, 0:nk], iw[:, qt, 0:1], None, ALU.mult)
                        else:
                            ins = stt(s, relu[:, e, 0:nk], iw[:, qt, h:h + 1], s, ALU.mult, ALU.add)
                            if e == 1:
                                ins.then_inc(S["relu_used"], 1)
                        v.drain()
                tt(isc[:, qt * P:nk], isc[:, qt * P:nk], C["before"], ALU.add)
                v.drain()
                for _ in range(TOPK // 8):
                    nc.vector.max(m8, s)
                    v.drain()
                    nc.vector.match_replace(s, m8, s, TAKEN)
                    v.drain()
                ts(pens[:, qt, 0:nk], s, TAKEN, 1.0, ALU.is_equal, ALU.subtract)
                v.drain()
                ts(pens[:, qt, 0:nk], pens[:, qt, 0:nk], -NEG, None, ALU.mult)
            meet(v)
            attention("dsa")
            meet(v)
            residual("hy_out")
            meet(v)
            layer_norm(0, xT, "ln1_g", "ln1_b", 0, hT)
            meet(v)
            ple(0)
            meet(v)
            mlp("mlp0", LAT)
            meet(v)
            layer_norm(1, acc, "ln2_g", "ln2_b", 0, xT)
            meet(v)

            ps, free = get_a(v, "mla_kr", 0)
            tt(krt[0:32, 0, :], ps[0:32, 0:512], C["cosM"][0:32], ALU.mult)
            tt(krt[0:32, 1, :], ps[0:32, 512:1024], C["sinM"][0:32], ALU.mult).then_inc(free, 1)
            v.drain()
            tt(krt[0:32, 0, :], krt[0:32, 0, :], krt[0:32, 1, :], ALU.add).then_inc(S["kr_set"], 1)
            for j, (t, n, name) in enumerate(((cqT, 4, "q_norm"), (ckvT, 2, "kv_norm"))):
                emptied(v, "mla_s", j)
                nc.vector.reciprocal(rs1[:, j, :], rs1[:, j, :])
                v.drain()
                for k in range(n):
                    stt(t[:, k, :], t[:, k, :], vec(name, k), rs1[:, j, :], ALU.mult, ALU.mult)
            meet(v)
            for c in range(4):
                ps, free = get_a(v, "uq", 3 * c + 2)
                if c >= 1:
                    v.wait_ge(S["rot_used"], c)
                tt(rt[:, 0, :], ps[:, 0:512], C["cosM"], ALU.mult)
                tt(rt[:, 1, :], ps[:, 512:1024], C["sinM"], ALU.mult).then_inc(free, 1)
                v.drain()
                tt(rt[:, 0, :], rt[:, 0, :], rt[:, 1, :], ALU.add).then_inc(S["rot_set"], 1)
            for c in range(4):
                for m in range(2):
                    ps, free = get_a(v, "ukv", 4 * c + 2 + m)
                    nc.vector.tensor_copy(vM[:, 2 * m:2 * m + 2, 256 * c:256 * c + 256],
                                          ps[:, 0:512].rearrange("p (e c) -> p e c", e=2)).then_inc(free, 1)
            meet(v)
            attention("mla")
            meet(v)
            residual("mla_out")
            meet(v)
            layer_norm(2, xT, "ln1_g", "ln1_b", 8, hT)
            meet(v)
            ple(1)
            meet(v)
            mlp("mlp1", LAT)
            meet(v)
            layer_norm(3, acc, "ln2_g", "ln2_b", 8, xT)
            meet(v)
            for l in range(2):
                for c in range(12):
                    ps, free = get_a(v, "ada", 12 * l + c)
                    for m in range(4):
                        ins = ts(mod[:, l, 4 * c + m, :], ps[:, 2 * m:2 * m + 2], vec("ada_b", 48 * l + 4 * c + m),
                                 None, ALU.add)
                    ins.then_inc(free, 1)
            meet(v)

            rms(0, 0, "norm1", 0, TOK)
            meet(v)
            nc.vector.memset(vaN[:, :, :, P:P + 1], 1.0)
            for t in range(6):
                ps, free = get_a(v, "ab_v", t)
                nc.vector.tensor_copy(vaN[:, t, :, 0:P], ps[:, 0:512].rearrange("p (h c) -> p h c", h=A_H)).then_inc(free, 1)
            for m in range(6):
                ps, free = get_a(v, "ab_qb", m) if m < 4 else get_a(v, "ab_kb", m - 4)
                nc.vector.tensor_copy(qkb[:, m, :], ps[:, 0:TOK]).then_inc(free, 1)
            ps, free = get_a(v, "ab_vb", 0)
            nc.vector.tensor_copy(vb, ps[:, 0:TOK].rearrange("p (t c) -> p t c", t=6)).then_inc(free, 1)
            meet(v)

            def head_norms(norm_stage, rope_stage, first, n, tile, rs, tmp, gain, cos, sin):
                for m in range(n):
                    emptied(v, norm_stage, m)
                    x = tile(m)
                    r = rs[:, 0:x.shape[-1]]
                    nc.vector.reciprocal(r, r)
                    v.drain()
                    stt(x, x, gain(m), r, ALU.mult, ALU.mult).then_inc(S["rope_raw"], 1)
                for m in range(n):
                    ps, free = get_a(v, rope_stage, m)
                    x = tile(m)[:, 0:LAT]
                    tt(tmp, ps[:, 0:LAT], sin, ALU.mult).then_inc(free, 1)
                    tt(x, x, cos, ALU.mult)
                    v.drain()
                    tt(x, x, tmp, ALU.add)
                    v.drain()

            head_norms("ab_n", "ab_r", 0, 6, lambda m: qkb[:, m, :], rsb, rtb,
                       lambda m: bq8 if m < 4 else vec("bk", 0), C["cosB"], C["sinB"])
            meet(v)
            v.wait_ge(S["abs_exp"], 1)
            z, s, s2, r = (x[0:4] for x in (R0, R1, R2, R3))
            log1p(z, s, s2, r)
            lf, gi_ = gF[0:4], gI[0:4]
            ts(lf, lf, 0.0, None, ALU.min)
            nc.vector.memset(z, 1.0)
            v.drain()
            stt(lf, r, -2.0, lf, ALU.mult, ALU.add)
            nc.vector.memset(z.rearrange("p a (c t) -> p a c t", t=P)[:, :, :, 0:1], 0.0)
            nc.vector.memset(mrow, 0.0)
            v.drain()
            flat = lambda x: x.rearrange("p a b -> p (a b)")
            nc.vector.tensor_tensor_scan(flat(s), flat(z), flat(lf), 0.0, ALU.mult, ALU.add)
            v.drain()
            tt(gi_, gi_, s, ALU.subtract)
            v.drain()
            for j in range(6):
                for dr in range(2):
                    a, b = j * P, j * P + P
                    nc.vector.tensor_tensor_scan(s2[:, dr, a:b], gi_[:, dr, a:b], gi_[:, dr, a:b],
                                                 mrow[:, dr, j:j + 1], ALU.max, ALU.max)
                v.drain()
                for dr in range(2):
                    tt(mrow[:, dr, j + 1:j + 2], s[:, dr, b - 1:b], s2[:, dr, b - 1:b], ALU.add)
                v.drain()
            last = s2.rearrange("p a (c t) -> p a c t", t=P)[:, :, :, P - 1]
            tt(crow, mrow[:, :, 0:6], last, ALU.subtract)
            for j in range(6):
                for dr in range(2):
                    a, b = j * P, j * P + P
                    ts(r[:, dr, a:b], s2[:, dr, a:b], -1.0, mrow[:, dr, j:j + 1], ALU.mult, ALU.add)
                    ts(lf[:, dr, a:b], gi_[:, dr, a:b], s2[:, dr, b - 1:b], None, ALU.subtract)
            stt(z, s, -1.0, s2, ALU.mult, ALU.subtract)
            v.drain()
            ts(s2, s2, -1.0, None, ALU.mult)
            v.drain().then_inc(S["row_arg"], 1)
            meet(v)
            meet(v)
            nc.vector.memset(hs, 0.0)
            nc.vector.memset(Cn, 0.0)
            v.drain().then_inc(S["state_set"], 1)
            pen = (C["after"], C["before"])

            def lstm_score(u):
                j, dr, h = lstm_units[u]
                ps, free = get_a(v, "lstm", u)
                v.wait_ge(S["exp_arg"], u + 1)
                if u >= 2:
                    s, c = B("lstm", u - 2)
                    v.wait_ge(b_ready[s], c + 1)
                tt(lw[:, u % 2, 1, 0:P], ps[:, 0:P], lw[:, u % 2, 0, 0:P], ALU.mult).then_inc(S["score_set"], 1)
                t = LSTM_ORDER[dr][j]
                ts(lw[:, u % 2, 3, :], ps[:, 512:512 + P + 1], gcol[:, 0, 6 * dr + t, h:h + 1], None,
                   ALU.mult).then_inc(free, 1)

            def lstm_out(u):
                j, dr, h = lstm_units[u]
                t = LSTM_ORDER[dr][j]
                ps, free = get_b(v, "lstm", u)
                num = lw[:, u % 2, 3, :]
                v.drain()
                tt(num, num, ps[:, 0:P + 1], ALU.add)
                stt(Cn[:, dr, h, :], Cn[:, dr, h, :], carry[:, h, 6 * dr + j:6 * dr + j + 1], ps[:, 256:256 + P + 1],
                    ALU.mult, ALU.add).then_inc(free, 1)
                v.drain().then_inc(S["state_set"], 1)
                stt(den[:, 0:1], num[:, P:P + 1], -1.0, num[:, P:P + 1], ALU.mult, ALU.max)
                v.drain()
                tt(den[:, 0:1], den[:, 0:1], gcol[:, 1, 6 * dr + t, h:h + 1], ALU.max)
                v.drain()
                nc.vector.reciprocal(den[:, 1:2], den[:, 0:1])
                v.drain()
                stt(hs[:, t, h, :], num[:, 0:P], den[:, 1:2], hs[:, t, h, :], ALU.mult, ALU.add)

            for u, (j, dr, h) in enumerate(lstm_units):
                ps, _ = get_a(v, "lstm", u)
                tt(lw[:, u % 2, 0, 0:P], ps[:, P:2 * P], pen[dr], ALU.add).then_inc(S["lstm_d"], 1)
                if u >= 1:
                    lstm_out(u - 1)
                lstm_score(u)
            lstm_out(47)
            meet(v)
            v.wait_ge(S["hs_sq"], 1)
            nc.vector.reciprocal(hrs, hrs)
            v.drain()
            for t in range(6):
                for h in range(A_H):
                    ts(hs[:, t, h, :], hs[:, t, h, :], hrs[:, 4 * t + h:4 * t + h + 1], None, ALU.mult)
            meet(v)
            for h in range(A_H):
                for e, (a, b) in enumerate(((0, LAT), (LAT, TOK))):
                    ps, free = get_b(v, "hs", 2 * h + e)
                    stt(mixT2[:, h, a:b], ps[:, 0:b - a], vec("a_norm", h), oaT[:, h, a:b], ALU.mult,
                        ALU.mult).then_inc(free, 1)
            meet(v)
            attention("swa")
            meet(v)
            attention("swc")
            meet(v)
            gated("ab_out", 0, TOK)
            meet(v)
            rms(1, 0, "norm2", 3, TOK)
            nc.vector.memset(acc, 0.0)
            meet(v)
            mlp("mlp2", TOK)
            mlp_residual(0, TOK)
            meet(v)

            rms(2, 1, "norm1", 0, TOK)
            meet(v)
            for g in range(2):
                n = 4 if g == 0 else 2
                ps, free = get_a(v, "c_v", g)
                nc.vector.tensor_copy(vC[:, 4 * g:4 * g + n, :],
                                      ps[:, 0:256 * n].rearrange("p (t c) -> p t c", c=256)).then_inc(free, 1)
            meet(v)
            head_norms("c_n", "c_r", 6, 10, lambda m: qC[:, m, :] if m < 8 else kC[:, m - 8, :], rsc, rtc,
                       lambda m: cq8 if m < 8 else vec("ck", 0), C["cosC"], C["sinC"])
            meet(v)
            attention("cat")
            meet(v)
            gated("c_out", 1, LAT)
            meet(v)
            rms(3, 1, "norm2", 3, LAT)
            nc.vector.memset(acc, 0.0)
            meet(v)
            mlp("mlp3", LAT)
            mlp_residual(1, LAT)
            meet(v)
            for t in range(LT):
                for e in range(2):
                    ps, free = get_b(v, "out", 2 * t + e)
                    nc.vector.tensor_copy(xn[:, t, 512 * e:512 * e + 512], ps).then_inc(free, 1)
            v.drain().then_inc(out_set, 1)
            meet(v)

        assert len(set(met.values())) == 1, met


LRU_HALF = 8.0 / 2
PRE_LSTM, POST_LSTM = 20, 16


def host_constants():
    import numpy as np
    c = np.zeros((P, NCONST), np.float32)

    def put(name, a):
        lo, hi = CONST[name]
        c[:a.shape[0], lo:hi] = a

    i = np.arange(P)
    put("ident", np.eye(P))
    put("ones", np.ones((P, P)))
    put("ones64", (i[:, None] // 64 == i[None] // 64) * 1.0)
    for name, w in (("rot64", 64), ("rot128", 128)):
        r = np.zeros((P, P))
        for o in range(P):
            b, e = o // w * w, o % w
            if e < w // 2:
                r[b + e + w // 2, o] = -1
            else:
                r[b + e - w // 2, o] = 1
        put(name, r)
    put("after", np.where(i[:, None] <= i[None], 0.0, NEG))
    put("before", np.where(i[:, None] >= i[None], 0.0, NEG))
    put("dist", (LAT - P + i[:, None] - np.arange(LAT)[None]) * 1.0)
    pick = np.zeros((4, 4, P))
    for h in range(4):
        pick[h, h] = 1
    put("pick", pick.reshape(4, 4 * P))
    f = np.float32

    def axial(dim):
        rows = LAT // 64
        row = np.repeat(np.arange(rows), 64).astype(f)
        col = np.tile(np.arange(64), rows).astype(f)
        n = dim // 4
        inv = f(10000.0) ** (-np.arange(n, dtype=f) / f(n))
        ang = np.concatenate([row[:, None] * inv, col[:, None] * inv], -1)
        return np.cos(ang).T, np.sin(ang).T

    for name, dim in (("B", 64), ("C", 128)):
        cs, sn = axial(dim)
        put("cos" + name, np.tile(cs, (P // (dim // 2), 1)))
        put("sin" + name, np.tile(sn, (P // (dim // 2), 1)))
    freq = f(10000.0) ** (-np.arange(0, ROPE, 2, dtype=f) / f(ROPE))
    ang = (np.arange(LAT, dtype=f)[:, None] * freq[None]).T
    cs, sn = np.cos(ang), np.sin(ang)
    put("cosM", np.tile(np.concatenate([cs, cs]), (4, 1)))
    put("sinM", np.tile(np.concatenate([-sn, sn]), (4, 1)))
    put("eps", np.tile(np.array([[LN_EPS, RMS_EPS]]), (P, 1)))
    return c


_INS = ["x", "p", "ln1_g", "ln1_b", "ln2_g", "ln2_b", "mlp_w1", "mlp_w2", "ple_w_proj", "ple_w_gate", "hy_w_in",
        "hy_conv_w", "hy_conv_b", "hy_ga_w", "hy_ga_b", "hy_gx_w", "hy_gx_b", "hy_lambda", "hy_w_out", "mla_w_down",
        "mla_q_norm", "mla_kv_norm", "mla_w_uq", "mla_w_ukv", "mla_w_out", "c_2", "ctx_2", "c_ctx_2", "ada_w_2",
        "ada_b_2", "norm1_g_2", "norm2_g_2", "ab_w_in_2", "ab_gate_b_2", "mlstm_norm_g_2", "swa_q_norm_g_2",
        "swa_k_norm_g_2", "swa_sink_2", "ab_w_out_2", "c_w_in_2", "c_q_norm_g_2", "c_k_norm_g_2", "c_w_out_2",
        "mlp_w1_2", "mlp_w2_2"]


def kernel(**inputs):
    import numpy as _np
    import concourse.bacc as _bacc
    from concourse import mybir as _mybir
    from concourse.bass_utils import run_bass_kernel_spmd as _run

    nc = _bacc.Bacc("TRN2", target_bir_lowering=False, num_devices=1)
    arrays, args = {}, {}
    for name in _INS:
        a = _np.ascontiguousarray(inputs[name])
        arrays[f"in_{name}_dram"] = a
        args[name] = nc.dram_tensor(f"in_{name}_dram", a.shape, _mybir.dt.from_np(a.dtype), kind="ExternalInput").ap()
    c = host_constants()
    arrays["shape_constants_dram"] = c
    consts = nc.dram_tensor("shape_constants_dram", c.shape, _mybir.dt.float32, kind="ExternalInput").ap()
    out = nc.dram_tensor("out_0_dram", (1, LAT, D), _mybir.dt.float32, kind="ExternalOutput").ap()
    build(nc, args, consts, out)
    r = _run(nc, [arrays], core_ids=[0])
    return r.results[0]["out_0_dram"]
```

```python
from contextlib import ExitStack

import concourse.bass as bass
from concourse import mybir

F32 = mybir.dt.float32
F32R = mybir.dt.float32r
ALU = mybir.AluOpType
ACT = mybir.ActivationFunctionType
AX = mybir.AxisListType

P = 128
D = 1024
KD = D // P
LAT, CTX = 512, 256
TOK = LAT + CTX
LT, CT = LAT // P, CTX // P
ALPHA = (2 * 2) ** 0.25
LN_EPS, RMS_EPS = 1e-5, 1e-6
NEG = -1e30
TAKEN = -3e38

RNN = 512
RC = RNN // P
DSA_H, DSA_D, TOPK = 8, 64, 128
IDX_H, IDX_D = 4, 64
MLA_H, NOPE, ROPE, MLA_V = 16, 64, 32, 64
QL, KVL = 512, 256
A_H = 4
B_H, B_KV, B_D = 8, 2, 64
C_H, C_KV = 8, 2
N_MOD = 6
FF = 4 * D
GROUPS = 8
GF = FF // GROUPS
GH = GF // P
UNITS = 2 * GH
CW = 512
NW = 2
WORK = 30208

CONST_SIZES = [("ident", P), ("ones", P), ("ones64", P), ("rot64", P), ("rot128", P), ("after", P), ("before", P),
               ("dist", LAT), ("pick", 4 * P), ("cosB", LAT), ("sinB", LAT), ("cosC", LAT), ("sinC", LAT),
               ("cosM", LAT), ("sinM", LAT), ("eps", 2), ("pair", 4)]
CONST = {}
_at = 0
for _name, _n in CONST_SIZES:
    CONST[_name] = (_at, _at + _n)
    _at += _n
NCONST = _at

ROW_SIZES = [("ln1_g", 16), ("ln1_b", 16), ("ln2_g", 16), ("ln2_b", 16), ("conv_w", 16), ("conv_b", 4), ("ga_b", 4),
             ("gx_b", 4), ("lam", 4), ("q_norm", 4), ("kv_norm", 2), ("c", 8), ("c_ctx", 8), ("a_norm", 4),
             ("cq", 1), ("ck", 1), ("bq", 1), ("bk", 1), ("pad", 2),
             ("norm1", 16), ("norm2", 16), ("ada_b", 96)]
ROW = {}
_at = 0
for _name, _n in ROW_SIZES:
    ROW[_name] = _at
    _at += _n
NROW = _at
assert ROW["norm1"] == P and NROW == 2 * P

PLAN_A = [("hy_xr", 4), ("hy_yr", 4), ("hy_q", 4), ("hy_ki", 4), ("hy_v", 1), ("hy_gate", 8), ("idx", 6),
          ("dsa", 4 * DSA_H), ("hy_out", 8), ("ln_m0", 1), ("ln_v0", 1), ("ple_g0", 8), ("ple_p0", 8), ("mlp0", GROUPS * (GH + KD)),
          ("ln_m1", 1), ("ln_v1", 1),
          ("mla_cq", 4), ("mla_kv", 2), ("mla_kr", 1), ("mla_s", 2), ("uq", 12), ("ukv", 16),
          ("mla", 4 * MLA_H), ("mla_out", 8), ("ln_m2", 1), ("ln_v2", 1), ("ple_g1", 8), ("ple_p1", 8),
          ("mlp1", GROUPS * (GH + KD)), ("ln_m3", 1), ("ln_v3", 1),
          ("rms0", 1), ("ab_q", 4), ("ab_k", 4), ("ab_v", 6), ("ab_o", 4), ("ab_qb", 4), ("ab_kb", 2), ("ab_vb", 1),
          ("ab_g", 4), ("ab_n", 6), ("ab_r", 6), ("carry", 1), ("lstm", 48), ("swa", LT * B_H), ("swc", CT * B_H),
          ("ab_out", 8), ("rms1", 1), ("mlp2", GROUPS * (GH + KD)),
          ("rms2", 1), ("c_q", 8), ("c_k", 2), ("c_v", 2), ("c_n", 10), ("c_r", 10), ("cat", LT * C_H), ("c_out", 8),
          ("rms3", 1), ("mlp3", GROUPS * (GH + KD))]
PLAN_B = [("load", 17), ("dsa", 4 * DSA_H), ("dsa_o", 4), ("mla", 4 * MLA_H), ("mla_o", 8), ("ka", 6), ("cols", 1),
          ("lstm", 48), ("hs", 8), ("swa", 6 * B_H), ("swa_o", 4), ("swc", CT * B_H), ("swc_o", 4),
          ("cat", 2 * LT * C_H), ("cat_o", 8), ("out", 8)]


PLAN_W = [(f"mlp{i}", GROUPS * UNITS) for i in range(4)]


def bases(plan):
    at, base = 0, {}
    for name, n in plan:
        base[name] = at
        at += n
    return base


BASE_A, BASE_B, BASE_W = bases(PLAN_A), bases(PLAN_B), bases(PLAN_W)


def build(nc, d, consts, out):
    with ExitStack() as ctx:
        def sb(name, shape):
            return ctx.enter_context(nc.sbuf_tensor(name, shape, F32))

        def sem(name):
            return ctx.enter_context(nc.semaphore(name))

        const = sb("const", [P, NCONST])
        vecT = sb("vecT", [P, NROW])
        small = sb("small", [P, 660])
        xT = sb("xT", [P, KD, TOK])
        pT = sb("pT", [P, 2, 2, LAT])
        mod = sb("mod", [P, 2, N_MOD * KD, 2])
        wbuf = sb("wbuf", [P, NW, 8, CW])
        WORK_AT = -(-nc.sbuf_base // 32) * 32
        work = sb("work", [P, WORK])
        psA = ctx.enter_context(nc.psum_tensor("psA", [P, 2, 1024], F32))
        psB = ctx.enter_context(nc.psum_tensor("psB", [P, 2, 512], F32))
        psO = ctx.enter_context(nc.psum_tensor("psO", [P, 1024], F32))

        C = {name: const[:, a:b] for name, (a, b) in CONST.items()}
        ident, ones = C["ident"], C["ones"]
        eps_ln, eps_rms = C["eps"][:, 0:1], C["eps"][:, 1:2]

        def vec(name, j):
            return vecT[:, ROW[name] + j:ROW[name] + j + 1]

        cursor = [0]

        def area(*shape, at=None):
            if at is not None:
                cursor[0] = at
            n = 1
            for s in shape:
                n *= s
            v = work[:, cursor[0]:cursor[0] + n]
            cursor[0] += n
            assert cursor[0] <= WORK, cursor[0]
            if len(shape) == 2:
                return v.rearrange("p (a b) -> p a b", b=shape[1])
            if len(shape) == 3:
                return v.rearrange("p (a b c) -> p a b c", b=shape[1], c=shape[2])
            if len(shape) == 4:
                return v.rearrange("p (a b c e) -> p a b c e", b=shape[1], c=shape[2], e=shape[3])
            return v

        def split(name, shape, at):
            return nc.alloc_sbuf_tensor_at(name, shape, F32R, offset=WORK_AT + 4 * at)

        xn, cn, pn, rows = area(LT, D, at=0), area(CT, D), area(2, LT, 256), area(2, P)
        hT, gT = area(KD, TOK, at=0), area(KD, TOK, at=2 * KD * TOK)
        accs = {n: area(KD, n, at=0) for n in (LAT, TOK)}
        squares = area(KD, LAT, at=2 * KD * LAT)
        gates = area(KD, LAT, at=3 * KD * LAT)
        hraw = area(KD, TOK, at=3 * KD * TOK)
        nrm, rstd = area(TOK, at=4 * KD * TOK), area(TOK)
        acc = accs[LAT]
        SPLIT_W = 4 * KD * TOK + 2 * TOK
        hid_at = {n: 3 * KD * n for n in (LAT, TOK)}
        sH, sL = ({n: split(f"{h}{n}", [P, KD, n], (1 + e) * KD * n) for n in (LAT, TOK)}
                  for e, h in enumerate(("act_hi", "act_lo")))
        gH, gL = ({n: split(f"{h}{n}", [P, GH, n], hid_at[n] + e * GH * n) for n in (LAT, TOK)}
                  for e, h in enumerate(("hid_hi", "hid_lo")))
        hid = {n: area(2, n, at=hid_at[n] + 2 * GH * n) for n in (LAT, TOK)}
        wH, wL = (split(h, [P, 2, KD * P], SPLIT_W + e * 2 * KD * P) for e, h in enumerate(("w_hi", "w_lo")))
        MC = N_MOD * D // GROUPS
        adaw, adas = area(2, KD // 2, MC, at=3 * KD * TOK), area(2, MC)
        adarow = area(MC, at=hid_at[LAT] + 2 * GH * LAT + 2 * LAT)
        xpad = area(RC, LAT + 3, at=0)
        xc, yg, qT = area(RC, LAT), area(RC, LAT), area(RC, LAT)
        kT, iqT, ikT, vN, iw = area(LAT), area(2, LAT), area(LAT), area(LT, DSA_D), area(LT, IDX_H)
        gr, gi, t2, mixT0 = area(RC, LAT), area(RC, LAT), area(RC, LAT), area(KD, LAT)
        isc, relu, pens = area(LAT), area(2, LAT), area(4, LAT)
        prob0, turn0, biasb = area(2, LAT), area(2, LAT), area(2, LAT)
        gw = area(2, RC, P)
        on0 = gr
        lru = area(RC, LAT, at=0)
        qf, kf, vM = area(MLA_H, LAT, at=0), area(MLA_H, LAT), area(LT, MLA_H * MLA_V)
        cqT, ckvT, sq1, rs1 = area(4, LAT), area(2, LAT), area(4, LAT), area(2, LAT)
        rt, krt = area(2, LAT), area(2, LAT)
        on1 = area(LT, D, at=2 * MLA_H * LAT + LT * D)
        prob1, turn1 = area(2, LAT), area(2, LAT)
        mixT1 = area(KD, LAT, at=0)
        mixT2 = area(KD, TOK, at=0)
        qkb = area(6, TOK)
        vb = area(6, P)
        stage2 = cursor[0]
        qaT, kaT, kaN = area(A_H, TOK), area(A_H, TOK), area(6, A_H * P)
        vaN, oaT = area(6, A_H, P + 1), area(A_H, TOK)
        late = cursor[0]
        gI, gF = area(2, TOK), area(2, TOK)
        hs = area(6, A_H, P, at=late)
        R0, R1, R2, R3 = area(2, TOK, at=0), area(2, TOK), area(2, TOK), area(2, TOK)
        sqb, rsb, rtb = area(TOK, at=0), area(TOK), area(LAT)
        Cn = area(2, A_H, P + 1, at=0)
        lw = area(2, 4, P + 1)
        row_out = [R1, gF, R2, R0, R3]
        prob2, turn2 = area(2, 640, at=stage2), area(2, 640)
        on2 = area(LT, 512)
        mixT3 = area(KD, LAT, at=0)
        qC = area(KD, LAT, at=KD * TOK)
        kC, vC = area(C_KV, TOK), area(6, 256)
        sqc, rsc, rtc = area(TOK), area(TOK), area(LAT)
        prob3, turn3, on3 = area(2, TOK), area(2, TOK), area(LT, D)

        const_in, rows_in, x_in, p_in, bias_in = (sem(n) for n in
                                                 ("const_in", "rows_in", "x_in", "p_in", "bias_in"))
        gates_in = sem("gates_in")
        ada_landed = [sem(f"ada_landed{i}") for i in range(2)]
        a_ready, a_free = [sem(f"a_ready{i}") for i in range(2)], [sem(f"a_free{i}") for i in range(2)]
        b_ready, b_free = [sem(f"b_ready{i}") for i in range(2)], [sem(f"b_free{i}") for i in range(2)]
        w_landed = [sem(f"w_landed{i}") for i in range(NW)]
        o_ready, o_free = sem("o_ready"), sem("o_free")
        stage_over = sem("stage_over")
        out_set, out_stored = sem("out_set"), sem("out_stored")
        S = {n: sem(n) for n in (
            "centered", "squared", "relu_used", "act_hi", "act_split", "w_hi", "w_split", "g_hi", "hidden_set",
            "ada_used", "ada_sum", "row_ready", "row_set", "row_turned", "conv_set", "sqrt_set", "lam_exp", "lam_set",
            "bias_set", "bias_used", "dsa_max", "mla_max", "swa_max", "swc_max", "cat_max", "rope_raw", "head_sq",
            "onat_set", "kr_set", "rot_set", "rot_used", "abs_exp", "row_arg", "exp_arg", "lstm_d",
            "score_set", "kw_set", "state_set", "hs_sq")}

        def A(stage, j):
            n = BASE_A[stage] + j
            return n % 2, n // 2

        def B(stage, j):
            n = BASE_B[stage] + j
            return n % 2, n // 2

        def get_a(eng, stage, j, more=0):
            s, c = A(stage, j)
            eng.wait_ge(a_ready[s], more + (c + 1))
            return psA[:, s, :], a_free[s]

        def get_b(eng, stage, j):
            s, c = B(stage, j)
            eng.wait_ge(b_ready[s], c + 1)
            return psB[:, s, :], b_free[s]

        def emptied(eng, stage, j):
            s, c = A(stage, j)
            eng.wait_ge(a_free[s], c + 1)

        def turned(eng, stage, j):
            s, c = B(stage, j)
            eng.wait_ge(b_free[s], c + 1)

        met = {}

        def meet(eng):
            met[eng.engine] = met.get(eng.engine, 0) + 1
            eng.drain().then_inc(stage_over, 1)
            eng.wait_ge(stage_over, 4 * met[eng.engine])

        def tile_cols(w, a, b, kt=KD):
            return w[:, a:b].rearrange("(k p) c -> p k c", p=P), kt, b - a

        chunks = []

        def chunk(stage, last, *copies):
            slot, pairs = wbuf[:, len(chunks) % NW], []
            for col, src, kt, cols, *pitch in copies:
                if isinstance(cols, int):
                    pairs.append((slot[:, 0:kt, col:col + cols], src))
                else:
                    pitch = pitch[0] if pitch else cols[1]
                    for k in range(kt):
                        dst = slot[:, k, :].rearrange("p (h c) -> p h c", c=pitch)
                        h0, c0 = col // pitch, col % pitch
                        pairs.append((dst[:, h0:h0 + cols[0], c0:c0 + cols[1]], src[:, k]))
            chunks.append((stage, last, pairs))

        def mlp_chunks(name):
            for n in range(2 * GROUPS):
                chunks.append((name, ("split", name, GH * n + GH - 1), None))

        w = d["hy_w_in"][0]
        chunk("hy", ("hy_xr", 3), (0, *tile_cols(w, 0, 512)))
        chunk("hy", ("hy_yr", 3), (0, *tile_cols(w, 512, 1024)))
        chunk("hy", ("hy_q", 3), (0, *tile_cols(w, 1024, 1536)))
        chunk("hy", ("hy_ki", 3), (0, *tile_cols(w, 1536, 1600)), (64, *tile_cols(w, 1536, 1600)),
              (128, *tile_cols(w, 1664, 1920)), (384, *tile_cols(w, 1920, 1984)), (448, *tile_cols(w, 1920, 1984)))
        chunk("hy", ("hy_v", 0), (0, *tile_cols(w, 1600, 1664)), (64, *tile_cols(w, 1984, 1988)))

        def out_chunks(stage, w):
            for c in range(2):
                chunk(stage, (stage, 4 * c + 3), (0, *tile_cols(w, c * 512, c * 512 + 512)))

        def ple_chunks(l):
            for c in range(2):
                chunk(f"ple{l}", (f"ple_g{l}", 4 * c + 3), (0, *tile_cols(d["ple_w_gate"][l], c * 512, c * 512 + 512)))
            for c in range(2):
                chunk(f"ple{l}", (f"ple_p{l}", 4 * c + 3),
                      (0, *tile_cols(d["ple_w_proj"][l], c * 512, c * 512 + 512, 2)))

        out_chunks("hy_out", d["hy_w_out"][0])
        ple_chunks(0)
        mlp_chunks("mlp0")
        w = d["mla_w_down"][0]
        chunk("mla", ("mla_cq", 3), (0, *tile_cols(w, 0, 512)))
        chunk("mla", ("mla_kr", 0), (0, *tile_cols(w, 512, 800)), (288, *tile_cols(w, 784, 800)),
              (304, *tile_cols(w, 768, 784)))
        w = d["mla_w_uq"][0]
        def head_cols(w, kt, h0, width, a, b):
            v = w.rearrange("(k p) (h c) -> p k h c", p=P, c=width)[:, :, h0:h0 + 4, a:b]
            return v, kt, (4, b - a)

        for c in range(4):
            chunk("uq", ("uq", 3 * c + 2), (0, *head_cols(w, 4, 4 * c, 96, 0, 64)),
                  (256, *head_cols(w, 4, 4 * c, 96, 64, 96)), (384, *head_cols(w, 4, 4 * c, 96, 80, 96), 32),
                  (400, *head_cols(w, 4, 4 * c, 96, 64, 80), 32))
        w = d["mla_w_ukv"][0]
        for c in range(4):
            chunk("ukv", ("ukv", 4 * c + 3), (0, *head_cols(w, 2, 4 * c, 128, 0, 64)),
                  (256, *head_cols(w, 2, 4 * c, 128, 64, 128)))
        out_chunks("mla_out", d["mla_w_out"][0])
        ple_chunks(1)
        mlp_chunks("mlp1")
        w = d["ab_w_in_2"][0]
        for c, name in enumerate(("ab_q", "ab_k", "ab_v", "ab_o")):
            chunk("ab", (name, 5 if name == "ab_v" else 3), (0, *tile_cols(w, c * 512, c * 512 + 512)))
        chunk("ab", ("ab_qb", 3), (0, *tile_cols(w, 2064, 2576)))
        chunk("ab", ("ab_g", 3), (0, *tile_cols(w, 2576, 2640)), (64, *tile_cols(w, 2576, 2640)),
              (128, *tile_cols(w, 2640, 2704)), (192, *tile_cols(w, 2640, 2704)),
              (256, *tile_cols(w, 2704, 2832)), (384, *tile_cols(w, 2048, 2064)))
        out_chunks("ab_out", d["ab_w_out_2"][0])
        mlp_chunks("mlp2")
        w = d["c_w_in_2"][0]
        chunk("cin", ("c_q", 3), (0, *tile_cols(w, 0, 512)))
        chunk("cin", ("c_q", 7), (0, *tile_cols(w, 512, 1024)))
        chunk("cin", ("c_v", 1), (0, *tile_cols(w, 1024, 1536)))
        out_chunks("c_out", d["c_w_out_2"][0])
        mlp_chunks("mlp3")

        first_chunk, landed = {}, []
        count = [0] * NW
        for n, (stage, _, copies) in enumerate(chunks):
            first_chunk.setdefault(stage, n)
            count[n % NW] += 16 * (1 if copies is None else len(copies))
            landed.append(count[n % NW])
        MLP = {"mlp0": (d["mlp_w1"][0], d["mlp_w2"][0]), "mlp1": (d["mlp_w1"][1], d["mlp_w2"][1]),
               "mlp2": (d["mlp_w1_2"][0], d["mlp_w2_2"][0]), "mlp3": (d["mlp_w1_2"][1], d["mlp_w2_2"][1])}

        def weights(eng, stage, j, more=0):
            n = first_chunk[stage] + j
            eng.wait_ge(w_landed[n % NW], more + landed[n])
            return wbuf[:, n % NW]

        def mlp_unit(name, u):
            w = wbuf[:, (first_chunk[name] + u // GH) % NW]
            if u < GH:
                return w[:, :, u * P:u * P + P]
            return w.rearrange("p a b -> p (a b)").rearrange("p (k c) -> p k c", c=D)[:, :, (u - GH) * 256:(u - GH) * 256 + 256]

        def split_place(w, u, kt):
            return w[:, u % 2].rearrange("p (k c) -> p k c", k=kt)

        ADA_FREE = (6, 14)
        ADA = {"mlp0": 0, "mlp1": 1}

        def dsa_logits(qt, h):
            r = slice(64 * (h % 2), 64 * (h % 2) + 64)
            return [(0, (qt + 1) * P, [(qT[r, h // 2, qt * P:qt * P + P], kT[r, 0:(qt + 1) * P])])]

        def mla_logits(qt, h):
            r = slice(0, NOPE + ROPE)
            return [(0, (qt + 1) * P, [(qf[r, h, qt * P:qt * P + P], kf[r, h, 0:(qt + 1) * P])])]

        def window(qt):
            return list(range(max(qt - 1, 0), min(qt + 2, LT)))

        def swa_logits(qt, h, lat=True):
            r = slice(64 * (h % 2), 64 * (h % 2) + 64)
            kv = 4 + h // (B_H // B_KV)
            q = qkb[r, h // 2, (0 if lat else LAT) + qt * P:(0 if lat else LAT) + qt * P + P]
            parts = [(0, CTX, [(q, qkb[r, kv, LAT:TOK])])]
            if lat:
                for i, b in enumerate(window(qt)):
                    parts.append((CTX + i * P, CTX + i * P + P, [(q, qkb[r, kv, b * P:b * P + P])]))
            return parts

        def swa_masks(qt, h):
            m = []
            for i, b in enumerate(window(qt)):
                if b != qt:
                    m.append((CTX + i * P, CTX + i * P + P, C["after"] if b < qt else C["before"]))
            return m

        def cat_logits(qt, h):
            q, kv = qC[:, h, qt * P:qt * P + P], h // (C_H // C_KV)
            return [(0, LAT, [(q, kC[:, kv, 0:LAT])]), (LAT, TOK, [(q, kC[:, kv, LAT:TOK])])]

        def swa_v(lat):
            def v(qt, kb, h):
                t = LT + kb if kb < CT else window(qt)[kb - CT]
                kv = h // (B_H // B_KV)
                return vb[:, t, kv * B_D:kv * B_D + B_D]
            return v

        diag = C["before"]
        ATT = {
            "dsa": dict(H=DSA_H, QT=LT, dv=DSA_D, nkb=lambda qt: qt + 1, logits=dsa_logits,
                        masks=lambda qt, h: [(0, (qt + 1) * P, biasb[:, h % 2, 0:(qt + 1) * P])],
                        v=lambda qt, kb, h: vN[:, kb, :], prob=prob0, turn=turn0, onat=on0, sink=False),
            "mla": dict(H=MLA_H, QT=LT, dv=MLA_V, nkb=lambda qt: qt + 1, logits=mla_logits,
                        masks=lambda qt, h: [(qt * P, qt * P + P, diag)],
                        v=lambda qt, kb, h: vM[:, kb, h * MLA_V:h * MLA_V + MLA_V], prob=prob1, turn=turn1, onat=on1,
                        sink=False),
            "swa": dict(H=B_H, QT=LT, dv=B_D, nkb=lambda qt: CT + len(window(qt)), logits=swa_logits, masks=swa_masks,
                        v=swa_v(True), prob=prob2, turn=turn2, onat=on2, sink=True),
            "swc": dict(H=B_H, QT=CT, dv=B_D, nkb=lambda qt: CT, logits=lambda qt, h: swa_logits(qt, h, False),
                        masks=lambda qt, h: [], v=swa_v(False), prob=prob2,
                        turn=turn2, onat=on2, sink=True),
            "cat": dict(H=C_H, QT=LT, dv=P, nkb=lambda qt: 6, logits=cat_logits, masks=lambda qt, h: [],
                        v=lambda qt, kb, h: vC[:, kb, (h // 4) * P:(h // 4) * P + P], prob=prob3,
                        turn=turn3, onat=on3, sink=False),
        }
        n_o = {"dsa": 0, "mla": 4, "swa": 8, "swc": 12, "cat": 14}
        nmax, rsum, rinv, sink, sarg = small[:, 0:64], small[:, 64:128], small[:, 128:192], small[:, 192:200], small[:, 200:232]
        sp4, lz, ls, ls2, lacc = (small[:, 232 + 4 * i:236 + 4 * i] for i in range(5))
        m8 = small[:, 252:260]
        silu = small[:, 260:276]
        aff = small[:, 276:308].rearrange("p (a b) -> p a b", b=2)
        gcol = small[:, 308:500].rearrange("p (a b c) -> p a b c", b=12, c=4)
        carry = small[:, 500:548].rearrange("p (a b) -> p a b", b=12)
        hss, hrs = small[:, 548:572], small[:, 572:596]
        bI, bF = small[0:4, 596:598], small[0:4, 598:600]
        mrow = small[0:4, 600:614].rearrange("p (a b) -> p a b", b=7)
        crow = small[0:4, 614:626].rearrange("p (a b) -> p a b", b=6)
        den = small[:, 626:628]
        nsink = small[:, 630:638]
        bq8, cq8 = small[:, 638:639], small[:, 639:640]
        ln_squares = [KD * i for i in range(4)]
        rms_squares = [4 * KD + KD * i for i in range(4)]

        def turned_groups(name, qt):
            n = ATT[name]["nkb"](qt)
            return [range(g, min(g + 4, n)) for g in range(0, n, 4)]

        def units(name):
            s, at, r = ATT[name], 0, []
            for qt in range(s["QT"]):
                for h in range(s["H"]):
                    r.append((len(r), qt, h, at))
                    at += len(turned_groups(name, qt))
            return r

        def rows_of(ap):
            return ap.rearrange("(c p) -> c p", p=P)

        ROW_SRC = [("ln1_g", 0, rows_of(d["ln1_g"][0])), ("ln1_g", 8, rows_of(d["ln1_g"][1])),
                   ("ln1_b", 0, rows_of(d["ln1_b"][0])), ("ln1_b", 8, rows_of(d["ln1_b"][1])),
                   ("ln2_g", 0, rows_of(d["ln2_g"][0])), ("ln2_g", 8, rows_of(d["ln2_g"][1])),
                   ("ln2_b", 0, rows_of(d["ln2_b"][0])), ("ln2_b", 8, rows_of(d["ln2_b"][1])),
                   ("conv_w", 0, d["hy_conv_w"][0].rearrange("w (c p) -> (w c) p", p=P)),
                   ("conv_b", 0, rows_of(d["hy_conv_b"][0])), ("ga_b", 0, rows_of(d["hy_ga_b"][0])),
                   ("gx_b", 0, rows_of(d["hy_gx_b"][0])), ("lam", 0, rows_of(d["hy_lambda"][0])),
                   ("q_norm", 0, rows_of(d["mla_q_norm"][0])), ("kv_norm", 0, rows_of(d["mla_kv_norm"][0])),
                   ("c", 0, rows_of(d["c_2"][0])), ("c_ctx", 0, rows_of(d["c_ctx_2"])),
                   ("a_norm", 0, rows_of(d["mlstm_norm_g_2"][0])),
                   ("cq", 0, d["c_q_norm_g_2"]), ("ck", 0, d["c_k_norm_g_2"]), ("pad", 0, rows_of(d["c_ctx_2"])[0:2]),
                   ("norm1", 0, rows_of(d["norm1_g_2"][0])), ("norm1", 8, rows_of(d["norm1_g_2"][1])),
                   ("norm2", 0, rows_of(d["norm2_g_2"][0])), ("norm2", 8, rows_of(d["norm2_g_2"][1])),
                   ("ada_b", 0, rows_of(d["ada_b_2"][0])), ("ada_b", 48, rows_of(d["ada_b_2"][1]))]
        ROWS_IN = 16 * (len(ROW_SRC) + 4)
        GATES_IN = 16 * 4
        BIAS_IN = 16 * 5

        LSTM_ORDER = [[4, 5, 0, 1, 2, 3], [5, 4, 3, 2, 1, 0]]
        lstm_units = [(j, dr, h) for j in range(6) for dr in range(2) for h in range(A_H)]

        block = ctx.enter_context(nc.Block())

        @block.sync
        def _(sp):
            def used(n, more=0):
                if n >= NW:
                    if chunks[n - NW][1][0] == "split":
                        _, stage, u = chunks[n - NW][1]
                        sp.wait_ge(S["w_split"], more + (BASE_W[stage] + u + 1))
                    else:
                        s, c = A(*chunks[n - NW][1])
                        sp.wait_ge(a_ready[s], c + 1)

            n = 0
            while n < len(chunks):
                stage, last, copies = chunks[n]
                if copies is not None:
                    used(n)
                    for dst, src in copies:
                        sp.dma_start(dst, src).then_inc(w_landed[n % NW], 16)
                    n += 1
                    continue
                w1, w2 = MLP[stage]
                w1 = w1.rearrange("(k p) f -> p k f", p=P)

                def group(i, n0, more, first):
                    part = bass.ds(i * GF, GF)
                    used(n0, more)
                    sp.dma_start(wbuf[:, n0 % NW], w1[:, :, part]).then_inc(w_landed[n0 % NW], 16)
                    used(n0 + 1, more)
                    sp.dma_start(wbuf[:, (n0 + 1) % NW].rearrange("p a b -> p (a b)").rearrange("p (k c) -> p k c", c=D),
                                 w2[part, :].rearrange("(k p) c -> p k c", p=P)).then_inc(w_landed[(n0 + 1) % NW], 16)
                    if stage in ADA:
                        l = ADA[stage]
                        src = d["ada_w_2"][l].rearrange("(e k p) c -> e p k c", p=P, e=2)
                        for e in range(2):
                            if not first:
                                sp.wait_ge(S["ada_used"], 2 * (i - 1) + (2 * GROUPS * l + e + 1))
                            elif e == 0:
                                sp.wait_ge(stage_over, 4 * ADA_FREE[l])
                            sp.dma_start(adaw[:, e], src[e][:, :, bass.ds(i * MC, MC)]).then_inc(ada_landed[e], 16)

                group(0, n, 0, True)
                with sp.Fori(1, GROUPS) as i:
                    group(i, n + 2, (i - 1) * UNITS, False)
                n += 2 * GROUPS
            sp.wait_ge(out_set, 1)
            sp.dma_start(out[0].rearrange("(a p) d -> p a d", p=P), xn).then_inc(out_stored, 16)
            sp.wait_ge(out_stored, 16)

        @block.tensor
        def _(pe):
            def product(stage, j, parts, more=0):
                s, c = A(stage, j)
                if c > 0:
                    pe.wait_ge(a_free[s], more + c)
                for a, b, pairs in parts:
                    m = 1
                    for e in pairs[0][0].shape[1:]:
                        m *= e
                    for i, (l, r) in enumerate(pairs):
                        ins = pe.matmul(psA[0:m, s, a:b], l, r, start=(i == 0), stop=(i == len(pairs) - 1))
                ins.then_inc(a_ready[s], 1)

            def turn(stage, j, parts):
                s, c = B(stage, j)
                if c > 0:
                    pe.wait_ge(b_free[s], c)
                for col, src in parts:
                    k, m = src.shape[0], src.shape[1]
                    ins = pe.transpose(psB[0:m, s, col:col + k], src, ident[0:k, 0:k])
                ins.then_inc(b_ready[s], 1)

            def features(w, col, rhs, n, kt=KD, m=P):
                return [(a, b, [(w[:, k, col:col + m], rhs[:, k, a:b]) for k in range(kt)])
                        for a, b in ((0, min(n, 512)), (512, n)) if b > a]

            def tokens(w, a, b, lhs, t, at, kt=KD):
                return (at, at + b - a, [(lhs[:, k, t * P:t * P + P], w[:, k, a:b]) for k in range(kt)])

            def linear(stage, chunk_stage, c0, rhs, n, nchunks=2, kt=KD):
                for c in range(nchunks):
                    w = weights(pe, chunk_stage, c0 + c)
                    for m in range(4):
                        product(stage, 4 * c + m, features(w, m * P, rhs, n, kt))

            def attention(name):
                s = ATT[name]
                us = units(name)

                def turn_probs(u, qt, h, b0):
                    emptied(pe, name, u)
                    for g, kbs in enumerate(turned_groups(name, qt)):
                        turn(name, b0 + g, [((kb - kbs[0]) * P, s["prob"][:, u % 2, kb * P:kb * P + P]) for kb in kbs])

                def weigh_values(u, qt, h, b0):
                    for g in range(len(turned_groups(name, qt))):
                        turned(pe, name, b0 + g)
                    n = n_o[name] + qt
                    if h == 0 and n > 0:
                        pe.wait_ge(o_free, n)
                    nkb = s["nkb"](qt)
                    for kb in range(nkb):
                        ins = pe.matmul(psO[:, h * s["dv"]:(h + 1) * s["dv"]], s["turn"][:, u % 2, kb * P:kb * P + P],
                                        s["v"](qt, kb, h), start=(kb == 0), stop=(kb == nkb - 1))
                    if h == s["H"] - 1:
                        ins.then_inc(o_ready, 1)

                for step in range(len(us) + 2):
                    if step < len(us):
                        u, qt, h, _ = us[step]
                        product(name, u, s["logits"](qt, h))
                    if 0 <= step - 1 < len(us):
                        turn_probs(*us[step - 1])
                    if step >= 2:
                        weigh_values(*us[step - 2])
                pe.wait_ge(S["onat_set"], n_o[name] + s["QT"])
                width = s["H"] * s["dv"] // P
                for t in range(width):
                    turn(name + "_o", t, [(qt * P, s["onat"][:, qt, t * P:t * P + P]) for qt in range(s["QT"])])

            def layer_norm(i, x, n=LAT):
                product(f"ln_m{i}", 0, [(0, n, [(ones, x[:, k, 0:n]) for k in range(KD)])])
                pe.wait_ge(S["squared"], ln_squares[i] + KD)
                product(f"ln_v{i}", 0, [(0, n, [(ones, squares[:, k, :]) for k in range(KD)])])

            def rms(i, n):
                pe.wait_ge(S["squared"], rms_squares[i] + KD)
                product(f"rms{i}", 0, [(a, b, [(ones, gT[:, k, a:b]) for k in range(KD)])
                                       for a, b in ((0, 512), (512, n)) if b > a])

            def split_product(stage, j, n, pairs, more, steps=None):
                s, c = A(stage, j)
                pe.wait_ge(a_free[s], more + c)
                for a, b in ((0, min(n, 512)), (512, n)):
                    if b <= a:
                        continue
                    for k, (l_hi, l_lo, r_hi, r_lo) in enumerate(pairs):
                        if steps is not None and a == 0:
                            pe.wait_ge(S["hidden_set"], steps[k])
                        pe.matmul(psA[:, s, a:b], l_hi, r_hi[:, a:b], start=(k == 0), stop=False)
                        pe.matmul(psA[:, s, a:b], l_hi, r_lo[:, a:b], start=False, stop=False)
                        ins = pe.matmul(psA[:, s, a:b], l_lo, r_hi[:, a:b], start=False, stop=(k == len(pairs) - 1))
                ins.then_inc(a_ready[s], 1)

            def mlp(name, index, n):
                pe.wait_ge(S["act_split"], KD * (index + 1))
                with pe.Fori(0, GROUPS) as i:
                    more = i * ((GH + KD) // 2)
                    for m in range(GH):
                        pe.wait_ge(S["w_split"], i * UNITS + (BASE_W[name] + m + 1))
                        hi, lo = split_place(wH, m, KD), split_place(wL, m, KD)
                        split_product(name, m, n, [(hi[:, k, :], lo[:, k, :], sH[n][:, k, :], sL[n][:, k, :])
                                                   for k in range(KD)], more)
                    for q in range(GH):
                        u = GH + q
                        pe.wait_ge(S["w_split"], i * UNITS + (BASE_W[name] + u + 1))
                        hi, lo = split_place(wH, u, GH), split_place(wL, u, GH)
                        for e in range(2):
                            if name in ADA and (q, e) == (GH - 1, 1):
                                mod_rows(ADA[name], i)
                            c = slice(e * P, e * P + P)
                            split_product(name, GH + 2 * q + e, n, [(hi[:, k, c], lo[:, k, c], gH[n][:, k, :], gL[n][:, k, :])
                                                                    for k in range(GH)], more,
                                          [i * GH + (index * GH * GROUPS + k + 1) for k in range(GH)]
                                          if q == e == 0 else None)
                    if name in ADA:
                        mod_turn(ADA[name], i)

            def mod_rows(l, i):
                pe.wait_ge(S["ada_sum"], i + (GROUPS * l + 1))
                for a, b in ((0, 512), (512, MC)):
                    for e in range(2):
                        ins = pe.matmul(psO[0:2, a:b], C["pair"][:, 2 * e:2 * e + 2], adas[:, e, a:b],
                                        start=(e == 0), stop=(e == 1))
                ins.then_inc(S["row_ready"], 1)

            def mod_turn(l, i):
                pe.wait_ge(S["row_set"], i + (GROUPS * l + 1))
                for m in range(MC // P):
                    ins = pe.matmul(psB[:, 0, 2 * m:2 * m + 2], adarow[0:2, m * P:m * P + P], ident[0:2, 0:2],
                                    start=True, stop=True)
                ins.then_inc(S["row_turned"], 1)

            def ple(l):
                linear(f"ple_g{l}", f"ple{l}", 0, acc, LAT)
                linear(f"ple_p{l}", f"ple{l}", 2, pT[:, l], LAT, kt=2)

            pe.wait_ge(const_in, 16)
            pe.wait_ge(x_in, 32)
            for k in range(KD):
                turn("load", k, [(t * P, xn[:, t, k * P:k * P + P]) for t in range(LT)])
            for k in range(0, KD, 2):
                turn("load", 8 + k // 2, [(2 * P * e + t * P, cn[:, t, (k + e) * P:(k + e) * P + P])
                                          for e in range(2) for t in range(CT)])
            pe.wait_ge(p_in, 32)
            for l in range(2):
                for k in range(2):
                    turn("load", 12 + 2 * l + k, [(t * P, pn[:, l, t, k * P:k * P + P]) for t in range(LT)])
            pe.wait_ge(rows_in, ROWS_IN)
            turn("load", 16, [(0, rows[:, 0, :]), (P, rows[:, 1, :])])
            meet(pe)

            linear("hy_xr", "hy", 0, xT, LAT, 1)
            linear("hy_yr", "hy", 1, xT, LAT, 1)
            linear("hy_q", "hy", 2, xT, LAT, 1)
            linear("hy_ki", "hy", 3, xT, LAT, 1)
            w = weights(pe, "hy", 4)
            product("hy_v", 0, [tokens(w, 0, 68, xT, t, 68 * t) for t in range(LT)])
            meet(pe)
            pe.wait_ge(gates_in, GATES_IN)
            pe.wait_ge(S["conv_set"], 1)
            for c in range(RC):
                product("hy_gate", 2 * c, [(0, LAT, [(gw[:, 0, c, :], xc[:, c, :])])])
                product("hy_gate", 2 * c + 1, [(0, LAT, [(gw[:, 1, c, :], xc[:, c, :])])])
            for qt in range(1, LT):
                for hp in range(2):
                    product("idx", 2 * (qt - 1) + hp, [
                        (512 * e, 512 * e + (qt + 1) * P,
                         [(iqT[64 * e:64 * e + 64, hp, qt * P:qt * P + P], ikT[64 * e:64 * e + 64, 0:(qt + 1) * P])])
                        for e in range(2)])
            meet(pe)
            attention("dsa")
            meet(pe)
            linear("hy_out", "hy_out", 0, mixT0, LAT)
            meet(pe)
            layer_norm(0, xT)
            meet(pe)
            ple(0)
            meet(pe)
            mlp("mlp0", 0, LAT)
            meet(pe)
            layer_norm(1, acc)
            meet(pe)

            linear("mla_cq", "mla", 0, xT, LAT, 1)
            w = weights(pe, "mla", 1)
            for m in range(2):
                product("mla_kv", m, features(w, m * P, xT, LAT))
            product("mla_kr", 0, [(0, LAT, [(w[:, k, 256:288], xT[:, k, 0:LAT]) for k in range(KD)]),
                                  (512, 512 + LAT, [(w[:, k, 288:320], xT[:, k, 0:LAT]) for k in range(KD)])])
            emptied(pe, "mla_cq", 3)
            product("mla_s", 0, [(0, LAT, [(ones, sq1[:, k, :]) for k in range(4)])])
            emptied(pe, "mla_kv", 1)
            product("mla_s", 1, [(0, LAT, [(ones, rt[:, k, :]) for k in range(2)])])
            meet(pe)
            for c in range(4):
                w = weights(pe, "uq", c)
                for m in range(2):
                    product("uq", 3 * c + m, features(w, m * P, cqT, LAT, 4))
                product("uq", 3 * c + 2, [(0, LAT, [(w[:, k, 256:384], cqT[:, k, :]) for k in range(4)]),
                                          (512, 512 + LAT, [(w[:, k, 384:512], cqT[:, k, :]) for k in range(4)])])
            for c in range(4):
                w = weights(pe, "ukv", c)
                for m in range(2):
                    product("ukv", 4 * c + m, features(w, m * P, ckvT, LAT, 2))
                for m in range(2):
                    product("ukv", 4 * c + 2 + m, [
                        (256 * e, 256 * e + 256,
                         [(ckvT[:, k, (2 * m + e) * P:(2 * m + e) * P + P],
                           w[:, k, 256:512]) for k in range(2)])
                        for e in range(2)])
            meet(pe)
            attention("mla")
            meet(pe)
            linear("mla_out", "mla_out", 0, mixT1, LAT)
            meet(pe)
            layer_norm(2, xT)
            meet(pe)
            ple(1)
            meet(pe)
            mlp("mlp1", 1, LAT)
            meet(pe)
            layer_norm(3, acc)
            meet(pe)

            rms(0, TOK)
            meet(pe)
            linear("ab_q", "ab", 0, hT, TOK, 1)
            linear("ab_k", "ab", 1, hT, TOK, 1)
            w = weights(pe, "ab", 2)
            for t in range(6):
                product("ab_v", t, [tokens(w, 0, 512, hT, t, 0)])
            linear("ab_o", "ab", 3, hT, TOK, 1)
            linear("ab_qb", "ab", 4, hT, TOK, 1)
            w = weights(pe, "ab", 5)
            for m in range(2):
                product("ab_kb", m, features(w, m * P, hT, TOK))
            product("ab_vb", 0, [tokens(w, 256, 384, hT, t, P * t) for t in range(6)])
            for g, col in enumerate((0, 8, 4, 12)):
                product("ab_g", g, features(w, 384 + col, hT, TOK, m=4))
            meet(pe)
            for h in range(0, 6):
                turn("ka", h, [(P * hh, kaT[:, hh, h * P:h * P + P]) for hh in range(A_H)])
            for m in range(6):
                pe.wait_ge(S["head_sq"], m + 1)
                product("ab_n", m, [(a, b, [(C["ones64"], sqb[:, a:b])]) for a, b in ((0, 512), (512, TOK))])
            for m in range(6):
                pe.wait_ge(S["rope_raw"], m + 1)
                product("ab_r", m, [(0, LAT, [(C["rot64"], qkb[:, m, 0:LAT])])])
            meet(pe)
            meet(pe)
            turn("cols", 0, [(4 * (12 * q + 6 * dr + t), src[0:4, dr, t * P:t * P + P])
                             for q, src in enumerate(row_out[0:4]) for dr in range(2) for t in range(6)])
            product("carry", 0, [(12 * h, 12 * h + 12, [(C["pick"][0:4, h * P:h * P + P],
                                                        small[0:4, 614:626])]) for h in range(A_H)])
            meet(pe)

            def lstm_out(u):
                j, dr, h = lstm_units[u]
                t = LSTM_ORDER[dr][j]
                pe.wait_ge(S["score_set"], u + 1)
                pe.wait_ge(S["kw_set"], u + 1)
                s, c = B("lstm", u)
                pe.wait_ge(b_free[s], c)
                pe.matmul(psB[:, s, 0:P + 1], lw[:, u % 2, 1, 0:P], vaN[:, t, h, :], start=True, stop=True)
                pe.matmul(psB[:, s, 256:256 + P + 1], lw[:, u % 2, 2, 0:P], vaN[:, t, h, :],
                          start=True, stop=True).then_inc(b_ready[s], 1)

            for u, (j, dr, h) in enumerate(lstm_units):
                t = LSTM_ORDER[dr][j]
                cols = slice(t * P, t * P + P)
                pe.wait_ge(S["state_set"], 1 + max(u - 8 + 1, 0))
                product("lstm", u, [(0, P, [(kaT[:, h, cols], qaT[:, h, cols])]),
                                    (P, 2 * P, [(C["pick"][0:4, h * P:h * P + P], row_out[4][0:4, dr, cols])]),
                                    (512, 512 + P + 1, [(qaT[:, h, cols], Cn[:, dr, h, :])])])
                if u >= 1:
                    lstm_out(u - 1)
            lstm_out(47)
            meet(pe)
            meet(pe)
            for h in range(A_H):
                turn("hs", 2 * h, [(t * P, hs[:, t, h, :]) for t in range(LT)])
                turn("hs", 2 * h + 1, [(t * P, hs[:, LT + t, h, :]) for t in range(CT)])
            meet(pe)
            attention("swa")
            meet(pe)
            attention("swc")
            meet(pe)
            linear("ab_out", "ab_out", 0, mixT2, TOK)
            meet(pe)
            rms(1, TOK)
            meet(pe)
            mlp("mlp2", 2, TOK)
            meet(pe)

            rms(2, TOK)
            meet(pe)
            linear("c_q", "cin", 0, hT, LAT)
            w = weights(pe, "cin", 2)
            for m in range(2):
                product("c_k", m, features(w, m * P, hT, TOK))
            for g in range(2):
                product("c_v", g, [tokens(w, 256, 512, hT, t, 256 * (t - 4 * g)) for t in range(4 * g, min(4 * g + 4, 6))])
            meet(pe)
            for m in range(10):
                n = LAT if m < 8 else TOK
                pe.wait_ge(S["head_sq"], 6 + m + 1)
                product("c_n", m, [(a, b, [(ones, sqc[:, a:b])]) for a, b in ((0, 512), (512, n)) if b > a])
            for m in range(10):
                pe.wait_ge(S["rope_raw"], 6 + m + 1)
                product("c_r", m, [(0, LAT, [(C["rot128"], (qC[:, m, :] if m < 8 else kC[:, m - 8, 0:LAT]))])])
            meet(pe)
            attention("cat")
            meet(pe)
            linear("c_out", "c_out", 0, mixT3, LAT)
            meet(pe)
            rms(3, LAT)
            meet(pe)
            mlp("mlp3", 3, LAT)
            meet(pe)
            for t in range(LT):
                for e in range(2):
                    turn("out", 2 * t + e, [((k - 4 * e) * P, xT[:, k, t * P:t * P + P]) for k in range(4 * e, 4 * e + 4)])
            meet(pe)

        @block.scalar
        def _(act):
            def f(out, in_, func, **kw):
                return nc.scalar.activation(out, in_, func, **kw)

            act.dma_start(const[:, :], consts).then_inc(const_in, 16)
            act.dma_start(xn, d["x"][0].rearrange("(a p) d -> p a d", p=P)).then_inc(x_in, 16)
            act.dma_start(cn, d["ctx_2"][0].rearrange("(a p) d -> p a d", p=P)).then_inc(x_in, 16)
            for l in range(2):
                act.dma_start(pn[:, l], d["p"][l, 0].rearrange("(a p) d -> p a d", p=P)).then_inc(p_in, 16)
            for name, at, src in ROW_SRC:
                r = ROW[name] + at
                n = src.shape[0]
                act.dma_start(rows[r % P:r % P + n, r // P, :], src).then_inc(rows_in, 16)
            for name, src in (("bq", d["swa_q_norm_g_2"]), ("bk", d["swa_k_norm_g_2"])):
                for e in range(2):
                    act.dma_start(rows[ROW[name]:ROW[name] + 1, 0, 64 * e:64 * e + 64], src).then_inc(rows_in, 16)
            gb = d["ab_gate_b_2"].rearrange("a (g h) -> g h a", h=A_H)
            for dst, g in ((bI[:, 0:1], 0), (bI[:, 1:2], 2), (bF[:, 0:1], 1), (bF[:, 1:2], 3)):
                act.dma_start(dst, gb[g]).then_inc(bias_in, 16)
            act.dma_start(sink, d["swa_sink_2"][0:1, :].to_broadcast([P, B_H])).then_inc(bias_in, 16)
            meet(act)

            def attention(name, dst):
                s = ATT[name]
                us = units(name)

                def evacuate(u, qt, h, b0):
                    for g, kbs in enumerate(turned_groups(name, qt)):
                        ps, free = get_b(act, name, b0 + g)
                        f(s["turn"][:, u % 2, kbs[0] * P:(kbs[-1] + 1) * P], ps[:, 0:len(kbs) * P], ACT.Copy).then_inc(free, 1)

                for u, qt, h, b0 in us:
                    c, n = qt * s["H"] + h, s["nkb"](qt) * P
                    act.wait_ge(S[name + "_max"], u + 1)
                    if s["sink"]:
                        f(sarg[:, c:c + 1], sink[:, h:h + 1], ACT.Exp, bias=nmax[:, c:c + 1])
                    slot, _ = A(name, u)
                    f(s["prob"][:, u % 2, 0:n], psA[:, slot, 0:n], ACT.Exp, bias=nmax[:, c:c + 1],
                      accum_out=rsum[:, c:c + 1]).then_inc(a_free[slot], 1)
                    if u >= 1:
                        evacuate(*us[u - 1])
                evacuate(*us[-1])
                for t in range(s["H"] * s["dv"] // P):
                    ps, free = get_b(act, name + "_o", t)
                    f(dst(t), ps[:, 0:s["QT"] * P], ACT.Copy).then_inc(free, 1)

            def root(stage, j, dst, n, width, eps, cols=None):
                ps, free = get_a(act, stage, j)
                f(dst, ps[:, 0:n], ACT.Sqrt, scale=1.0 / width, bias=eps).then_inc(free, 1)

            def layer_norm(i, x, n=LAT):
                for k in range(KD):
                    act.wait_ge(S["centered"], KD * i + k + 1)
                    f(squares[:, k, :], x[:, k, 0:n], ACT.Square).then_inc(S["squared"], 1)
                root(f"ln_v{i}", 0, rstd[:, 0:n], n, D, eps_ln)

            def rms(i, n):
                for k in range(KD):
                    f(gT[:, k, 0:n], xT[:, k, 0:n], ACT.Square).then_inc(S["squared"], 1)
                root(f"rms{i}", 0, rstd[:, 0:n], n, D, eps_rms)

            def split_hi(x, n):
                for k in range(KD):
                    f(sH[n][:, k, :], x[:, k, 0:n], ACT.Copy).then_inc(S["act_hi"], 1)

            def ple(l):
                split_hi(acc, LAT)
                for j in range(KD):
                    ps, free = get_a(act, f"ple_g{l}", j)
                    f(gates[:, j, :], ps[:, 0:LAT], ACT.Sigmoid).then_inc(free, 1)

            def mlp(name, index, n):
                with act.Fori(0, GROUPS) as i:
                    more = i * ((GH + KD) // 2)

                    def w_hi(u):
                        if u % GH == 0:
                            weights(act, name, u // GH, i * 16)
                        if u < 2:
                            j = 2 * u - 3
                        else:
                            j = u - 2 if u - 2 < GH else GH + 2 * (u - 2 - GH) + 1
                        s, c = A(name, j)
                        act.wait_ge(a_ready[s], more + (c + 1))
                        f(split_place(wH, u, KD if u < GH else GH), mlp_unit(name, u), ACT.Copy).then_inc(S["w_hi"], 1)

                    w_hi(0)
                    w_hi(1)
                    for m in range(GH):
                        if m < GH - 1:
                            w_hi(m + 2)
                        g = hid[n][:, m % 2, :]
                        ps, free = get_a(act, name, m, more)
                        if m >= 2:
                            act.wait_ge(S["hidden_set"], i * GH + (index * GH * GROUPS + m - 1))
                        f(g, ps[:, 0:n], ACT.Relu).then_inc(free, 1)
                        act.drain()
                        f(g, g, ACT.Square)
                        act.drain()
                        f(gH[n][:, m, :], g, ACT.Copy).then_inc(S["g_hi"], 1)
                    w_hi(GH + 1)
                    w_hi(GH + 2)
                    w_hi(GH + 3)
                    if name in ADA:
                        act.wait_ge(S["row_ready"], i + (GROUPS * ADA[name] + 1))
                        f(adarow[0:2], psO[0:2, 0:MC], ACT.Copy).then_inc(S["row_set"], 1)

            f(lz, vecT[:, ROW["lam"]:ROW["lam"] + 4], ACT.Abs)
            act.drain()
            f(lz, lz, ACT.Exp, scale=-1.0).then_inc(S["lam_exp"], 1)
            for m in range(4):
                ps, free = get_a(act, "hy_xr", m)
                f(xpad[:, m, 3:3 + LAT], ps[:, 0:LAT], ACT.Copy).then_inc(free, 1)
            for m in range(4):
                ps, free = get_a(act, "hy_yr", m)
                f(yg[:, m, :], ps[:, 0:LAT], ACT.Gelu_apprx_tanh).then_inc(free, 1)
            for m in range(4):
                ps, free = get_a(act, "hy_q", m)
                f(qT[:, m, :], ps[:, 0:LAT], ACT.Copy, scale=DSA_D ** -0.5).then_inc(free, 1)
            for v, name in enumerate(("c", "c_ctx")):
                f(silu.rearrange("p (k v) -> p k v", v=2)[:, :, v], vecT[:, ROW[name]:ROW[name] + KD], ACT.Sigmoid)
            meet(act)
            for c in range(RC):
                for g, dst, name in ((0, gr, "ga_b"), (1, gi, "gx_b")):
                    ps, free = get_a(act, "hy_gate", 2 * c + g)
                    f(dst[:, c, :], ps[:, 0:LAT], ACT.Sigmoid, bias=vec(name, c)).then_inc(free, 1)
            act.drain()
            act.wait_ge(S["lam_set"], 1)
            for c in range(RC):
                f(t2[:, c, :], gr[:, c, :], ACT.Tanh, scale=sp4[:, c:c + 1])
            act.drain()
            f(gr, t2, ACT.Sqrt).then_inc(S["sqrt_set"], 1)
            for n in range(6):
                ps, free = get_a(act, "idx", n)
                nk = (n // 2 + 2) * P
                if n >= 1:
                    act.wait_ge(S["relu_used"], n)
                f(relu[:, :, 0:nk], ps.rearrange("p (e c) -> p e c", e=2)[:, :, 0:nk], ACT.Relu).then_inc(free, 1)
            meet(act)
            attention("dsa", lambda t: mixT0[:, RC + t, :])
            meet(act)
            meet(act)
            layer_norm(0, xT)
            meet(act)
            ple(0)
            meet(act)
            mlp("mlp0", 0, LAT)
            meet(act)
            layer_norm(1, acc)
            meet(act)

            for m in range(4):
                ps, free = get_a(act, "mla_cq", m)
                f(cqT[:, m, :], ps[:, 0:LAT], ACT.Copy)
                f(sq1[:, m, :], ps[:, 0:LAT], ACT.Square).then_inc(free, 1)
            for m in range(2):
                ps, free = get_a(act, "mla_kv", m)
                f(ckvT[:, m, :], ps[:, 0:LAT], ACT.Copy)
                f(rt[:, m, :], ps[:, 0:LAT], ACT.Square).then_inc(free, 1)
            root("mla_s", 0, rs1[:, 0, :], LAT, QL, eps_rms)
            root("mla_s", 1, rs1[:, 1, :], LAT, KVL, eps_rms)
            act.wait_ge(S["kr_set"], 1)
            for h in range(MLA_H):
                f(kf[64:96, h, :], krt[0:32, 0, :], ACT.Copy)
            meet(act)
            scale = (NOPE + ROPE) ** -0.5
            for c in range(4):
                for m in range(2):
                    ps, free = get_a(act, "uq", 3 * c + m)
                    h = 4 * c + 2 * m
                    f(qf[0:64, h, :], ps[0:64, 0:LAT], ACT.Copy, scale=scale)
                    f(qf[0:64, h + 1, :], ps[64:128, 0:LAT], ACT.Copy, scale=scale).then_inc(free, 1)
                act.wait_ge(S["rot_set"], c + 1)
                for e in range(4):
                    ins = f(qf[64:96, 4 * c + e, :], rt[32 * e:32 * e + 32, 0, :], ACT.Copy, scale=scale)
                ins.then_inc(S["rot_used"], 1)
            for c in range(4):
                for m in range(2):
                    ps, free = get_a(act, "ukv", 4 * c + m)
                    h = 4 * c + 2 * m
                    f(kf[0:64, h, :], ps[0:64, 0:LAT], ACT.Copy)
                    f(kf[0:64, h + 1, :], ps[64:128, 0:LAT], ACT.Copy).then_inc(free, 1)
            meet(act)
            attention("mla", lambda t: mixT1[:, t, :])
            meet(act)
            meet(act)
            layer_norm(2, xT)
            meet(act)
            ple(1)
            meet(act)
            mlp("mlp1", 1, LAT)
            meet(act)
            layer_norm(3, acc)
            meet(act)

            rms(0, TOK)
            meet(act)
            for m in range(4):
                ps, free = get_a(act, "ab_q", m)
                f(qaT[:, m, :], ps[:, 0:TOK], ACT.Copy).then_inc(free, 1)
            for m in range(4):
                ps, free = get_a(act, "ab_k", m)
                f(kaT[:, m, :], ps[:, 0:TOK], ACT.Copy, scale=P ** -0.5).then_inc(free, 1)
            for m in range(4):
                ps, free = get_a(act, "ab_o", m)
                f(oaT[:, m, :], ps[:, 0:TOK], ACT.Sigmoid).then_inc(free, 1)
            act.wait_ge(bias_in, BIAS_IN)
            for g in range(4):
                ps, free = get_a(act, "ab_g", g)
                dr, dst, b = g % 2, (gI, gF)[g // 2], (bI, bF)[g // 2]
                lat, cx = ps[0:4, 0:LAT], ps[0:4, LAT:TOK]
                if dr:
                    lat, cx = lat[:, ::-1], cx[:, ::-1]
                f(dst[0:4, dr, CTX:TOK], lat, ACT.Identity, bias=b[:, dr:dr + 1])
                f(dst[0:4, dr, 0:CTX], cx, ACT.Identity, bias=b[:, dr:dr + 1]).then_inc(free, 1)
            meet(act)
            for t in range(6):
                ps, free = get_b(act, "ka", t)
                f(kaN[:, t, :], ps[:, 0:512], ACT.Copy).then_inc(free, 1)

            def head_norms(stage, first, n, tile, sq, rs, width, cols):
                for m in range(n):
                    if m >= 1:
                        act.wait_ge(S["rope_raw"], first + m)
                    f(sq[:, 0:cols(m)], tile(m), ACT.Square).then_inc(S["head_sq"], 1)
                    root(stage, m, rs[:, 0:cols(m)], cols(m), width, eps_rms)

            head_norms("ab_n", 0, 6, lambda m: qkb[:, m, :], sqb, rsb, B_D, lambda m: TOK)
            meet(act)
            f(R0[0:4], gF[0:4], ACT.Abs)
            act.drain()
            f(R0[0:4], R0[0:4], ACT.Exp, scale=-1.0).then_inc(S["abs_exp"], 1)
            act.wait_ge(S["row_arg"], 1)
            f(crow, crow, ACT.Exp)
            for src, dst, func in ((R3, R1, ACT.Exp), (R2, R3, ACT.Copy), (gF, R2, ACT.Exp), (R0, gF, ACT.Exp),
                                   (gI, R0, ACT.Copy)):
                for dr in range(2):
                    lat, cx = src[0:4, dr, CTX:TOK], src[0:4, dr, 0:CTX]
                    if dr:
                        lat, cx = lat[:, ::-1], cx[:, ::-1]
                    f(dst[0:4, dr, 0:LAT], lat, func)
                    f(dst[0:4, dr, LAT:TOK], cx, func)
                act.drain()
            meet(act)
            ps, free = get_b(act, "cols", 0)
            f(small[:, 308:500], ps[:, 0:192], ACT.Copy).then_inc(free, 1)
            ps, free = get_a(act, "carry", 0)
            f(small[:, 500:548], ps[:, 0:48], ACT.Copy).then_inc(free, 1)
            meet(act)
            for u, (j, dr, h) in enumerate(lstm_units):
                t = LSTM_ORDER[dr][j]
                act.wait_ge(S["lstm_d"], u + 1)
                f(lw[:, u % 2, 0, 0:P], lw[:, u % 2, 0, 0:P], ACT.Exp,
                  bias=gcol[:, 3, 6 * dr + t, h:h + 1]).then_inc(S["exp_arg"], 1)
            meet(act)
            for t in range(6):
                for h in range(A_H):
                    f(qaT[:, h, t * P:t * P + P], hs[:, t, h, :], ACT.Square, accum_out=hss[:, 4 * t + h:4 * t + h + 1])
            act.drain()
            f(hrs, hss, ACT.Sqrt, scale=1.0 / P, bias=eps_rms).then_inc(S["hs_sq"], 1)
            meet(act)
            meet(act)
            attention("swa", lambda t: mixT2[:, 4 + t, 0:LAT])
            meet(act)
            attention("swc", lambda t: mixT2[:, 4 + t, LAT:TOK])
            meet(act)
            meet(act)
            rms(1, TOK)
            meet(act)
            split_hi(hraw, TOK)
            mlp("mlp2", 2, TOK)
            meet(act)

            rms(2, TOK)
            meet(act)
            for m in range(8):
                ps, free = get_a(act, "c_q", m)
                f(qC[:, m, :], ps[:, 0:LAT], ACT.Copy).then_inc(free, 1)
            for m in range(2):
                ps, free = get_a(act, "c_k", m)
                f(kC[:, m, :], ps[:, 0:TOK], ACT.Copy).then_inc(free, 1)
            meet(act)
            head_norms("c_n", 6, 10, lambda m: qC[:, m, :] if m < 8 else kC[:, m - 8, :], sqc, rsc, P,
                       lambda m: LAT if m < 8 else TOK)
            meet(act)
            attention("cat", lambda t: mixT3[:, t, :])
            meet(act)
            meet(act)
            rms(3, LAT)
            meet(act)
            split_hi(hraw, LAT)
            mlp("mlp3", 3, LAT)
            meet(act)
            meet(act)

        @block.gpsimd
        def _(pool):
            nc.gpsimd.memset(gw, 0.0)
            pool.drain()
            for g, name in enumerate(("hy_ga_w", "hy_gx_w")):
                for e in range(2):
                    src = d[name][0].rearrange("(c e) i o -> e i c o", e=2)[e]
                    pool.dma_start(gw[64 * e:64 * e + 64, g, :, 64 * e:64 * e + 64], src).then_inc(gates_in, 16)
            for _ in range(3):
                meet(pool)
            for u, qt, h, _ in units("dsa"):
                n = (qt + 1) * P
                if u >= 2:
                    pool.wait_ge(S["bias_used"], u - 1)
                b = biasb[:, u % 2, 0:n]
                slope = 2.0 ** (-8.0 * (h + 1) / DSA_H)
                nc.gpsimd.tensor_scalar(b, C["dist"][:, LAT - n:LAT], -slope, None, ALU.mult)
                pool.drain()
                pen = C["before"] if qt == 0 else pens[:, qt, 0:n]
                nc.gpsimd.tensor_tensor(b, b, pen, ALU.add).then_inc(S["bias_set"], 1)
            for _ in range(PRE_LSTM):
                meet(pool)
            for u, (j, dr, h) in enumerate(lstm_units):
                t = LSTM_ORDER[dr][j]
                if u >= 2:
                    s, c = B("lstm", u - 2)
                    pool.wait_ge(b_ready[s], c + 1)
                nc.gpsimd.tensor_scalar(lw[:, u % 2, 2, 0:P], kaN[:, t, h * P:h * P + P],
                                        gcol[:, 2, 6 * dr + t, h:h + 1], None, ALU.mult).then_inc(S["kw_set"], 1)
            for _ in range(POST_LSTM):
                meet(pool)

        @block.vector
        def _(v):
            ts, tt, stt = nc.vector.tensor_scalar, nc.vector.tensor_tensor, nc.vector.scalar_tensor_tensor

            def log1p(z, s, s2, r):
                ts(s, z, 2.0, None, ALU.add)
                v.drain()
                nc.vector.reciprocal(s, s)
                v.drain()
                tt(s, s, z, ALU.mult)
                v.drain()
                tt(s2, s, s, ALU.mult)
                v.drain()
                ts(r, s2, 1.0 / 15, None, ALU.mult)
                for n in (13, 11, 9, 7, 5, 3):
                    v.drain()
                    stt(r, r, 1.0 / n, s2, ALU.add, ALU.mult)
                v.drain()
                stt(r, r, 1.0, s, ALU.add, ALU.mult)
                v.drain()

            def attention(name):
                s = ATT[name]

                def finish(qt):
                    n = n_o[name] + qt
                    H, dv = s["H"], s["dv"]
                    c = slice(qt * H, qt * H + H)
                    v.wait_ge(o_ready, n + 1)
                    if s["sink"]:
                        tt(rsum[:, c], rsum[:, c], sarg[:, c], ALU.add)
                        v.drain()
                    nc.vector.reciprocal(rinv[:, c], rsum[:, c])
                    v.drain()
                    for h in range(H):
                        ins = ts(s["onat"][:, qt, h * dv:h * dv + dv], psO[:, h * dv:h * dv + dv],
                                 rinv[:, qt * H + h:qt * H + h + 1], None, ALU.mult)
                    ins.then_inc(o_free, 1)
                    v.drain().then_inc(S["onat_set"], 1)

                for u, qt, h, _ in units(name):
                    c, n = qt * s["H"] + h, s["nkb"](qt) * P
                    ps, _ = get_a(v, name, u)
                    if name == "dsa":
                        v.wait_ge(S["bias_set"], u + 1)
                    ins = None
                    for a, b, m in s["masks"](qt, h):
                        ins = tt(ps[:, a:b], ps[:, a:b], m, ALU.add)
                    if ins is not None:
                        if name == "dsa":
                            ins.then_inc(S["bias_used"], 1)
                        v.drain()
                    ins = nc.vector.tensor_reduce(nmax[:, c:c + 1], ps[:, 0:n], AX.X, ALU.max, negate=True)
                    if s["sink"]:
                        v.drain()
                        ins = tt(nmax[:, c:c + 1], nmax[:, c:c + 1], nsink[:, h:h + 1], ALU.min)
                    ins.then_inc(S[name + "_max"], 1)
                    if h == 1 and qt > 0:
                        finish(qt - 1)
                finish(s["QT"] - 1)

            def layer_norm(i, x, gain, bias, j0, dst, n=LAT):
                ps, free = get_a(v, f"ln_m{i}", 0)
                ts(nrm[:, 0:n], ps[:, 0:n], 1.0 / D, None, ALU.mult).then_inc(free, 1)
                v.drain()
                for k in range(KD):
                    tt(x[:, k, 0:n], x[:, k, 0:n], nrm[:, 0:n], ALU.subtract).then_inc(S["centered"], 1)
                emptied(v, f"ln_v{i}", 0)
                nc.vector.reciprocal(rstd[:, 0:n], rstd[:, 0:n])
                v.drain()
                for k in range(KD):
                    stt(dst[:, k, 0:n], x[:, k, 0:n], vec(gain, j0 + k), rstd[:, 0:n], ALU.mult, ALU.mult)
                v.drain()
                for k in range(KD):
                    ts(dst[:, k, 0:n], dst[:, k, 0:n], vec(bias, j0 + k), None, ALU.add)

            def rms(i, layer, norm, first, n, hT=hT):
                for k in range(KD):
                    ts(aff[:, k, :], mod[:, layer, (first + 1) * KD + k, :], 1.0, vec(norm, 8 * layer + k),
                       ALU.add, ALU.mult)
                emptied(v, f"rms{i}", 0)
                nc.vector.reciprocal(rstd[:, 0:n], rstd[:, 0:n])
                v.drain()
                spans = [(0, LAT, 0)] + ([(LAT, n, 1)] if n > LAT else [])
                for k in range(KD):
                    for a, b, e in spans:
                        stt(hT[:, k, a:b], xT[:, k, a:b], aff[:, k, e:e + 1], rstd[:, a:b], ALU.mult, ALU.mult)
                v.drain()
                for k in range(KD):
                    for a, b, e in spans:
                        ts(hT[:, k, a:b], hT[:, k, a:b], mod[:, layer, first * KD + k, e:e + 1], None, ALU.add)

            def residual(stage):
                for m in range(KD):
                    ps, free = get_a(v, stage, m)
                    stt(xT[:, m, 0:LAT], xT[:, m, 0:LAT], ALPHA, ps[:, 0:LAT], ALU.mult, ALU.add).then_inc(free, 1)

            def gated(stage, layer, n):
                spans = [(0, LAT, 0)] + ([(LAT, n, 1)] if n > LAT else [])
                for m in range(KD):
                    ps, free = get_a(v, stage, m)
                    for a, b, e in spans:
                        ins = stt(xT[:, m, a:b], ps[:, a:b], mod[:, layer, 2 * KD + m, e:e + 1], xT[:, m, a:b],
                                  ALU.mult, ALU.add)
                    ins.then_inc(free, 1)

            def split_lo(x, index, n):
                for k in range(KD):
                    v.wait_ge(S["act_hi"], index * KD + k + 1)
                    tt(sL[n][:, k, :], x[:, k, 0:n], sH[n][:, k, :], ALU.subtract).then_inc(S["act_split"], 1)

            def ple(l):
                split_lo(acc, l, LAT)
                emptied(v, f"ple_g{l}", 7)
                for j in range(KD):
                    ps, free = get_a(v, f"ple_p{l}", j)
                    tt(gates[:, j, :], gates[:, j, :], ps[:, 0:LAT], ALU.mult).then_inc(free, 1)
                v.drain()
                for j in range(KD):
                    stt(acc[:, j, :], acc[:, j, :], ALPHA, gates[:, j, :], ALU.mult, ALU.add)

            def mlp(name, index, n):
                acc = accs[n]
                with v.Fori(0, GROUPS) as i:
                    more = i * ((GH + KD) // 2)

                    def w_lo(u):
                        v.wait_ge(S["w_hi"], i * UNITS + (BASE_W[name] + u + 1))
                        kt = KD if u < GH else GH
                        tt(split_place(wL, u, kt), mlp_unit(name, u), split_place(wH, u, kt),
                           ALU.subtract).then_inc(S["w_split"], 1)

                    def hidden_lo(m):
                        v.wait_ge(S["g_hi"], i * GH + (index * GH * GROUPS + m + 1))
                        tt(gL[n][:, m, :], hid[n][:, m % 2, :], gH[n][:, m, :], ALU.subtract).then_inc(S["hidden_set"], 1)

                    def add_up(j):
                        ps, free = get_a(v, name, GH + j, more)
                        tt(acc[:, j, :], acc[:, j, :], ps[:, 0:n], ALU.add).then_inc(free, 1)

                    def modulations(k):
                        if name not in ADA:
                            return
                        l, e, r = ADA[name], k // (KD // 2), k % (KD // 2)
                        if r == 0:
                            v.wait_ge(ada_landed[e], i * 16 + (16 * GROUPS * l + 16))
                        for x in range(2):
                            c = silu[:, 2 * k + x:2 * k + x + 1]
                            if k == 0:
                                ts(adas[:, x, :], adaw[:, e, r, :], c, None, ALU.mult)
                            else:
                                ins = stt(adas[:, x, :], adaw[:, e, r, :], c, adas[:, x, :], ALU.mult, ALU.add)
                        if r == KD // 2 - 1:
                            ins.then_inc(S["ada_used"], 1)
                        if k == KD - 1:
                            v.drain().then_inc(S["ada_sum"], 1)
                        else:
                            v.drain()

                    w_lo(0)
                    w_lo(1)
                    modulations(0)
                    modulations(1)
                    for m in range(GH):
                        if m < GH - 1:
                            w_lo(m + 2)
                        hidden_lo(m)
                        if m < GH - 1:
                            modulations(2 + m)
                    w_lo(GH + 1)
                    for q in range(GH):
                        add_up(2 * q)
                        add_up(2 * q + 1)
                        if q < GH - 2:
                            w_lo(GH + 2 + q)
                        if q < GH - 1:
                            modulations(5 + q)
                    if name in ADA:
                        v.wait_ge(S["row_turned"], i + (GROUPS * ADA[name] + 1))
                        nc.vector.tensor_copy(mod[:, ADA[name], bass.ds(i * (MC // P), MC // P), :],
                                              psB[:, 0, 0:2 * MC // P].rearrange("p (a b) -> p a b", b=2))
                    v.drain()
                if name in ADA:
                    l = ADA[name]
                    b = vecT[:, ROW["ada_b"] + 48 * l:ROW["ada_b"] + 48 * l + 48]
                    for x in range(2):
                        tt(mod[:, l, :, x], mod[:, l, :, x], b, ALU.add)

            def mlp_residual(layer, n):
                acc = accs[n]
                v.drain()
                for k in range(KD):
                    for a, b, e in [(0, LAT, 0)] + ([(LAT, n, 1)] if n > LAT else []):
                        stt(xT[:, k, a:b], acc[:, k, a:b], mod[:, layer, 5 * KD + k, e:e + 1], xT[:, k, a:b],
                            ALU.mult, ALU.add)

            for k in range(KD):
                ps, free = get_b(v, "load", k)
                nc.vector.tensor_copy(xT[:, k, 0:LAT], ps).then_inc(free, 1)
            for k in range(0, KD, 2):
                ps, free = get_b(v, "load", 8 + k // 2)
                nc.vector.tensor_copy(xT[:, k:k + 2, LAT:TOK], ps.rearrange("p (a b) -> p a b", a=2)).then_inc(free, 1)
            for l in range(2):
                for k in range(2):
                    ps, free = get_b(v, "load", 12 + 2 * l + k)
                    nc.vector.tensor_copy(pT[:, l, k, :], ps).then_inc(free, 1)
            ps, free = get_b(v, "load", 16)
            nc.vector.tensor_copy(vecT[:, :], ps[:, 0:NROW]).then_inc(free, 1)
            meet(v)

            v.wait_ge(bias_in, BIAS_IN)
            ts(nsink, sink, -1.0, None, ALU.mult)
            ts(bq8, vec("bq", 0), B_D ** -0.5, None, ALU.mult)
            ts(cq8, vec("cq", 0), P ** -0.5, None, ALU.mult)
            nc.vector.memset(xpad[:, :, 0:3], 0.0)
            v.wait_ge(S["lam_exp"], 1)
            log1p(lz, ls, ls2, lacc)
            ts(ls, vecT[:, ROW["lam"]:ROW["lam"] + 4], -1.0, 0.0, ALU.mult, ALU.max)
            v.drain()
            stt(sp4, lacc, 2.0, ls, ALU.mult, ALU.add)
            v.drain()
            ts(sp4, sp4, LRU_HALF, None, ALU.mult).then_inc(S["lam_set"], 1)
            for m in range(3):
                ps, free = get_a(v, "hy_ki", m)
                nc.vector.tensor_copy(kT if m == 0 else iqT[:, m - 1, :], ps[:, 0:LAT]).then_inc(free, 1)
            ps, free = get_a(v, "hy_ki", 3)
            nc.vector.tensor_copy(ikT, ps[:, 0:LAT]).then_inc(free, 1)
            ps, free = get_a(v, "hy_v", 0)
            ps = ps[:, 0:4 * 68].rearrange("p (t c) -> p t c", c=68)
            nc.vector.tensor_copy(vN, ps[:, :, 0:64])
            ts(iw, ps[:, :, 64:68], IDX_H ** -0.5 * IDX_D ** -0.5, None, ALU.mult).then_inc(free, 1)
            meet(v)
            s16 = silu.rearrange("p (k v) -> p k v", v=2)
            for e, name in enumerate(("c", "c_ctx")):
                tt(s16[:, :, e], s16[:, :, e], vecT[:, ROW[name]:ROW[name] + KD], ALU.mult)
            for c in range(RC):
                ts(xc[:, c, :], xpad[:, c, 0:LAT], vec("conv_w", c), vec("conv_b", c), ALU.mult, ALU.add)
            for i in range(1, 4):
                v.drain()
                for c in range(RC):
                    stt(xc[:, c, :], xpad[:, c, i:i + LAT], vec("conv_w", RC * i + c), xc[:, c, :], ALU.mult, ALU.add)
            v.drain().then_inc(S["conv_set"], 1)
            v.wait_ge(S["sqrt_set"], 1)
            ts(lru, t2, 1.0, None, ALU.add)
            v.drain()
            nc.vector.reciprocal(lru, lru)
            tt(gi, gi, xc, ALU.mult)
            v.drain()
            tt(gr, gr, lru, ALU.mult)
            ts(t2, t2, -1.0, 1.0, ALU.mult, ALU.add)
            v.drain()
            stt(gi, gi, 2.0, gr, ALU.mult, ALU.mult)
            tt(t2, t2, lru, ALU.mult)
            v.drain()
            for c in range(RC):
                nc.vector.tensor_tensor_scan(xc[:, c, :], t2[:, c, :], gi[:, c, :], 0.0, ALU.mult, ALU.add)
            v.drain()
            tt(mixT0[:, 0:RC, :], xc, yg, ALU.mult)
            for qt in range(1, LT):
                nk = (qt + 1) * P
                s = isc[:, 0:nk]
                for hp in range(2):
                    n = 2 * (qt - 1) + hp
                    emptied(v, "idx", n)
                    for e in range(2):
                        h = 2 * hp + e
                        if h == 0:
                            ts(s, relu[:, 0, 0:nk], iw[:, qt, 0:1], None, ALU.mult)
                        else:
                            ins = stt(s, relu[:, e, 0:nk], iw[:, qt, h:h + 1], s, ALU.mult, ALU.add)
                            if e == 1:
                                ins.then_inc(S["relu_used"], 1)
                        v.drain()
                tt(isc[:, qt * P:nk], isc[:, qt * P:nk], C["before"], ALU.add)
                v.drain()
                for _ in range(TOPK // 8):
                    nc.vector.max(m8, s)
                    v.drain()
                    nc.vector.match_replace(s, m8, s, TAKEN)
                    v.drain()
                ts(pens[:, qt, 0:nk], s, TAKEN, 1.0, ALU.is_equal, ALU.subtract)
                v.drain()
                ts(pens[:, qt, 0:nk], pens[:, qt, 0:nk], -NEG, None, ALU.mult)
            meet(v)
            attention("dsa")
            meet(v)
            residual("hy_out")
            meet(v)
            layer_norm(0, xT, "ln1_g", "ln1_b", 0, acc)
            meet(v)
            ple(0)
            meet(v)
            mlp("mlp0", 0, LAT)
            meet(v)
            layer_norm(1, acc, "ln2_g", "ln2_b", 0, xT)
            meet(v)

            ps, free = get_a(v, "mla_kr", 0)
            tt(krt[0:32, 0, :], ps[0:32, 0:512], C["cosM"][0:32], ALU.mult)
            tt(krt[0:32, 1, :], ps[0:32, 512:1024], C["sinM"][0:32], ALU.mult).then_inc(free, 1)
            v.drain()
            tt(krt[0:32, 0, :], krt[0:32, 0, :], krt[0:32, 1, :], ALU.add).then_inc(S["kr_set"], 1)
            for j, (t, n, name) in enumerate(((cqT, 4, "q_norm"), (ckvT, 2, "kv_norm"))):
                emptied(v, "mla_s", j)
                nc.vector.reciprocal(rs1[:, j, :], rs1[:, j, :])
                v.drain()
                for k in range(n):
                    stt(t[:, k, :], t[:, k, :], vec(name, k), rs1[:, j, :], ALU.mult, ALU.mult)
            meet(v)
            for c in range(4):
                ps, free = get_a(v, "uq", 3 * c + 2)
                if c >= 1:
                    v.wait_ge(S["rot_used"], c)
                tt(rt[:, 0, :], ps[:, 0:512], C["cosM"], ALU.mult)
                tt(rt[:, 1, :], ps[:, 512:1024], C["sinM"], ALU.mult).then_inc(free, 1)
                v.drain()
                tt(rt[:, 0, :], rt[:, 0, :], rt[:, 1, :], ALU.add).then_inc(S["rot_set"], 1)
            for c in range(4):
                for m in range(2):
                    ps, free = get_a(v, "ukv", 4 * c + 2 + m)
                    nc.vector.tensor_copy(vM[:, 2 * m:2 * m + 2, 256 * c:256 * c + 256],
                                          ps[:, 0:512].rearrange("p (e c) -> p e c", e=2)).then_inc(free, 1)
            meet(v)
            attention("mla")
            meet(v)
            residual("mla_out")
            meet(v)
            layer_norm(2, xT, "ln1_g", "ln1_b", 8, acc)
            meet(v)
            ple(1)
            meet(v)
            mlp("mlp1", 1, LAT)
            meet(v)
            layer_norm(3, acc, "ln2_g", "ln2_b", 8, xT)
            meet(v)
            rms(0, 0, "norm1", 0, TOK)
            meet(v)
            nc.vector.memset(vaN[:, :, :, P:P + 1], 1.0)
            for t in range(6):
                ps, free = get_a(v, "ab_v", t)
                nc.vector.tensor_copy(vaN[:, t, :, 0:P], ps[:, 0:512].rearrange("p (h c) -> p h c", h=A_H)).then_inc(free, 1)
            for m in range(6):
                ps, free = get_a(v, "ab_qb", m) if m < 4 else get_a(v, "ab_kb", m - 4)
                nc.vector.tensor_copy(qkb[:, m, :], ps[:, 0:TOK]).then_inc(free, 1)
            ps, free = get_a(v, "ab_vb", 0)
            nc.vector.tensor_copy(vb, ps[:, 0:TOK].rearrange("p (t c) -> p t c", t=6)).then_inc(free, 1)
            meet(v)

            def head_norms(norm_stage, rope_stage, first, n, tile, rs, tmp, gain, cos, sin):
                for m in range(n):
                    emptied(v, norm_stage, m)
                    x = tile(m)
                    r = rs[:, 0:x.shape[-1]]
                    nc.vector.reciprocal(r, r)
                    v.drain()
                    stt(x, x, gain(m), r, ALU.mult, ALU.mult).then_inc(S["rope_raw"], 1)
                for m in range(n):
                    ps, free = get_a(v, rope_stage, m)
                    x = tile(m)[:, 0:LAT]
                    tt(tmp, ps[:, 0:LAT], sin, ALU.mult).then_inc(free, 1)
                    tt(x, x, cos, ALU.mult)
                    v.drain()
                    tt(x, x, tmp, ALU.add)
                    v.drain()

            head_norms("ab_n", "ab_r", 0, 6, lambda m: qkb[:, m, :], rsb, rtb,
                       lambda m: bq8 if m < 4 else vec("bk", 0), C["cosB"], C["sinB"])
            meet(v)
            v.wait_ge(S["abs_exp"], 1)
            z, s, s2, r = (x[0:4] for x in (R0, R1, R2, R3))
            log1p(z, s, s2, r)
            lf, gi_ = gF[0:4], gI[0:4]
            ts(lf, lf, 0.0, None, ALU.min)
            nc.vector.memset(z, 1.0)
            v.drain()
            stt(lf, r, -2.0, lf, ALU.mult, ALU.add)
            nc.vector.memset(z.rearrange("p a (c t) -> p a c t", t=P)[:, :, :, 0:1], 0.0)
            nc.vector.memset(mrow, 0.0)
            v.drain()
            flat = lambda x: x.rearrange("p a b -> p (a b)")
            nc.vector.tensor_tensor_scan(flat(s), flat(z), flat(lf), 0.0, ALU.mult, ALU.add)
            v.drain()
            tt(gi_, gi_, s, ALU.subtract)
            v.drain()
            for j in range(6):
                for dr in range(2):
                    a, b = j * P, j * P + P
                    nc.vector.tensor_tensor_scan(s2[:, dr, a:b], gi_[:, dr, a:b], gi_[:, dr, a:b],
                                                 mrow[:, dr, j:j + 1], ALU.max, ALU.max)
                v.drain()
                for dr in range(2):
                    tt(mrow[:, dr, j + 1:j + 2], s[:, dr, b - 1:b], s2[:, dr, b - 1:b], ALU.add)
                v.drain()
            last = s2.rearrange("p a (c t) -> p a c t", t=P)[:, :, :, P - 1]
            tt(crow, mrow[:, :, 0:6], last, ALU.subtract)
            for j in range(6):
                for dr in range(2):
                    a, b = j * P, j * P + P
                    ts(r[:, dr, a:b], s2[:, dr, a:b], -1.0, mrow[:, dr, j:j + 1], ALU.mult, ALU.add)
                    ts(lf[:, dr, a:b], gi_[:, dr, a:b], s2[:, dr, b - 1:b], None, ALU.subtract)
            stt(z, s, -1.0, s2, ALU.mult, ALU.subtract)
            v.drain()
            ts(s2, s2, -1.0, None, ALU.mult)
            v.drain().then_inc(S["row_arg"], 1)
            meet(v)
            meet(v)
            nc.vector.memset(hs, 0.0)
            nc.vector.memset(Cn, 0.0)
            v.drain().then_inc(S["state_set"], 1)
            pen = (C["after"], C["before"])

            def lstm_score(u):
                j, dr, h = lstm_units[u]
                ps, free = get_a(v, "lstm", u)
                v.wait_ge(S["exp_arg"], u + 1)
                if u >= 2:
                    s, c = B("lstm", u - 2)
                    v.wait_ge(b_ready[s], c + 1)
                tt(lw[:, u % 2, 1, 0:P], ps[:, 0:P], lw[:, u % 2, 0, 0:P], ALU.mult).then_inc(S["score_set"], 1)
                t = LSTM_ORDER[dr][j]
                ts(lw[:, u % 2, 3, :], ps[:, 512:512 + P + 1], gcol[:, 0, 6 * dr + t, h:h + 1], None,
                   ALU.mult).then_inc(free, 1)

            def lstm_out(u):
                j, dr, h = lstm_units[u]
                t = LSTM_ORDER[dr][j]
                ps, free = get_b(v, "lstm", u)
                num = lw[:, u % 2, 3, :]
                v.drain()
                tt(num, num, ps[:, 0:P + 1], ALU.add)
                stt(Cn[:, dr, h, :], Cn[:, dr, h, :], carry[:, h, 6 * dr + j:6 * dr + j + 1], ps[:, 256:256 + P + 1],
                    ALU.mult, ALU.add).then_inc(free, 1)
                v.drain().then_inc(S["state_set"], 1)
                stt(den[:, 0:1], num[:, P:P + 1], -1.0, num[:, P:P + 1], ALU.mult, ALU.max)
                v.drain()
                tt(den[:, 0:1], den[:, 0:1], gcol[:, 1, 6 * dr + t, h:h + 1], ALU.max)
                v.drain()
                nc.vector.reciprocal(den[:, 1:2], den[:, 0:1])
                v.drain()
                stt(hs[:, t, h, :], num[:, 0:P], den[:, 1:2], hs[:, t, h, :], ALU.mult, ALU.add)

            for u, (j, dr, h) in enumerate(lstm_units):
                ps, _ = get_a(v, "lstm", u)
                tt(lw[:, u % 2, 0, 0:P], ps[:, P:2 * P], pen[dr], ALU.add).then_inc(S["lstm_d"], 1)
                if u >= 1:
                    lstm_out(u - 1)
                lstm_score(u)
            lstm_out(47)
            meet(v)
            v.wait_ge(S["hs_sq"], 1)
            nc.vector.reciprocal(hrs, hrs)
            v.drain()
            for t in range(6):
                for h in range(A_H):
                    ts(hs[:, t, h, :], hs[:, t, h, :], hrs[:, 4 * t + h:4 * t + h + 1], None, ALU.mult)
            meet(v)
            for h in range(A_H):
                for e, (a, b) in enumerate(((0, LAT), (LAT, TOK))):
                    ps, free = get_b(v, "hs", 2 * h + e)
                    stt(mixT2[:, h, a:b], ps[:, 0:b - a], vec("a_norm", h), oaT[:, h, a:b], ALU.mult,
                        ALU.mult).then_inc(free, 1)
            meet(v)
            attention("swa")
            meet(v)
            attention("swc")
            meet(v)
            gated("ab_out", 0, TOK)
            meet(v)
            rms(1, 0, "norm2", 3, TOK, hraw)
            nc.vector.memset(accs[TOK], 0.0)
            meet(v)
            split_lo(hraw, 2, TOK)
            mlp("mlp2", 2, TOK)
            mlp_residual(0, TOK)
            meet(v)

            rms(2, 1, "norm1", 0, TOK)
            meet(v)
            for g in range(2):
                n = 4 if g == 0 else 2
                ps, free = get_a(v, "c_v", g)
                nc.vector.tensor_copy(vC[:, 4 * g:4 * g + n, :],
                                      ps[:, 0:256 * n].rearrange("p (t c) -> p t c", c=256)).then_inc(free, 1)
            meet(v)
            head_norms("c_n", "c_r", 6, 10, lambda m: qC[:, m, :] if m < 8 else kC[:, m - 8, :], rsc, rtc,
                       lambda m: cq8 if m < 8 else vec("ck", 0), C["cosC"], C["sinC"])
            meet(v)
            attention("cat")
            meet(v)
            gated("c_out", 1, LAT)
            meet(v)
            rms(3, 1, "norm2", 3, LAT, hraw)
            nc.vector.memset(accs[LAT], 0.0)
            meet(v)
            split_lo(hraw, 3, LAT)
            mlp("mlp3", 3, LAT)
            mlp_residual(1, LAT)
            meet(v)
            for t in range(LT):
                for e in range(2):
                    ps, free = get_b(v, "out", 2 * t + e)
                    nc.vector.tensor_copy(xn[:, t, 512 * e:512 * e + 512], ps).then_inc(free, 1)
            v.drain().then_inc(out_set, 1)
            meet(v)

        assert len(set(met.values())) == 1, met


LRU_HALF = 8.0 / 2
PRE_LSTM, POST_LSTM = 19, 16


def host_constants():
    import numpy as np
    c = np.zeros((P, NCONST), np.float32)

    def put(name, a):
        lo, hi = CONST[name]
        c[:a.shape[0], lo:hi] = a

    i = np.arange(P)
    put("ident", np.eye(P))
    put("ones", np.ones((P, P)))
    put("ones64", (i[:, None] // 64 == i[None] // 64) * 1.0)
    for name, w in (("rot64", 64), ("rot128", 128)):
        r = np.zeros((P, P))
        for o in range(P):
            b, e = o // w * w, o % w
            if e < w // 2:
                r[b + e + w // 2, o] = -1
            else:
                r[b + e - w // 2, o] = 1
        put(name, r)
    put("after", np.where(i[:, None] <= i[None], 0.0, NEG))
    put("before", np.where(i[:, None] >= i[None], 0.0, NEG))
    put("dist", (LAT - P + i[:, None] - np.arange(LAT)[None]) * 1.0)
    pick = np.zeros((4, 4, P))
    for h in range(4):
        pick[h, h] = 1
    put("pick", pick.reshape(4, 4 * P))
    f = np.float32

    def axial(dim):
        rows = LAT // 64
        row = np.repeat(np.arange(rows), 64).astype(f)
        col = np.tile(np.arange(64), rows).astype(f)
        n = dim // 4
        inv = f(10000.0) ** (-np.arange(n, dtype=f) / f(n))
        ang = np.concatenate([row[:, None] * inv, col[:, None] * inv], -1)
        return np.cos(ang).T, np.sin(ang).T

    for name, dim in (("B", 64), ("C", 128)):
        cs, sn = axial(dim)
        put("cos" + name, np.tile(cs, (P // (dim // 2), 1)))
        put("sin" + name, np.tile(sn, (P // (dim // 2), 1)))
    freq = f(10000.0) ** (-np.arange(0, ROPE, 2, dtype=f) / f(ROPE))
    ang = (np.arange(LAT, dtype=f)[:, None] * freq[None]).T
    cs, sn = np.cos(ang), np.sin(ang)
    put("cosM", np.tile(np.concatenate([cs, cs]), (4, 1)))
    put("sinM", np.tile(np.concatenate([-sn, sn]), (4, 1)))
    put("pair", np.tile(np.array([[1, 0, 0, 1]]), (P, 1)))
    put("eps", np.tile(np.array([[LN_EPS, RMS_EPS]]), (P, 1)))
    return c


_INS = ["x", "p", "ln1_g", "ln1_b", "ln2_g", "ln2_b", "mlp_w1", "mlp_w2", "ple_w_proj", "ple_w_gate", "hy_w_in",
        "hy_conv_w", "hy_conv_b", "hy_ga_w", "hy_ga_b", "hy_gx_w", "hy_gx_b", "hy_lambda", "hy_w_out", "mla_w_down",
        "mla_q_norm", "mla_kv_norm", "mla_w_uq", "mla_w_ukv", "mla_w_out", "c_2", "ctx_2", "c_ctx_2", "ada_w_2",
        "ada_b_2", "norm1_g_2", "norm2_g_2", "ab_w_in_2", "ab_gate_b_2", "mlstm_norm_g_2", "swa_q_norm_g_2",
        "swa_k_norm_g_2", "swa_sink_2", "ab_w_out_2", "c_w_in_2", "c_q_norm_g_2", "c_k_norm_g_2", "c_w_out_2",
        "mlp_w1_2", "mlp_w2_2"]


def kernel(**inputs):
    import numpy as _np
    import concourse.bacc as _bacc
    from concourse import mybir as _mybir
    from concourse.bass_utils import run_bass_kernel_spmd as _run

    nc = _bacc.Bacc("TRN2", target_bir_lowering=False, num_devices=1)
    arrays, args = {}, {}
    for name in _INS:
        a = _np.ascontiguousarray(inputs[name])
        arrays[f"in_{name}_dram"] = a
        args[name] = nc.dram_tensor(f"in_{name}_dram", a.shape, _mybir.dt.from_np(a.dtype), kind="ExternalInput").ap()
    c = host_constants()
    arrays["shape_constants_dram"] = c
    consts = nc.dram_tensor("shape_constants_dram", c.shape, _mybir.dt.float32, kind="ExternalInput").ap()
    out = nc.dram_tensor("out_0_dram", (1, LAT, D), _mybir.dt.float32, kind="ExternalOutput").ap()
    build(nc, args, consts, out)
    r = _run(nc, [arrays], core_ids=[0])
    return r.results[0]["out_0_dram"]
```

```python
from contextlib import ExitStack

import concourse.bass as bass
from concourse import mybir

F32 = mybir.dt.float32
F32R = mybir.dt.float32r
ALU = mybir.AluOpType
ACT = mybir.ActivationFunctionType
AX = mybir.AxisListType

P = 128
D = 1024
KD = D // P
LAT, CTX = 512, 256
TOK = LAT + CTX
LT, CT = LAT // P, CTX // P
ALPHA = (2 * 2) ** 0.25
LN_EPS, RMS_EPS = 1e-5, 1e-6
NEG = -1e30
TAKEN = -3e38

RNN = 512
RC = RNN // P
DSA_H, DSA_D, TOPK = 8, 64, 128
IDX_H, IDX_D = 4, 64
MLA_H, NOPE, ROPE, MLA_V = 16, 64, 32, 64
QL, KVL = 512, 256
A_H = 4
B_H, B_KV, B_D = 8, 2, 64
C_H, C_KV = 8, 2
N_MOD = 6
FF = 4 * D
GROUPS = 8
GF = FF // GROUPS
GH = GF // P
UNITS = 2 * GH
CW = 512
NW = 2
WORK = 30208

CONST_SIZES = [("ident", P), ("mean", P), ("mean128", P), ("mean64", P), ("rot64", P), ("rot128", P), ("after", P), ("before", P),
               ("pick", 4 * P), ("cosB", LAT), ("sinB", LAT), ("cosC", LAT), ("sinC", LAT),
               ("cosM", LAT), ("sinM", LAT), ("dist", LAT), ("pair", 4), ("eps", 2)]
CONST = {}
_at = 0
for _name, _n in CONST_SIZES:
    CONST[_name] = (_at, _at + _n)
    _at += _n
NCONST = _at

ROW_SIZES = [("ln1_g", 16), ("ln1_b", 16), ("ln2_g", 16), ("ln2_b", 16), ("conv_w", 16), ("conv_b", 4), ("ga_b", 4),
             ("gx_b", 4), ("lam", 4), ("q_norm", 4), ("kv_norm", 2), ("c", 8), ("c_ctx", 8), ("a_norm", 4),
             ("cq", 1), ("ck", 1), ("bq", 1), ("bk", 1), ("pad", 2),
             ("norm1", 16), ("norm2", 16), ("ada_b", 96)]
ROW = {}
_at = 0
for _name, _n in ROW_SIZES:
    ROW[_name] = _at
    _at += _n
NROW = _at
assert ROW["norm1"] == P and NROW == 2 * P

AB_TILES = {"q": range(0, 4), "k": range(4, 8), "v": range(8, 12), "o": range(12, 16), "qb": range(16, 20),
            "kb": range(20, 22), "vb": range(22, 23), "g": range(23, 24)}
AB_UNITS = 24
AB_W = 2 * P

PLAN_A = [("hy_xr", 4), ("hy_yr", 4), ("hy_q", 4), ("hy_ki", 4), ("hy_v", 1), ("hy_gate", 8), ("idx", 6),
          ("dsa", 4 * DSA_H), ("hy_out", 8), ("ln_v0", 1), ("ple_g0", 8), ("ple_p0", 8), ("mlp0", GROUPS * (GH + KD)),
          ("ln_m1", 1), ("ln_v1", 1),
          ("mla_cq", 4), ("mla_kv", 2), ("mla_sq", 1), ("mla_kr", 1), ("mla_skv", 1), ("uq", 12), ("ukv", 16),
          ("mla", 4 * MLA_H), ("mla_out", 8), ("ln_v2", 1), ("ple_g1", 8), ("ple_p1", 8),
          ("mlp1", GROUPS * (GH + KD)), ("ln_m3", 1), ("ln_v3", 1),
          ("rms0", 1), ("ab", AB_UNITS), ("ab_n", 12), ("carry", 1), ("mix", 2 * 6 * B_H),
          ("ab_out", 8), ("mlp2", GROUPS * (GH + KD)),
          ("rms2", 1), ("c_k", 2), ("c_v", 2), ("c_q", 8), ("c_n", 20), ("cat", LT * C_H), ("c_out", 8),
          ("mlp3", GROUPS * (GH + KD))]
PLAN_B = [("load", 17), ("dsa", 4 * DSA_H), ("dsa_o", 4), ("mla", 4 * MLA_H), ("mla_o", 8), ("ka", 6), ("va", 6), ("vb", 2), ("cols", 1),
          ("sw", 8 * B_H), ("sw_o", 8), ("hs", 8),
          ("cat", 2 * LT * C_H), ("cat_o", 8), ("out", 8)]


PLAN_W = [("hy_xr", 4), ("hy_yr", 4), ("hy_q", 4), ("hy_ki", 4), ("hy_out", 8), ("ple_g0", 8), ("mlp0", GROUPS * UNITS),
          ("mla_out", 8), ("ple_g1", 8), ("mlp1", GROUPS * UNITS), ("ab", AB_UNITS), ("ab_out", 8), ("mlp2", GROUPS * UNITS),
          ("c_k", 2), ("c_q", 8), ("c_out", 8), ("mlp3", GROUPS * UNITS)]
PLAN_X = [(n, KD) for n in ("hy", "hy_out", "mlp0", "mla_out", "mlp1", "ab", "ab_out", "mlp2", "cin", "c_out", "mlp3")]


def bases(plan):
    at, base = 0, {}
    for name, n in plan:
        base[name] = at
        at += n
    return base


BASE_A, BASE_B, BASE_W, BASE_X = bases(PLAN_A), bases(PLAN_B), bases(PLAN_W), bases(PLAN_X)


def build(nc, d, consts, out):
    with ExitStack() as ctx:
        def sb(name, shape):
            return ctx.enter_context(nc.sbuf_tensor(name, shape, F32))

        def sem(name):
            return ctx.enter_context(nc.semaphore(name))

        const = sb("const", [P, NCONST])
        vecT = sb("vecT", [P, NROW])
        small = sb("small", [P, 660])
        xT = sb("xT", [P, KD, TOK])
        pT = sb("pT", [P, 2, 2, LAT])
        mod = sb("mod", [P, 2, N_MOD * KD, 2])
        WBUF_AT = -(-nc.sbuf_base // 32) * 32
        wbuf = sb("wbuf", [P, NW, 8, CW])
        WORK_AT = -(-nc.sbuf_base // 32) * 32
        work = sb("work", [P, WORK])
        psA = ctx.enter_context(nc.psum_tensor("psA", [P, 2, 1024], F32))
        psB = ctx.enter_context(nc.psum_tensor("psB", [P, 2, 512], F32))
        psO = ctx.enter_context(nc.psum_tensor("psO", [P, 1024], F32))

        C = {name: const[:, a:b] for name, (a, b) in CONST.items()}
        ident = C["ident"]
        eps_ln, eps_rms = C["eps"][:, 0:1], C["eps"][:, 1:2]

        def vec(name, j):
            return vecT[:, ROW[name] + j:ROW[name] + j + 1]

        cursor = [0]

        def area(*shape, at=None):
            if at is not None:
                cursor[0] = at
            n = 1
            for s in shape:
                n *= s
            v = work[:, cursor[0]:cursor[0] + n]
            cursor[0] += n
            assert cursor[0] <= WORK, cursor[0]
            if len(shape) == 2:
                return v.rearrange("p (a b) -> p a b", b=shape[1])
            if len(shape) == 3:
                return v.rearrange("p (a b c) -> p a b c", b=shape[1], c=shape[2])
            if len(shape) == 4:
                return v.rearrange("p (a b c e) -> p a b c e", b=shape[1], c=shape[2], e=shape[3])
            return v

        def split(name, shape, at):
            return nc.alloc_sbuf_tensor_at(name, shape, F32R, offset=WORK_AT + 4 * at)

        xn = area(LT, D, at=0)
        cn, pn, rows = area(CT, D, at=20764), area(2, LT, 256), area(2, P)
        hT = area(KD, TOK, at=0)
        accs = {n: area(KD, n, at=0) for n in (LAT, TOK)}
        squares = {LAT: area(KD, LAT, at=2 * KD * LAT), TOK: area(KD, TOK, at=2 * KD * TOK)}
        gates = area(KD, LAT, at=3 * KD * LAT)
        hraw = area(KD, TOK, at=3 * KD * TOK)
        rstd = area(TOK, at=4 * KD * TOK)
        acc = accs[LAT]
        SPLIT_W = 4 * KD * TOK + 2 * TOK
        hid_at = {n: 3 * KD * n for n in (LAT, TOK)}
        sH, sL = ({n: split(f"{h}{n}", [P, KD, n], (1 + e) * KD * n) for n in (LAT, TOK)}
                  for e, h in enumerate(("act_hi", "act_lo")))
        gH, gL = ({n: split(f"{h}{n}", [P, GH, n], hid_at[n] + e * GH * n) for n in (LAT, TOK)}
                  for e, h in enumerate(("hid_hi", "hid_lo")))
        hid = {n: area(2, n, at=hid_at[n] + 2 * GH * n) for n in (LAT, TOK)}
        wH, wL = (split(h, [P, 2, KD * P], SPLIT_W + e * 2 * KD * P) for e, h in enumerate(("w_hi", "w_lo")))
        MC = N_MOD * D // GROUPS
        adaw, adas = area(2, KD // 2, MC, at=3 * KD * TOK), area(2, MC)
        adarow = area(MC, at=hid_at[LAT] + 2 * GH * LAT + 2 * LAT)
        xpad = area(RC, LAT + 3, at=0)
        xc, yg, qT = area(RC, LAT), area(RC, LAT), area(RC, LAT)
        kT, iqT, ikT, vN, iw = area(LAT), area(2, LAT), area(LAT), area(LT, DSA_D), area(LT, IDX_H)
        gr, gi, t2, mixT0 = area(RC, LAT), area(RC, LAT), area(RC, LAT), area(KD, LAT)
        isc, relu, pens = area(LT, LAT), area(2, 2, LAT), area(4, LAT)
        prob0, turn0, biasb = area(2, LAT), area(2, LAT), area(2, LAT)
        xH, xL = split("x_hi", [P, KD, LAT], 10528), split("x_lo", [P, KD, LAT], 10528 + KD * LAT)
        gw = area(2, RC, P, at=10528 + 2 * KD * LAT)
        on0 = relu.rearrange("p a b c -> p (a b) c")
        lru = area(RC, LAT, at=0)
        qf, kf, vM = area(MLA_H, LAT, at=0), area(MLA_H, LAT), area(LT, MLA_H * MLA_V)
        cqT, ckvT, sq1, rs1 = area(4, LAT), area(2, LAT), area(4, LAT), area(2, LAT)
        rt, krt = area(2, LAT), area(2, LAT)
        on1 = area(LT, D, at=2 * MLA_H * LAT + LT * D)
        prob1, turn1 = area(2, LAT), area(2, LAT)
        mixT1 = area(KD, LAT, at=0)
        mixT2 = area(KD, TOK, at=0)
        qkb = area(6, TOK)
        vb = area(6, P)
        stage2 = cursor[0]
        qaT, kaT, kaN = area(A_H, TOK), area(A_H, TOK), area(6, A_H * P)
        abL, abH = split("ab_lo", [P, KD, TOK], 0), split("ab_hi", [P, KD, TOK], stage2 + 2 * A_H * TOK)
        ab_raw = area(KD, TOK, at=KD * TOK)
        vaN, oaT = area(6, A_H, P + 1, at=stage2 + 3 * A_H * TOK), area(A_H, TOK)
        abwH, abwL = (nc.alloc_sbuf_tensor_at(n, [P, 2, KD * P], F32R, offset=WBUF_AT + 4 * (KD * CW * e + KD * AB_W))
                      for e, n in enumerate(("ab_w_hi", "ab_w_lo")))
        late = cursor[0]
        gI, gF = area(2, TOK), area(2, TOK)
        hs = area(6, A_H, P, at=late)
        R0, R1, R2, R3 = area(2, TOK, at=0), area(2, TOK), area(2, TOK), area(2, TOK)
        sqb, rsb, rtb = area(4, TOK, at=0), area(2, TOK), area(2, LAT)
        Cn = area(2, A_H, P + 1, at=0)
        lw = area(2, 4, P + 1)
        peak = const[:, CONST["cosM"][0]:CONST["dist"][1]].rearrange("p (a b) -> p a b", a=2)
        vaT = [peak[:, h, :] for h in range(2)] + [pT.rearrange("p a b c -> p (a b c)")[:, TOK * h:TOK * h + TOK] for h in range(2)]
        vbT = [pT.rearrange("p a b c -> p (a b c)")[:, 2 * TOK:2 * TOK + LAT], sb("vb_ctx", [P, CTX])[:, :]]
        row_out = [R3, R0, gF, R1]
        on2c = area(CT, 512, at=2 * (2 * A_H * (P + 1)))
        prob2, turn2 = area(2, 640), area(2, 640)
        assert cursor[0] <= KD * TOK
        on2 = pT.rearrange("p a b c -> p (a b) c")
        mixT3 = area(KD, LAT, at=0)
        qC, vC, kC = area(KD, LAT, at=3 * KD * TOK), area(6, 256, at=4 * KD * TOK), area(C_KV, TOK, at=0)
        sqc, rsc, rtc = area(4, TOK), area(2, TOK), area(2, LAT)
        prob3, turn3 = area(2, TOK), area(2, TOK)
        on3 = area(LT, D, at=3 * KD * LAT)

        ident_in, const_in, rows_in, x_in, c_in, p_in, bias_in = (
            sem(n) for n in ("ident_in", "const_in", "rows_in", "x_in", "c_in", "p_in", "bias_in"))
        gates_in = sem("gates_in")
        ada_landed = [sem(f"ada_landed{i}") for i in range(2)]
        a_ready, a_free = [sem(f"a_ready{i}") for i in range(2)], [sem(f"a_free{i}") for i in range(2)]
        b_ready, b_free = [sem(f"b_ready{i}") for i in range(2)], [sem(f"b_free{i}") for i in range(2)]
        w_landed = [sem(f"w_landed{i}") for i in range(NW)]
        o_ready, o_free = sem("o_ready"), sem("o_free")
        stage_over = sem("stage_over")
        out_set, out_stored = sem("out_set"), sem("out_stored")
        S = {n: sem(n) for n in (
            "centered", "squared", "sum_ready", "sum_read", "mean_read", "norm_set", "acc_zero", "relu_used", "act_hi", "act_split", "w_hi", "w_split", "g_hi", "hidden_set",
            "ada_used", "ada_sum", "row_ready", "row_set", "row_turned", "conv_set", "sqrt_set", "lam_exp", "lam_set",
            "bias_set", "dsa_max", "mla_max", "sw_max", "cat_max", "rope_raw", "root_set", "head_sq",
            "onat_set", "kr_set", "rot_set", "rot_used", "log_set", "pens_set", "row_arg", "exp_arg", "lstm_d",
            "lstm_ready", "lstm_free", "score_set", "kw_set", "state_set", "hs_sq", "residual_set",
            "shifted", "latent_set", "hs_set", "hs_normed")}

        def A(stage, j):
            n = BASE_A[stage] + j
            return n % 2, n // 2

        def B(stage, j):
            n = BASE_B[stage] + j
            return n % 2, n // 2

        def get_a(eng, stage, j, more=0):
            s, c = A(stage, j)
            eng.wait_ge(a_ready[s], more + (c + 1))
            return psA[:, s, :], a_free[s]

        def get_b(eng, stage, j):
            s, c = B(stage, j)
            eng.wait_ge(b_ready[s], c + 1)
            return psB[:, s, :], b_free[s]

        def emptied(eng, stage, j):
            s, c = A(stage, j)
            eng.wait_ge(a_free[s], c + 1)

        def turned(eng, stage, j):
            s, c = B(stage, j)
            eng.wait_ge(b_free[s], c + 1)

        def norm_product(n, m):
            return 2 * max(2 * (m // 2) - 1, 0) + m % 2

        def rope_product(n, m):
            return 2 * min(2 * (m // 2) + 2, n - 1) + m % 2

        met = {}

        def meet(eng):
            met[eng.engine] = met.get(eng.engine, 0) + 1
            eng.drain().then_inc(stage_over, 1)
            eng.wait_ge(stage_over, 4 * met[eng.engine])

        def tile_cols(w, a, b, kt=KD):
            return w[:, a:b].rearrange("(k p) c -> p k c", p=P), kt, b - a

        chunks = []

        def chunk(stage, last, *copies):
            slot, pairs = wbuf[:, len(chunks) % NW], []
            for col, src, kt, cols, *pitch in copies:
                if isinstance(cols, int):
                    pairs.append((slot[:, 0:kt, col:col + cols], src))
                else:
                    pitch = pitch[0] if pitch else cols[1]
                    for k in range(kt):
                        dst = slot[:, k, :].rearrange("p (h c) -> p h c", c=pitch)
                        h0, c0 = col // pitch, col % pitch
                        pairs.append((dst[:, h0:h0 + cols[0], c0:c0 + cols[1]], src[:, k]))
            chunks.append((stage, last, pairs))

        def mlp_chunks(name):
            for n in range(2 * GROUPS):
                chunks.append((name, ("split", name, GH * n + GH - 1), None))

        w = d["hy_w_in"][0]
        chunk("hy", ("split", "hy_xr", 3), (0, *tile_cols(w, 0, 512)))
        chunk("hy", ("split", "hy_yr", 3), (0, *tile_cols(w, 512, 1024)))
        chunk("hy", ("split", "hy_q", 3), (0, *tile_cols(w, 1024, 1536)))
        chunk("hy", ("split", "hy_ki", 3), (0, *tile_cols(w, 1536, 1600)), (64, *tile_cols(w, 1536, 1600)),
              (128, *tile_cols(w, 1664, 1920)), (384, *tile_cols(w, 1920, 1984)), (448, *tile_cols(w, 1920, 1984)))
        chunk("hy", ("hy_v", 0), (0, *tile_cols(w, 1600, 1664)), (64, *tile_cols(w, 1984, 1988)))

        def out_chunks(stage, w):
            for c in range(2):
                chunk(stage, ("split", stage, 4 * c + 3), (0, *tile_cols(w, c * 512, c * 512 + 512)))

        def ple_chunks(l):
            for c in range(2):
                chunk(f"ple{l}", ("split", f"ple_g{l}", 4 * c + 3), (0, *tile_cols(d["ple_w_gate"][l], c * 512, c * 512 + 512)))
            for c in range(2):
                chunk(f"ple{l}", (f"ple_p{l}", 4 * c + 3),
                      (0, *tile_cols(d["ple_w_proj"][l], c * 512, c * 512 + 512, 2)))

        out_chunks("hy_out", d["hy_w_out"][0])
        ple_chunks(0)
        mlp_chunks("mlp0")
        w = d["mla_w_down"][0]
        chunk("mla", ("mla_cq", 3), (0, *tile_cols(w, 0, 512)))
        chunk("mla", ("mla_kr", 0), (0, *tile_cols(w, 512, 800)), (288, *tile_cols(w, 784, 800)),
              (304, *tile_cols(w, 768, 784)))
        w = d["mla_w_uq"][0]
        def head_cols(w, kt, h0, width, a, b):
            v = w.rearrange("(k p) (h c) -> p k h c", p=P, c=width)[:, :, h0:h0 + 4, a:b]
            return v, kt, (4, b - a)

        for c in range(4):
            chunk("uq", ("uq", 3 * c + 2), (0, *head_cols(w, 4, 4 * c, 96, 0, 64)),
                  (256, *head_cols(w, 4, 4 * c, 96, 64, 96)), (384, *head_cols(w, 4, 4 * c, 96, 80, 96), 32),
                  (400, *head_cols(w, 4, 4 * c, 96, 64, 80), 32))
        w = d["mla_w_ukv"][0]
        for c in range(4):
            chunk("ukv", ("ukv", 4 * c + 3), (0, *head_cols(w, 2, 4 * c, 128, 0, 64)),
                  (256, *head_cols(w, 2, 4 * c, 128, 64, 128)))
        out_chunks("mla_out", d["mla_w_out"][0])
        ple_chunks(1)
        mlp_chunks("mlp1")
        w = d["ab_w_in_2"][0]
        cols = [(c * AB_W, c * AB_W + AB_W) for c in range(8)] + [(2064, 2320), (2320, 2576)]
        for c in range(AB_UNITS // 2):
            slot = wbuf[:, len(chunks) % NW].rearrange("p a b -> p (a b)")[:, 0:KD * AB_W]
            slot = slot.rearrange("p (k c) -> p k c", c=AB_W)
            if c < 10:
                copies = [(0, *cols[c])]
            elif c == 10:
                copies = [(0, 2576, 2640), (64, 2576, 2640), (128, 2640, 2704), (192, 2640, 2704)]
            else:
                copies = [(0, 2704, 2832), (P, 2048, 2064)]
            last = ("split", "ab", 2 * c + 1) if c < 10 else ("ab", AB_UNITS - 1)
            chunks.append(("ab", last, [(slot[:, :, at:at + b - a], tile_cols(w, a, b)[0]) for at, a, b in copies]))
        out_chunks("ab_out", d["ab_w_out_2"][0])
        mlp_chunks("mlp2")
        w = d["c_w_in_2"][0]
        chunk("cin", ("c_v", 1), (0, *tile_cols(w, 1024, 1536)))
        chunk("cin", ("split", "c_q", 3), (0, *tile_cols(w, 0, 512)))
        chunk("cin", ("split", "c_q", 7), (0, *tile_cols(w, 512, 1024)))
        out_chunks("c_out", d["c_w_out_2"][0])
        mlp_chunks("mlp3")

        first_chunk, landed = {}, []
        count = [0] * NW
        for n, (stage, _, copies) in enumerate(chunks):
            first_chunk.setdefault(stage, n)
            count[n % NW] += 16 * (1 if copies is None else len(copies))
            landed.append(count[n % NW])
        MLP = {"mlp0": (d["mlp_w1"][0], d["mlp_w2"][0]), "mlp1": (d["mlp_w1"][1], d["mlp_w2"][1]),
               "mlp2": (d["mlp_w1_2"][0], d["mlp_w2_2"][0]), "mlp3": (d["mlp_w1_2"][1], d["mlp_w2_2"][1])}

        def weights(eng, stage, j, more=0):
            n = first_chunk[stage] + j
            eng.wait_ge(w_landed[n % NW], more + landed[n])
            return wbuf[:, n % NW]

        SPLIT_CHUNK = {"hy_xr": ("hy", 0), "hy_yr": ("hy", 1), "hy_q": ("hy", 2), "hy_ki": ("hy", 3),
                       "ple_g0": ("ple0", 0), "ple_g1": ("ple1", 0), "c_k": ("cin", 0), "c_q": ("cin", 1)}
        unit_use = []
        for name, n in PLAN_W:
            for u in range(n):
                if name[:3] == "mlp":
                    g, r = u // UNITS, u % UNITS
                    unit_use.append((name, g * (GH + KD) + (r if r < GH else GH + 2 * (r - GH) + 1)))
                else:
                    unit_use.append((name, u))

        def unit(eng, stage, u, g=0):
            if stage[:3] == "mlp":
                w = weights(eng, stage, u // GH, 16 * g)
                if u < GH:
                    return w[:, :, u * P:u * P + P]
                w, a = w.rearrange("p a b -> p (a b)").rearrange("p (k c) -> p k c", c=D), (u - GH) * 256
                return w[:, :, a:a + 256]
            if stage == "ab":
                w = weights(eng, "ab", u // 2).rearrange("p a b -> p (a b)")[:, 0:KD * AB_W]
                w = w.rearrange("p (k c) -> p k c", c=AB_W)
                if u in AB_TILES["g"]:
                    return w[:, :, P:P + 4 * A_H].rearrange("p k (g h) -> p k g h", h=A_H)
                return w[:, :, u % 2 * P:u % 2 * P + P]
            cs, c0 = SPLIT_CHUNK.get(stage, (stage, 0))
            return weights(eng, cs, c0 + u // 4)[:, :, u % 4 * P:u % 4 * P + P]

        def split_place(w, stage, u):
            if stage == "ab":
                w = abwH if w is wH else abwL
            kt = GH if stage[:3] == "mlp" and u >= GH else KD
            return w[:, (BASE_W[stage] + u) % 2].rearrange("p (k c) -> p k c", k=kt)

        def split_target(w, stage, u):
            w = split_place(w, stage, u)
            if stage == "ab" and u in AB_TILES["g"]:
                return w.rearrange("p k (g c) -> p k g c", c=32)[:, :, :, 0:A_H]
            return w

        RESIDUAL = {"mlp2": 0, "mlp3": 1}
        ADA = {"mlp0": 0, "mlp1": 1}

        def dsa_logits(qt, h):
            r = slice(64 * (h % 2), 64 * (h % 2) + 64)
            n = (qt + 1) * P
            return [(0, n, [(qT[r, h // 2, qt * P:qt * P + P], kT[r, 0:n]), (ident, biasb[:, h % 2, 0:n])])]

        def mla_logits(qt, h):
            r = slice(0, NOPE + ROPE)
            return [(0, (qt + 1) * P, [(qf[r, h, qt * P:qt * P + P], kf[r, h, 0:(qt + 1) * P])])]

        def window(qt):
            return list(range(max(qt - 1, 0), min(qt + 2, LT)))

        def swa_logits(qt, h, lat=True):
            r = slice(64 * (h % 2), 64 * (h % 2) + 64)
            kv = 4 + h // (B_H // B_KV)
            q = qkb[r, h // 2, (0 if lat else LAT) + qt * P:(0 if lat else LAT) + qt * P + P]
            parts = [(0, CTX, [(q, qkb[r, kv, LAT:TOK])])]
            if lat:
                for i, b in enumerate(window(qt)):
                    parts.append((CTX + i * P, CTX + i * P + P, [(q, qkb[r, kv, b * P:b * P + P])]))
            return parts

        def swa_masks(qt, h):
            m = []
            for i, b in enumerate(window(qt)):
                if b != qt:
                    m.append((CTX + i * P, CTX + i * P + P, C["after"] if b < qt else C["before"]))
            return m

        def cat_logits(qt, h):
            q, kv = qC[:, h, qt * P:qt * P + P], h // (C_H // C_KV)
            return [(0, LAT, [(q, kC[:, kv, 0:LAT])]), (LAT, TOK, [(q, kC[:, kv, LAT:TOK])])]

        def swa_v(qt, kb, h):
            t = LT + kb if kb < CT else window(qt)[kb - CT]
            kv = h // (B_H // B_KV)
            return vb[:, t, kv * B_D:kv * B_D + B_D]

        diag = C["before"]
        ATT = {
            "dsa": dict(H=DSA_H, QT=LT, dv=DSA_D, nkb=lambda qt: qt + 1, logits=dsa_logits,
                        masks=lambda qt, h: [],
                        v=lambda qt, kb, h: vN[:, kb, :], prob=prob0, turn=turn0, onat=lambda qt: on0.rearrange("p a b -> p (a b)")[:, qt * 512:qt * 512 + 512], sink=False),
            "mla": dict(H=MLA_H, QT=LT, dv=MLA_V, nkb=lambda qt: qt + 1, logits=mla_logits,
                        masks=lambda qt, h: [(qt * P, qt * P + P, diag)],
                        v=lambda qt, kb, h: vM[:, kb, h * MLA_V:h * MLA_V + MLA_V], prob=prob1, turn=turn1, onat=lambda qt: on1[:, qt, :],
                        sink=False),
            "sw": dict(H=B_H, QT=6, dv=B_D, nkb=lambda qt: CT + len(window(qt)) if qt < LT else CT,
                       logits=lambda qt, h: swa_logits(qt, h) if qt < LT else swa_logits(qt - LT, h, False),
                       masks=lambda qt, h: swa_masks(qt, h) if qt < LT else [], v=swa_v, prob=prob2, turn=turn2,
                       onat=lambda qt: on2[:, qt, :] if qt < LT else on2c[:, qt - LT, :], sink=True),
            "cat": dict(H=C_H, QT=LT, dv=P, nkb=lambda qt: 6, logits=cat_logits, masks=lambda qt, h: [],
                        v=lambda qt, kb, h: vC[:, kb, (h // 4) * P:(h // 4) * P + P], prob=prob3,
                        turn=turn3, onat=lambda qt: on3[:, qt, :], sink=False),
        }
        n_o = {"dsa": 0, "mla": 4, "sw": 8, "cat": 14}
        nmax, rsum, rinv, sink, sarg = small[:, 0:64], small[:, 64:128], small[:, 128:192], small[:, 192:200], small[:, 200:248]
        sp4, lz, ls, ls2, lacc = (small[:, 232 + 4 * i:236 + 4 * i] for i in range(5))
        m8 = small[:, 252:260]
        sp8 = small[:, 640:644]
        silu = small[:, 260:276]
        aff = small[:, 276:308].rearrange("p (a b) -> p a b", b=2)
        gcol = small[:, 308:500].rearrange("p (a b c) -> p a b c", b=12, c=4)
        carry = small[:, 500:548].rearrange("p (a b) -> p a b", b=12)
        hss, hrs = small[:, 548:572], small[:, 572:596]
        bI, bF = small[0:4, 596:598], small[0:4, 598:600]
        mrow = small[0:4, 600:614].rearrange("p (a b) -> p a b", b=7)
        crow = small[0:4, 614:626].rearrange("p (a b) -> p a b", b=6)
        den = small[:, 626:628]
        nsink = small[:, 630:638]
        bq8, cq8 = small[:, 638:639], small[:, 639:640]
        ln_squares = [KD * i for i in range(4)]
        rms_squares = [4 * KD + KD * i for i in range(4)]

        def unit_product(name, u):
            return ("mix", 2 * u + 1) if name == "sw" else (name, u)

        def turned_groups(name, qt):
            n = ATT[name]["nkb"](qt)
            return [range(g, min(g + 4, n)) for g in range(0, n, 4)]

        def rows_of_queries(name):
            return list(range(ATT[name]["QT"]))[::-1 if name == "mla" else 1]

        def units(name):
            s, at, r = ATT[name], 0, []
            for qt in rows_of_queries(name):
                for h in range(s["H"]):
                    r.append((len(r), qt, h, at))
                    at += len(turned_groups(name, qt))
            return r

        def rows_of(ap):
            return ap.rearrange("(c p) -> c p", p=P)

        ROW_SRC = [("ln1_g", 0, rows_of(d["ln1_g"][0])), ("ln1_g", 8, rows_of(d["ln1_g"][1])),
                   ("ln1_b", 0, rows_of(d["ln1_b"][0])), ("ln1_b", 8, rows_of(d["ln1_b"][1])),
                   ("ln2_g", 0, rows_of(d["ln2_g"][0])), ("ln2_g", 8, rows_of(d["ln2_g"][1])),
                   ("ln2_b", 0, rows_of(d["ln2_b"][0])), ("ln2_b", 8, rows_of(d["ln2_b"][1])),
                   ("conv_w", 0, d["hy_conv_w"][0].rearrange("w (c p) -> (w c) p", p=P)),
                   ("conv_b", 0, rows_of(d["hy_conv_b"][0])), ("ga_b", 0, rows_of(d["hy_ga_b"][0])),
                   ("gx_b", 0, rows_of(d["hy_gx_b"][0])), ("lam", 0, rows_of(d["hy_lambda"][0])),
                   ("q_norm", 0, rows_of(d["mla_q_norm"][0])), ("kv_norm", 0, rows_of(d["mla_kv_norm"][0])),
                   ("c", 0, rows_of(d["c_2"][0])), ("c_ctx", 0, rows_of(d["c_ctx_2"])),
                   ("a_norm", 0, rows_of(d["mlstm_norm_g_2"][0])),
                   ("cq", 0, d["c_q_norm_g_2"]), ("ck", 0, d["c_k_norm_g_2"]), ("pad", 0, rows_of(d["c_ctx_2"])[0:2]),
                   ("norm1", 0, rows_of(d["norm1_g_2"][0])), ("norm1", 8, rows_of(d["norm1_g_2"][1])),
                   ("norm2", 0, rows_of(d["norm2_g_2"][0])), ("norm2", 8, rows_of(d["norm2_g_2"][1])),
                   ("ada_b", 0, rows_of(d["ada_b_2"][0])), ("ada_b", 48, rows_of(d["ada_b_2"][1]))]
        ROWS_IN = 16 * (len(ROW_SRC) + 4)
        GATES_IN = 16 * 4
        BIAS_IN = 16 * 5

        LSTM_ORDER = [[4, 5, 0, 1, 2, 3], [5, 4, 3, 2, 1, 0]]
        lstm_units = [(j, dr, h) for j in range(6) for dr in range(2) for h in range(A_H)]
        lstm_last = {(LSTM_ORDER[dr][j], h): u for u, (j, dr, h) in enumerate(lstm_units)}

        block = ctx.enter_context(nc.Block())

        @block.sync
        def _(sp):
            def used(n, more=0):
                if n >= NW:
                    if chunks[n - NW][1][0] == "split":
                        _, stage, u = chunks[n - NW][1]
                        sp.wait_ge(S["w_split"], more + (BASE_W[stage] + u + 1))
                    else:
                        s, c = A(*chunks[n - NW][1])
                        sp.wait_ge(a_ready[s], c + 1)

            def small_loads():
                for name, at, src in ROW_SRC:
                    r = ROW[name] + at
                    n = src.shape[0]
                    sp.dma_start(rows[r % P:r % P + n, r // P, :], src).then_inc(rows_in, 16)
                for name, src in (("bq", d["swa_q_norm_g_2"]), ("bk", d["swa_k_norm_g_2"])):
                    for e in range(2):
                        sp.dma_start(rows[ROW[name]:ROW[name] + 1, 0, 64 * e:64 * e + 64], src).then_inc(rows_in, 16)
                gb = d["ab_gate_b_2"].rearrange("a (g h) -> g h a", h=A_H)
                for dst, g in ((bI[:, 0:1], 0), (bI[:, 1:2], 2), (bF[:, 0:1], 1), (bF[:, 1:2], 3)):
                    sp.dma_start(dst, gb[g]).then_inc(bias_in, 16)
                sp.dma_start(sink, d["swa_sink_2"][0:1, :].to_broadcast([P, B_H])).then_inc(bias_in, 16)

            sp.dma_start(xn, d["x"][0].rearrange("(a p) d -> p a d", p=P)).then_inc(x_in, 16)
            n = 0
            while n < len(chunks):
                stage, last, copies = chunks[n]
                if n == NW:
                    small_loads()
                if copies is not None:
                    used(n)
                    for dst, src in copies:
                        sp.dma_start(dst, src).then_inc(w_landed[n % NW], 16)
                    n += 1
                    continue
                w1, w2 = MLP[stage]
                w1 = w1.rearrange("(k p) f -> p k f", p=P)

                def group(i, n0, more, first):
                    part = bass.ds(i * GF, GF)
                    used(n0, more)
                    sp.dma_start(wbuf[:, n0 % NW], w1[:, :, part]).then_inc(w_landed[n0 % NW], 16)
                    used(n0 + 1, more)
                    sp.dma_start(wbuf[:, (n0 + 1) % NW].rearrange("p a b -> p (a b)").rearrange("p (k c) -> p k c", c=D),
                                 w2[part, :].rearrange("(k p) c -> p k c", p=P)).then_inc(w_landed[(n0 + 1) % NW], 16)
                    if stage in ADA:
                        l = ADA[stage]
                        src = d["ada_w_2"][l].rearrange("(e k p) c -> e p k c", p=P, e=2)
                        for e in range(2):
                            if not first:
                                sp.wait_ge(S["ada_used"], 2 * (i - 1) + (2 * GROUPS * l + e + 1))
                            elif e == 0:
                                sp.wait_ge(S["act_split"], BASE_X[("hy_out", "mla_out")[l]] + KD)
                            sp.dma_start(adaw[:, e], src[e][:, :, bass.ds(i * MC, MC)]).then_inc(ada_landed[e], 16)

                group(0, n, 0, True)
                with sp.Fori(1, GROUPS) as i:
                    group(i, n + 2, (i - 1) * UNITS, False)
                n += 2 * GROUPS
            for t in range(LT):
                sp.wait_ge(out_set, t + 1)
                sp.dma_start(out[0][t * P:t * P + P], xn[:, t, :]).then_inc(out_stored, 16)
            sp.wait_ge(out_stored, 16 * LT)

        @block.tensor
        def _(pe):
            def product(stage, j, parts, more=0, wait=None):
                s, c = A(stage, j)
                if c > 0:
                    pe.wait_ge(a_free[s], more + c)
                for a, b, pairs in parts:
                    m = 1
                    for e in pairs[0][0].shape[1:]:
                        m *= e
                    for i, (l, r) in enumerate(pairs):
                        if wait is not None:
                            wait(i)
                        ins = pe.matmul(psA[0:m, s, a:b], l, r, start=(i == 0), stop=(i == len(pairs) - 1))
                ins.then_inc(a_ready[s], 1)

            def turn(stage, j, parts):
                s, c = B(stage, j)
                if c > 0:
                    pe.wait_ge(b_free[s], c)
                for col, src in parts:
                    k, m = src.shape[0], src.shape[1]
                    ins = pe.transpose(psB[0:m, s, col:col + k], src, ident[0:k, 0:k])
                ins.then_inc(b_ready[s], 1)

            def features(w, col, rhs, n, kt=KD, m=P):
                return [(a, b, [(w[:, k, col:col + m], rhs[:, k, a:b]) for k in range(kt)])
                        for a, b in ((0, min(n, 512)), (512, n)) if b > a]

            def tokens(w, a, b, lhs, t, at, kt=KD):
                return (at, at + b - a, [(lhs[:, k, t * P:t * P + P], w[:, k, a:b]) for k in range(kt)])

            def linear(stage, chunk_stage, c0, rhs, n, nchunks=2, kt=KD):
                for c in range(nchunks):
                    w = weights(pe, chunk_stage, c0 + c)
                    for m in range(4):
                        product(stage, 4 * c + m, features(w, m * P, rhs, n, kt))

            def split_products(stage, js, n, operands, more=0, halves=None, wait=None):
                for j in js:
                    s, c = A(stage, j)
                    if c > 0:
                        pe.wait_ge(a_free[s], more + c)
                halves = halves or [range(KD)]
                for ks in halves:
                    for j in js:
                        s, _ = A(stage, j)
                        for a, b in ((0, min(n, 512)), (512, n)):
                            if b <= a:
                                continue
                            for k in ks:
                                if wait is not None and j == js[0] and a == 0:
                                    wait(k)
                                w_hi, w_lo, x_hi, x_lo = operands(j, k)
                                first, last = k == halves[0][0], k == halves[-1][-1]
                                pe.matmul(psA[:, s, a:b], w_hi, x_hi[:, a:b], start=first, stop=False)
                                pe.matmul(psA[:, s, a:b], w_hi, x_lo[:, a:b], start=False, stop=False)
                                ins = pe.matmul(psA[:, s, a:b], w_lo, x_hi[:, a:b], start=False, stop=last)
                        if ks is halves[-1]:
                            ins.then_inc(a_ready[s], 1)

            def split_here(name):
                return lambda k: pe.wait_ge(S["act_split"], BASE_X[name] + k + 1)

            def split_linear(stage, x_hi, x_lo, n, wait=None, units=KD, behind=None):
                for u in range(units):
                    pe.wait_ge(S["w_split"], BASE_W[stage] + u + 1)
                    hi, lo = split_place(wH, stage, u), split_place(wL, stage, u)
                    split_products(stage, [u], n, lambda j, k: (hi[:, k, :], lo[:, k, :], x_hi[:, k, :], x_lo[:, k, :]),
                                   wait=wait if u == 0 else None)
                    if behind and u >= 2:
                        behind(u - 2)
                if behind:
                    behind(units - 2)
                    behind(units - 1)

            def mean_of(stage):
                def add(k):
                    emptied(pe, stage, k)
                    ins = pe.matmul(psO[:, 0:LAT], C["mean"], xT[:, k, 0:LAT], start=(k == 0), stop=(k == KD - 1))
                    if k == KD - 1:
                        ins.then_inc(S["sum_ready"], 1)
                return add

            def mean_square_of(i, n):
                def add(k):
                    pe.wait_ge(S["squared"], rms_squares[i] + k + 1)
                    for a, b in ((0, 512), (512, n)):
                        if b > a:
                            ins = pe.matmul(psO[:, a:b], C["mean"], hraw[:, k, a:b], start=(k == 0), stop=(k == KD - 1))
                    if k == KD - 1:
                        ins.then_inc(S["sum_ready"], 1)
                return add

            def attention(name, beside=None):
                s = ATT[name]
                us = units(name)

                def turn_probs(u, qt, h, b0):
                    emptied(pe, *unit_product(name, u))
                    for g, kbs in enumerate(turned_groups(name, qt)):
                        turn(name, b0 + g, [((kb - kbs[0]) * P, s["prob"][:, u % 2, kb * P:kb * P + P]) for kb in kbs])

                def weigh_values(u, qt, h, b0):
                    for g in range(len(turned_groups(name, qt))):
                        turned(pe, name, b0 + g)
                    n = n_o[name] + rows_of_queries(name).index(qt)
                    if h == 0 and n > 0:
                        pe.wait_ge(o_free, n)
                    nkb = s["nkb"](qt)
                    for kb in range(nkb):
                        ins = pe.matmul(psO[:, h * s["dv"]:(h + 1) * s["dv"]], s["turn"][:, u % 2, kb * P:kb * P + P],
                                        s["v"](qt, kb, h), start=(kb == 0), stop=(kb == nkb - 1))
                    if h == s["H"] - 1:
                        ins.then_inc(o_ready, 1)

                for step in range(len(us) + 2):
                    if beside:
                        beside[0](step)
                    if step < len(us):
                        u, qt, h, _ = us[step]
                        if name == "dsa":
                            pe.wait_ge(S["bias_set"], u + 1)
                        product(*unit_product(name, u), s["logits"](qt, h))
                    if 0 <= step - 1 < len(us):
                        turn_probs(*us[step - 1])
                    if beside:
                        beside[1](step - 1)
                    if step >= 2:
                        weigh_values(*us[step - 2])
                pe.wait_ge(S["onat_set"], n_o[name] + s["QT"])
                width = s["H"] * s["dv"] // P
                if name == "sw":
                    for t in range(width):
                        turn("sw_o", t, [(qt * P, s["onat"](LT + qt)[:, t * P:t * P + P]) for qt in range(CT)])
                for t in range(width):
                    turn(name + "_o", t + (width if name == "sw" else 0),
                         [(qt * P, s["onat"](qt)[:, t * P:t * P + P]) for qt in range(LT)])

            def layer_norm(i, x):
                if i % 2:
                    product(f"ln_m{i}", 0, [(0, LAT, [(C["mean"], x[:, k, 0:LAT]) for k in range(KD)])])
                sum_squares(f"ln_v{i}", ln_squares[i], LAT)

            def sum_squares(stage, base, n):
                s, c = A(stage, 0)
                pe.wait_ge(a_free[s], c)
                for k in range(KD):
                    pe.wait_ge(S["squared"], base + k + 1)
                    for a, b in ((0, 512), (512, n)):
                        if b > a:
                            ins = pe.matmul(psA[:, s, a:b], C["mean"], squares[n][:, k, a:b],
                                            start=(k == 0), stop=(k == KD - 1))
                ins.then_inc(a_ready[s], 1)

            def head_norms(stage, first, n, tile, sq, mean, rot):
                def norm(m):
                    w = tile(m).shape[-1]
                    pe.wait_ge(S["head_sq"], first + m + 1)
                    product(stage, norm_product(n, m), [(a, b, [(mean, sq[:, m % 4, a:b])])
                                                        for a, b in ((0, 512), (512, w)) if b > a])

                norm(0)
                norm(1)
                for p in range(0, n, 2):
                    for m in range(p + 2, min(p + 4, n)):
                        norm(m)
                    for m in (p, p + 1):
                        pe.wait_ge(S["rope_raw"], first + m + 1)
                        product(stage, rope_product(n, m), [(0, LAT, [(rot, tile(m)[:, 0:LAT])])])

            def rms(i, n):
                sum_squares(f"rms{i}", rms_squares[i], n)

            def mlp(name, index, n):
                with pe.Fori(0, GROUPS) as i:
                    more = i * ((GH + KD) // 2)
                    for u in range(GH):
                        pe.wait_ge(S["w_split"], i * UNITS + (BASE_W[name] + u + 1))
                        hi, lo = split_place(wH, name, u), split_place(wL, name, u)
                        split_products(name, [u], n, lambda j, k: (hi[:, k, :], lo[:, k, :], sH[n][:, k, :], sL[n][:, k, :]),
                                       more, wait=split_here(name) if u == 0 else None)
                    for q in range(GH):
                        u, j0 = GH + q, GH + 2 * q
                        pe.wait_ge(S["w_split"], i * UNITS + (BASE_W[name] + u + 1))
                        hi, lo = split_place(wH, name, u), split_place(wL, name, u)

                        def operands(j, k):
                            c = slice((j - j0) * P, (j - j0) * P + P)
                            return hi[:, k, c], lo[:, k, c], gH[n][:, k, :], gL[n][:, k, :]

                        if q == 0:
                            split_products(name, [j0, j0 + 1], n, operands, more, [range(GH - 1), range(GH - 1, GH)],
                                           lambda k: pe.wait_ge(S["hidden_set"], i * GH + (index * GH * GROUPS + k + 1)))
                            continue
                        if name in ADA and q == GH - 1:
                            mod_rows(ADA[name], i)
                        split_products(name, [j0], n, operands, more, [range(GH)])
                        if name in ADA and q == GH - 1:
                            pe.wait_ge(S["row_set"], i + (GROUPS * ADA[name] + 1))
                        split_products(name, [j0 + 1], n, operands, more, [range(GH)])
                        if name in ADA and q == GH - 1:
                            mod_turn()

            def mod_rows(l, i):
                pe.wait_ge(S["ada_sum"], i + (GROUPS * l + 1))
                for a, b in ((0, 512), (512, MC)):
                    for e in range(2):
                        ins = pe.matmul(psO[0:2, a:b], C["pair"][:, 2 * e:2 * e + 2], adas[:, e, a:b],
                                        start=(e == 0), stop=(e == 1))
                ins.then_inc(S["row_ready"], 1)

            def mod_turn():
                for m in range(MC // P):
                    ins = pe.transpose(psB[:, 0, 2 * m:2 * m + 2], adarow[0:2, m * P:m * P + P], ident[0:2, 0:2])
                ins.then_inc(S["row_turned"], 1)

            def ple(l):
                split_linear(f"ple_g{l}", sH[LAT], sL[LAT], LAT, split_here(f"mlp{l}"))
                linear(f"ple_p{l}", f"ple{l}", 2, pT[:, l], LAT, kt=2)

            pe.wait_ge(ident_in, 16)
            pe.wait_ge(x_in, 16)
            for k in range(KD):
                turn("load", k, [(t * P, xn[:, t, k * P:k * P + P]) for t in range(LT)])
            meet(pe)

            split_linear("hy_xr", xH, xL, LAT, split_here("hy"), 4)
            split_linear("hy_yr", xH, xL, LAT, None, 4)
            pe.wait_ge(rows_in, ROWS_IN)
            turn("load", 8, [(0, rows[:, 0, :]), (P, rows[:, 1, :])])
            split_linear("hy_q", xH, xL, LAT, None, 4)
            split_linear("hy_ki", xH, xL, LAT, None, 4)
            w = weights(pe, "hy", 4)
            product("hy_v", 0, [tokens(w, 0, 68, xT, t, 68 * t) for t in range(LT)])
            pe.wait_ge(c_in, 16)
            for k in range(0, KD, 2):
                turn("load", 9 + k // 2, [(2 * P * e + t * P, cn[:, t, (k + e) * P:(k + e) * P + P])
                                          for e in range(2) for t in range(CT)])
            pe.wait_ge(p_in, 32)
            for l in range(2):
                for k in range(2):
                    turn("load", 13 + 2 * l + k, [(t * P, pn[:, l, t, k * P:k * P + P]) for t in range(LT)])
            pe.wait_ge(const_in, 16)
            pe.wait_ge(gates_in, GATES_IN)
            pe.wait_ge(S["conv_set"], 1)
            for c in range(RC):
                product("hy_gate", 2 * c, [(0, LAT, [(gw[:, 0, c, :], xc[:, c, :])])])
                product("hy_gate", 2 * c + 1, [(0, LAT, [(gw[:, 1, c, :], xc[:, c, :])])])
            emptied(pe, "hy_ki", 3)
            for qt in range(1, LT):
                for hp in range(2):
                    product("idx", 2 * (qt - 1) + hp, [
                        (512 * e, 512 * e + (qt + 1) * P,
                         [(iqT[64 * e:64 * e + 64, hp, qt * P:qt * P + P], ikT[64 * e:64 * e + 64, 0:(qt + 1) * P])])
                        for e in range(2)])
            meet(pe)
            attention("dsa")
            meet(pe)
            split_linear("hy_out", sH[LAT], sL[LAT], LAT, split_here("hy_out"), behind=mean_of("hy_out"))
            layer_norm(0, xT)
            ple(0)
            meet(pe)
            mlp("mlp0", 0, LAT)
            meet(pe)
            layer_norm(1, acc)

            w = weights(pe, "mla", 0)
            for m in range(4):
                product("mla_cq", m, features(w, m * P, xT, LAT),
                        wait=(lambda k: pe.wait_ge(S["shifted"], k + 1)) if m == 0 else None)
            w = weights(pe, "mla", 1)
            for m in range(2):
                product("mla_kv", m, features(w, m * P, xT, LAT))
            emptied(pe, "mla_cq", 3)
            product("mla_sq", 0, [(0, LAT, [(C["mean"], sq1[:, k, :]) for k in range(4)])])
            product("mla_kr", 0, [(0, LAT, [(w[:, k, 256:288], xT[:, k, 0:LAT]) for k in range(KD)]),
                                  (512, 512 + LAT, [(w[:, k, 288:320], xT[:, k, 0:LAT]) for k in range(KD)])])
            emptied(pe, "mla_kv", 1)
            product("mla_skv", 0, [(0, LAT, [(C["mean"], rt[:, k, :]) for k in range(2)])])
            for c in range(4):
                w = weights(pe, "uq", c)
                for m in range(2):
                    product("uq", 3 * c + m, features(w, m * P, cqT, LAT, 4),
                            wait=(lambda k: pe.wait_ge(S["latent_set"], k + 1)) if c + m == 0 else None)
                product("uq", 3 * c + 2, [(0, LAT, [(w[:, k, 256:384], cqT[:, k, :]) for k in range(4)]),
                                          (512, 512 + LAT, [(w[:, k, 384:512], cqT[:, k, :]) for k in range(4)])])
            pe.wait_ge(S["latent_set"], 6)
            for c in range(4):
                w = weights(pe, "ukv", c)
                for m in range(2):
                    product("ukv", 4 * c + m, features(w, m * P, ckvT, LAT, 2))
                for m in range(2):
                    product("ukv", 4 * c + 2 + m, [
                        (256 * e, 256 * e + 256,
                         [(ckvT[:, k, (2 * m + e) * P:(2 * m + e) * P + P],
                           w[:, k, 256:512]) for k in range(2)])
                        for e in range(2)])
            meet(pe)
            attention("mla")
            split_linear("mla_out", sH[LAT], sL[LAT], LAT, split_here("mla_out"), behind=mean_of("mla_out"))
            layer_norm(2, xT)
            ple(1)
            meet(pe)
            mlp("mlp1", 1, LAT)
            meet(pe)
            layer_norm(3, acc)

            rms(0, TOK)
            split_linear("ab", abH, abL, TOK, split_here("ab"), AB_UNITS)
            meet(pe)
            for h in range(0, 6):
                turn("ka", h, [(P * hh, kaT[:, hh, h * P:h * P + P]) for hh in range(A_H)])
            for t in range(6):
                turn("va", t, [(P * h, vaT[h][:, t * P:t * P + P]) for h in range(A_H)])
            for e, n in enumerate((LT, CT)):
                turn("vb", e, [(P * t, vbT[e][:, t * P:t * P + P]) for t in range(n)])
            head_norms("ab_n", 0, 6, lambda m: qkb[:, m, :], sqb, C["mean64"], C["rot64"])
            meet(pe)
            meet(pe)
            turn("cols", 0, [(4 * (12 * q + 6 * dr + t), src[0:4, dr, t * P:t * P + P])
                             for q, src in enumerate(row_out) for dr in range(2) for t in range(6)])
            product("carry", 0, [(12 * h, 12 * h + 12, [(C["pick"][0:4, h * P:h * P + P],
                                                        small[0:4, 614:626])]) for h in range(A_H)])
            meet(pe)

            def lstm_in(u):
                if u >= len(lstm_units):
                    return
                j, dr, h = lstm_units[u]
                t = LSTM_ORDER[dr][j]
                cols = slice(t * P, t * P + P)
                pe.wait_ge(S["state_set"], 1 + max(u - 8 + 1, 0))
                product("mix", 2 * u, [(0, P, [(kaT[:, h, cols], qaT[:, h, cols])]),
                                       (P, 2 * P, [(C["pick"][0:4, h * P:h * P + P], peak[0:4, dr, cols])]),
                                       (512, 512 + P + 1, [(qaT[:, h, cols], Cn[:, dr, h, :])])])

            def lstm_out(u):
                if not 0 <= u < len(lstm_units):
                    return
                j, dr, h = lstm_units[u]
                t = LSTM_ORDER[dr][j]
                pe.wait_ge(S["score_set"], u + 1)
                pe.wait_ge(S["kw_set"], u + 1)
                if u >= 1:
                    pe.wait_ge(S["lstm_free"], u)
                pe.matmul(psO[:, 512:512 + P + 1], lw[:, u % 2, 1, 0:P], vaN[:, t, h, :], start=True, stop=True)
                pe.matmul(psO[:, 768:768 + P + 1], lw[:, u % 2, 2, 0:P], vaN[:, t, h, :],
                          start=True, stop=True).then_inc(S["lstm_ready"], 1)

            attention("sw", (lstm_in, lstm_out))
            for h in range(A_H):
                pe.wait_ge(S["hs_normed"], h + 1)
                turn("hs", 2 * h, [(t * P, hs[:, t, h, :]) for t in range(LT)])
                turn("hs", 2 * h + 1, [(t * P, hs[:, LT + t, h, :]) for t in range(CT)])
            split_linear("ab_out", sH[TOK], sL[TOK], TOK, split_here("ab_out"), behind=mean_square_of(1, TOK))
            mlp("mlp2", 2, TOK)

            rms(2, TOK)
            split_linear("c_k", sH[TOK], sL[TOK], TOK, split_here("cin"), 2)
            w = weights(pe, "cin", 0)
            for g in range(2):
                product("c_v", g, [tokens(w, 256, 512, hraw, t, 256 * (t - 4 * g)) for t in range(4 * g, min(4 * g + 4, 6))])
            split_linear("c_q", sH[TOK], sL[TOK], LAT)
            meet(pe)
            head_norms("c_n", 6, 10, lambda m: qC[:, m, :] if m < 8 else kC[:, m - 8, :], sqc, C["mean128"], C["rot128"])
            meet(pe)
            attention("cat")
            split_linear("c_out", sH[LAT], sL[LAT], LAT, split_here("c_out"), behind=mean_square_of(3, LAT))
            mlp("mlp3", 3, LAT)
            pe.wait_ge(S["residual_set"], 2 * KD)
            for t in range(LT):
                for e in range(2):
                    turn("out", 2 * t + e, [((k - 4 * e) * P, xT[:, k, t * P:t * P + P]) for k in range(4 * e, 4 * e + 4)])
            meet(pe)

        @block.scalar
        def _(act):
            def f(out, in_, func, **kw):
                return nc.scalar.activation(out, in_, func, **kw)

            def w_hi(stage, u, g=0):
                w = unit(act, stage, u, g)
                n = BASE_W[stage] + u
                if n >= 2:
                    s, c = A(*unit_use[n - 2])
                    act.wait_ge(a_ready[s], g * ((GH + KD) // 2) + (c + 1))
                f(split_target(wH, stage, u), w, ACT.Copy).then_inc(S["w_hi"], 1)

            act.dma_start(const[:, 0:P], consts[:, 0:P]).then_inc(ident_in, 16)
            act.dma_start(cn, d["ctx_2"][0].rearrange("(a p) d -> p a d", p=P)).then_inc(c_in, 16)
            for l in range(2):
                act.dma_start(pn[:, l], d["p"][l, 0].rearrange("(a p) d -> p a d", p=P)).then_inc(p_in, 16)
            act.dma_start(const[:, P:], consts[:, P:]).then_inc(const_in, 16)
            w_hi("hy_xr", 0)
            w_hi("hy_xr", 1)
            meet(act)

            def attention(name, dst, beside=None, out=None):
                s = ATT[name]
                us = units(name)

                def evacuate(u, qt, h, b0):
                    for g, kbs in enumerate(turned_groups(name, qt)):
                        ps, free = get_b(act, name, b0 + g)
                        f(s["turn"][:, u % 2, kbs[0] * P:(kbs[-1] + 1) * P], ps[:, 0:len(kbs) * P], ACT.Copy).then_inc(free, 1)

                for u, qt, h, b0 in us:
                    if beside:
                        beside(u)
                    c, n = qt * s["H"] + h, s["nkb"](qt) * P
                    act.wait_ge(S[name + "_max"], u + 1)
                    if s["sink"]:
                        f(sarg[:, c:c + 1], sink[:, h:h + 1], ACT.Exp, bias=nmax[:, c:c + 1])
                    slot, _ = A(*unit_product(name, u))
                    f(s["prob"][:, u % 2, 0:n], psA[:, slot, 0:n], ACT.Exp, bias=nmax[:, c:c + 1],
                      accum_out=rsum[:, c:c + 1]).then_inc(a_free[slot], 1)
                    if u >= 1:
                        evacuate(*us[u - 1])
                evacuate(*us[-1])
                width = s["H"] * s["dv"] // P
                for n in range(2 * width if name == "sw" else width):
                    ps, free = get_b(act, name + "_o", n)
                    x = dst(n)
                    f(x, ps[:, 0:x.shape[-1]], ACT.Copy).then_inc(free, 1)
                    if out:
                        act.drain()
                        f(sH[LAT][:, n, :], x, ACT.Copy).then_inc(S["act_hi"], 1)
                        if n < 2:
                            w_hi(out, n)

            def split_hi(x, x_hi, n):
                for k in range(KD):
                    f(x_hi[:, k, :], x[:, k, 0:n], ACT.Copy).then_inc(S["act_hi"], 1)

            def split_linear(stage, evacuate=None, units=KD, before=None, start=0):
                for u in range(units + 2):
                    if start <= u < units:
                        w_hi(stage, u)
                    if u == 1 and before:
                        before()
                    if u >= 2 and evacuate:
                        evacuate(u - 2)

            def shift_and_split(first, x, spans, shift, x_hi=None, n=None, behind=None):
                for k in range(KD):
                    act.wait_ge(S["norm_set"], first + k + 1)
                    for a, b, e in spans:
                        ins = f(x[:, k, a:b], x[:, k, a:b], ACT.Identity, bias=shift(k, e))
                    if x_hi is not None:
                        act.drain()
                        f(x_hi[:, k, :], x[:, k, 0:n], ACT.Copy).then_inc(S["act_hi"], 1)
                    else:
                        ins.then_inc(S["shifted"], 1)
                    if behind:
                        act.drain()
                        behind(k)

            def inverse_root(stage, j, dst, n, eps, scale=1.0):
                ps, free = get_a(act, stage, j)
                f(dst, ps[:, 0:n], ACT.Ln, scale=scale, bias=eps)
                act.drain()
                f(dst, dst, ACT.Exp, scale=-0.5).then_inc(free, 1)

            def layer_norm(i, x, bias, j0, dst, x_hi=None, ahead=(), behind=None):
                for a in ahead:
                    w_hi(*a)
                for k in range(KD):
                    act.wait_ge(S["centered"], KD * i + k + 1)
                    f(squares[LAT][:, k, :], x[:, k, 0:LAT], ACT.Square).then_inc(S["squared"], 1)
                inverse_root(f"ln_v{i}", 0, rstd[:, 0:LAT], LAT, eps_ln)
                shift_and_split(ln_squares[i], dst, [(0, LAT, 0)], lambda k, e: vec(bias, j0 + k), x_hi, LAT, behind)

            def square_of(stage, n):
                def square(m):
                    emptied(act, stage, m)
                    f(hraw[:, m, 0:n], xT[:, m, 0:n], ACT.Square).then_inc(S["squared"], 1)
                return square

            def rms(i, layer, first, n, dst, x_hi=None, ahead=()):
                if i % 2 == 0:
                    for k in range(KD if i else 0):
                        act.wait_ge(S["residual_set"], k + 1)
                        f(squares[n][:, k, :], xT[:, k, 0:n], ACT.Square).then_inc(S["squared"], 1)
                for a in ahead:
                    w_hi(*a)
                spans = [(0, LAT, 0)] + ([(LAT, n, 1)] if n > LAT else [])
                if i % 2 == 0:
                    inverse_root(f"rms{i}", 0, rstd[:, 0:n], n, eps_rms)
                else:
                    act.wait_ge(S["sum_ready"], 2 + (i + 1) // 2)
                    f(rstd[:, 0:n], psO[:, 0:n], ACT.Ln, bias=eps_rms)
                    act.drain()
                    f(rstd[:, 0:n], rstd[:, 0:n], ACT.Exp, scale=-0.5).then_inc(S["sum_read"], 1)
                shift_and_split(rms_squares[i], dst, spans, lambda k, e: mod[:, layer, first * KD + k, e:e + 1], x_hi, n)

            def ple(l):
                def gate(j):
                    ps, free = get_a(act, f"ple_g{l}", j)
                    f(gates[:, j, :], ps[:, 0:LAT], ACT.Sigmoid).then_inc(free, 1)

                split_linear(f"ple_g{l}", gate, start=2)
                w_hi(f"mlp{l}", 0)
                w_hi(f"mlp{l}", 1)

            def mlp(name, index, n):
                def part(i, last):
                    more = i * ((GH + KD) // 2)
                    for m in range(GH):
                        if m < GH - 1:
                            w_hi(name, m + 2, i)
                        g = hid[n][:, m % 2, :]
                        ps, free = get_a(act, name, m, more)
                        if m >= 2:
                            act.wait_ge(S["hidden_set"], i * GH + (index * GH * GROUPS + m - 1))
                        f(g, ps[:, 0:n], ACT.Relu).then_inc(free, 1)
                        act.drain()
                        f(g, g, ACT.Square)
                        act.drain()
                        f(gH[n][:, m, :], g, ACT.Copy).then_inc(S["g_hi"], 1)
                    w_hi(name, GH + 1, i)
                    w_hi(name, GH + 2, i)
                    w_hi(name, GH + 3, i)
                    if not last:
                        w_next(0, i)
                    if name in ADA:
                        act.wait_ge(S["row_ready"], i + (GROUPS * ADA[name] + 1))
                        f(adarow[0:2], psO[0:2, 0:MC], ACT.Copy).then_inc(S["row_set"], 1)
                    if not last:
                        w_next(1, i)

                def w_next(u, i):
                    w = unit(act, name, u, i + 1)
                    s, c = A(name, GH + 2 * (GH - 2 + u) + 1)
                    act.wait_ge(a_ready[s], i * ((GH + KD) // 2) + (c + 1))
                    f(split_place(wH, name, u), w, ACT.Copy).then_inc(S["w_hi"], 1)

                with act.Fori(0, GROUPS - 1) as i:
                    part(i, False)
                part(GROUPS - 1, True)

            hy_units = [(name, m) for name in ("hy_xr", "hy_yr", "hy_q", "hy_ki") for m in range(4)]
            for n in range(len(hy_units) + 2):
                if 2 <= n < len(hy_units):
                    w_hi(*hy_units[n])
                if n == 1:
                    split_hi(xT, xH, LAT)
                if n == 11:
                    turned(act, "load", 8)
                    f(lz, vecT[:, ROW["lam"]:ROW["lam"] + 4], ACT.Abs)
                    act.drain()
                    f(lz, lz, ACT.Exp, scale=-1.0).then_inc(S["lam_exp"], 1)
                if n < 2 or hy_units[n - 2][0] == "hy_ki":
                    continue
                name, m = hy_units[n - 2]
                ps, free = get_a(act, name, m)
                if name == "hy_xr":
                    f(xpad[:, m, 3:3 + LAT], ps[:, 0:LAT], ACT.Copy).then_inc(free, 1)
                elif name == "hy_yr":
                    f(yg[:, m, :], ps[:, 0:LAT], ACT.Gelu_apprx_tanh).then_inc(free, 1)
                else:
                    f(qT[:, m, :], ps[:, 0:LAT], ACT.Copy, scale=DSA_D ** -0.5).then_inc(free, 1)
            for v, name in enumerate(("c", "c_ctx")):
                f(silu.rearrange("p (k v) -> p k v", v=2)[:, :, v], vecT[:, ROW[name]:ROW[name] + KD], ACT.Sigmoid)
            for c in range(RC):
                for g, dst, name in ((0, gr, "ga_b"), (1, gi, "gx_b")):
                    ps, free = get_a(act, "hy_gate", 2 * c + g)
                    f(dst[:, c, :], ps[:, 0:LAT], ACT.Sigmoid, bias=vec(name, c)).then_inc(free, 1)
            for n in range(6):
                ps, free = get_a(act, "idx", n)
                nk = (n // 2 + 2) * P
                if n >= 2:
                    act.wait_ge(S["relu_used"], n - 1)
                f(relu[:, n % 2, :, 0:nk], ps.rearrange("p (e c) -> p e c", e=2)[:, :, 0:nk], ACT.Relu).then_inc(free, 1)
            meet(act)
            
            def decay(u):
                if u == 0:
                    act.wait_ge(S["lam_set"], 1)
                if u < RC:
                    f(t2[:, u, :], gr[:, u, :], ACT.Tanh, scale=sp4[:, u:u + 1])
                    f(lru[:, u, :], gr[:, u, :], ACT.Exp, scale=sp8[:, u:u + 1])
                elif u == RC:
                    act.drain()
                    f(gr, t2, ACT.Sqrt).then_inc(S["sqrt_set"], 1)

            attention("dsa", lambda t: mixT0[:, RC + t, :], decay)
            meet(act)
            split_linear("hy_out", before=lambda: split_hi(mixT0, sH[LAT], LAT))
            layer_norm(0, xT, "ln1_b", 0, acc, sH[LAT], ahead=[("ple_g0", 0), ("ple_g0", 1)])
            ple(0)
            meet(act)
            mlp("mlp0", 0, LAT)
            meet(act)
            layer_norm(1, acc, "ln2_b", 0, xT)

            for m in range(4):
                ps, free = get_a(act, "mla_cq", m)
                f(cqT[:, m, :], ps[:, 0:LAT], ACT.Copy)
                f(sq1[:, m, :], ps[:, 0:LAT], ACT.Square).then_inc(free, 1)
            for m in range(2):
                ps, free = get_a(act, "mla_kv", m)
                f(ckvT[:, m, :], ps[:, 0:LAT], ACT.Copy)
                f(rt[:, m, :], ps[:, 0:LAT], ACT.Square).then_inc(free, 1)
            inverse_root("mla_sq", 0, rs1[:, 0, :], LAT, eps_rms, D / QL)
            inverse_root("mla_skv", 0, rs1[:, 1, :], LAT, eps_rms, D / KVL)
            scale = (NOPE + ROPE) ** -0.5
            for c in range(4):
                for m in range(2):
                    ps, free = get_a(act, "uq", 3 * c + m)
                    h = 4 * c + 2 * m
                    f(qf[0:64, h, :], ps[0:64, 0:LAT], ACT.Copy, scale=scale)
                    f(qf[0:64, h + 1, :], ps[64:128, 0:LAT], ACT.Copy, scale=scale).then_inc(free, 1)
                act.wait_ge(S["rot_set"], c + 1)
                for e in range(4):
                    ins = f(qf[64:96, 4 * c + e, :], rt[32 * e:32 * e + 32, 0, :], ACT.Copy, scale=scale)
                ins.then_inc(S["rot_used"], 1)
                if c == 0:
                    act.wait_ge(S["kr_set"], 1)
                for h in range(4 * c, 4 * c + 4):
                    f(kf[64:96, h, :], krt[0:32, 0, :], ACT.Copy)
            for c in range(4):
                for m in range(2):
                    ps, free = get_a(act, "ukv", 4 * c + m)
                    h = 4 * c + 2 * m
                    f(kf[0:64, h, :], ps[0:64, 0:LAT], ACT.Copy)
                    f(kf[0:64, h + 1, :], ps[64:128, 0:LAT], ACT.Copy).then_inc(free, 1)
            meet(act)
            attention("mla", lambda t: mixT1[:, t, :], out="mla_out")
            split_linear("mla_out", start=2)
            layer_norm(2, xT, "ln1_b", 8, acc, sH[LAT], ahead=[("ple_g1", 0), ("ple_g1", 1)])
            ple(1)
            meet(act)
            mlp("mlp1", 1, LAT)
            meet(act)
            for k in range(KD):
                f(squares[TOK][:, k, LAT:TOK], xT[:, k, LAT:TOK], ACT.Square)
            layer_norm(3, acc, "ln2_b", 8, xT, behind=lambda k: f(
                squares[TOK][:, k, 0:LAT], xT[:, k, 0:LAT], ACT.Square).then_inc(S["squared"], 1))

            rms(0, 0, 0, TOK, ab_raw, abH, ahead=[("ab", 0), ("ab", 1)])

            def ab_read(u):
                if u in AB_TILES["q"]:
                    ps, free = get_a(act, "ab", u)
                    f(qaT[:, u, :], ps[:, 0:TOK], ACT.Copy).then_inc(free, 1)
                elif u in AB_TILES["k"]:
                    ps, free = get_a(act, "ab", u)
                    f(kaT[:, u - 4, :], ps[:, 0:TOK], ACT.Copy, scale=P ** -0.5).then_inc(free, 1)
                elif u in AB_TILES["o"]:
                    ps, free = get_a(act, "ab", u)
                    f(oaT[:, u - 12, :], ps[:, 0:TOK], ACT.Sigmoid).then_inc(free, 1)
                elif u in AB_TILES["g"]:
                    ps, free = get_a(act, "ab", u)
                    act.wait_ge(bias_in, BIAS_IN)
                    for g in range(4):
                        dr, dst, b = g // 2, (gI, gF)[g % 2], (bI, bF)[g % 2]
                        lat, cx = ps[32 * g:32 * g + 4, 0:LAT], ps[32 * g:32 * g + 4, LAT:TOK]
                        if dr:
                            lat, cx = lat[:, ::-1], cx[:, ::-1]
                        f(dst[0:4, dr, CTX:TOK], lat, ACT.Identity, bias=b[:, dr:dr + 1])
                        ins = f(dst[0:4, dr, 0:CTX], cx, ACT.Identity, bias=b[:, dr:dr + 1])
                    ins.then_inc(free, 1)

            split_linear("ab", ab_read, AB_UNITS, start=2)
            meet(act)
            for t in range(6):
                ps, free = get_b(act, "ka", t)
                f(kaN[:, t, :], ps[:, 0:512], ACT.Copy).then_inc(free, 1)

            def head_norms(stage, first, n, tile, sq, rs):
                def square(m):
                    x = tile(m)
                    f(sq[:, m % 4, 0:x.shape[-1]], x, ACT.Square).then_inc(S["head_sq"], 1)

                square(0)
                square(1)
                for p in range(0, n, 2):
                    for m in range(p + 2, min(p + 4, n)):
                        square(m)
                    if p >= 2:
                        act.wait_ge(S["rope_raw"], first + p)
                    roots = [rs[:, m % 2, 0:tile(m).shape[-1]] for m in (p, p + 1)]
                    for m in (p, p + 1):
                        ps, free = get_a(act, stage, norm_product(n, m))
                        f(roots[m % 2], ps[:, 0:roots[m % 2].shape[-1]], ACT.Ln, bias=eps_rms).then_inc(free, 1)
                    act.drain()
                    for m in (p, p + 1):
                        f(roots[m % 2], roots[m % 2], ACT.Exp, scale=-0.5).then_inc(S["root_set"], 1)

            head_norms("ab_n", 0, 6, lambda m: qkb[:, m, :], sqb, rsb)
            meet(act)
            f(R0[0:4], gF[0:4], ACT.Abs)
            act.drain()
            f(R0[0:4], R0[0:4], ACT.Exp, scale=-1.0)
            act.drain()
            f(R3[0:4], R0[0:4], ACT.Ln, bias=C["pair"][0:4, 0:1]).then_inc(S["log_set"], 1)
            act.wait_ge(S["row_arg"], 1)
            f(crow, crow, ACT.Exp)
            meet(act)
            ps, free = get_b(act, "cols", 0)
            f(small[:, 308:452], ps[:, 0:144], ACT.Exp)
            f(small[:, 452:500], ps[:, 144:192], ACT.Copy).then_inc(free, 1)
            ps, free = get_a(act, "carry", 0)
            f(small[:, 500:548], ps[:, 0:48], ACT.Copy).then_inc(free, 1)
            meet(act)
            def hs_square(u):
                j, dr, h = lstm_units[u]
                t = LSTM_ORDER[dr][j]
                if lstm_last[t, h] == u:
                    act.wait_ge(S["hs_set"], u + 1)
                    f(qaT[:, h, t * P:t * P + P], hs[:, t, h, :], ACT.Square, accum_out=hss[:, 4 * t + h:4 * t + h + 1])

            def lstm_decay(u):
                if u >= 3:
                    hs_square(u - 3)
                j, dr, h = lstm_units[u]
                t = LSTM_ORDER[dr][j]
                act.wait_ge(S["lstm_d"], u + 1)
                f(lw[:, u % 2, 0, 0:P], lw[:, u % 2, 0, 0:P], ACT.Exp,
                  bias=gcol[:, 3, 6 * dr + t, h:h + 1]).then_inc(S["exp_arg"], 1)

            attention("sw", lambda n: mixT2[:, 4 + n, LAT:TOK] if n < 4 else mixT2[:, n, 0:LAT], lstm_decay)
            for u in range(len(lstm_units) - 3, len(lstm_units)):
                hs_square(u)
            act.drain()
            f(hrs, hss, ACT.Ln, scale=1.0 / P, bias=eps_rms)
            act.drain()
            f(hrs, hrs, ACT.Exp, scale=-0.5).then_inc(S["hs_sq"], 1)
            for k in range(KD):
                if k < A_H:
                    turned(act, "hs", 2 * k)
                    turned(act, "hs", 2 * k + 1)
                if k == A_H:
                    w_hi("ab_out", 0)
                    w_hi("ab_out", 1)
                f(sH[TOK][:, k, :], mixT2[:, k, 0:TOK], ACT.Copy).then_inc(S["act_hi"], 1)
            split_linear("ab_out", square_of("ab_out", TOK), start=2)
            rms(1, 0, 3, TOK, hraw, sH[TOK], ahead=[("mlp2", 0), ("mlp2", 1)])
            mlp("mlp2", 2, TOK)

            rms(2, 1, 0, TOK, hraw, sH[TOK], ahead=[("c_k", 0), ("c_k", 1)])
            c_units = [("c_k", m) for m in range(2)] + [("c_q", m) for m in range(8)]
            for n in range(len(c_units) + 2):
                if 2 <= n < len(c_units):
                    w_hi(*c_units[n])
                if n >= 2:
                    name, m = c_units[n - 2]
                    ps, free = get_a(act, name, m)
                    dst = kC[:, m, :] if name == "c_k" else qC[:, m, :]
                    f(dst, ps[:, 0:dst.shape[-1]], ACT.Copy).then_inc(free, 1)
            meet(act)
            head_norms("c_n", 6, 10, lambda m: qC[:, m, :] if m < 8 else kC[:, m - 8, :], sqc, rsc)
            meet(act)
            attention("cat", lambda t: mixT3[:, t, :], out="c_out")
            split_linear("c_out", square_of("c_out", LAT), start=2)
            rms(3, 1, 3, LAT, hraw, sH[LAT], ahead=[("mlp3", 0), ("mlp3", 1)])
            mlp("mlp3", 3, LAT)
            meet(act)

        @block.gpsimd
        def _(pool):
            meet(pool)
            nc.gpsimd.memset(gw, 0.0)
            pool.drain()
            for g, name in enumerate(("hy_ga_w", "hy_gx_w")):
                for e in range(2):
                    src = d[name][0].rearrange("(c e) i o -> e i c o", e=2)[e]
                    pool.dma_start(gw[64 * e:64 * e + 64, g, :, 64 * e:64 * e + 64], src).then_inc(gates_in, 16)
            meet(pool)
            for u, qt, h, _ in units("dsa"):
                n = (qt + 1) * P
                if u >= 2:
                    s, c = A("dsa", u - 2)
                    pool.wait_ge(a_ready[s], c + 1)
                if qt > 0 and h == 0:
                    pool.wait_ge(S["pens_set"], qt)
                b = biasb[:, u % 2, 0:n]
                slope = 2.0 ** (-8.0 * (h + 1) / DSA_H)
                nc.gpsimd.tensor_scalar(b, C["dist"][:, LAT - n:LAT], -slope, None, ALU.mult)
                pool.drain()
                pen = C["before"] if qt == 0 else pens[:, qt, 0:n]
                nc.gpsimd.tensor_tensor(b, b, pen, ALU.add).then_inc(S["bias_set"], 1)
            for _ in range(PRE_LSTM):
                meet(pool)
            for u, (j, dr, h) in enumerate(lstm_units):
                t = LSTM_ORDER[dr][j]
                if u >= 2:
                    pool.wait_ge(S["lstm_ready"], u - 1)
                nc.gpsimd.tensor_scalar(lw[:, u % 2, 2, 0:P], kaN[:, t, h * P:h * P + P],
                                        gcol[:, 2, 6 * dr + t, h:h + 1], None, ALU.mult).then_inc(S["kw_set"], 1)
            pool.wait_ge(S["act_split"], BASE_X["ab_out"] + KD)
            nc.gpsimd.memset(accs[TOK], 0.0).then_inc(S["acc_zero"], 1)
            for _ in range(BEFORE_MLP3):
                meet(pool)
            pool.wait_ge(S["act_split"], BASE_X["c_out"] + KD)
            nc.gpsimd.memset(accs[LAT], 0.0).then_inc(S["acc_zero"], 1)
            meet(pool)

        @block.vector
        def _(v):
            ts, tt, stt = nc.vector.tensor_scalar, nc.vector.tensor_tensor, nc.vector.scalar_tensor_tensor

            def log1p(z, s, s2, r):
                ts(s, z, 2.0, None, ALU.add)
                v.drain()
                nc.vector.reciprocal(s, s)
                v.drain()
                tt(s, s, z, ALU.mult)
                v.drain()
                tt(s2, s, s, ALU.mult)
                v.drain()
                ts(r, s2, 1.0 / 15, None, ALU.mult)
                for n in (13, 11, 9, 7, 5, 3):
                    v.drain()
                    stt(r, r, 1.0 / n, s2, ALU.add, ALU.mult)
                v.drain()
                stt(r, r, 1.0, s, ALU.add, ALU.mult)
                v.drain()

            def attention(name, beside=None):
                s = ATT[name]

                def finish(qt):
                    n = n_o[name] + rows_of_queries(name).index(qt)
                    H, dv = s["H"], s["dv"]
                    c = slice(qt * H, qt * H + H)
                    v.wait_ge(o_ready, n + 1)
                    if s["sink"]:
                        tt(rsum[:, c], rsum[:, c], sarg[:, c], ALU.add)
                        v.drain()
                    nc.vector.reciprocal(rinv[:, c], rsum[:, c])
                    v.drain()
                    for h in range(H):
                        ins = ts(s["onat"](qt)[:, h * dv:h * dv + dv], psO[:, h * dv:h * dv + dv],
                                 rinv[:, qt * H + h:qt * H + h + 1], None, ALU.mult)
                    ins.then_inc(o_free, 1)
                    v.drain().then_inc(S["onat_set"], 1)

                for u, qt, h, _ in units(name):
                    c, n = qt * s["H"] + h, s["nkb"](qt) * P
                    if beside and name == "sw":
                        beside[0](u)
                    ps, _ = get_a(v, *unit_product(name, u))
                    ins = None
                    for a, b, m in s["masks"](qt, h):
                        ins = tt(ps[:, a:b], ps[:, a:b], m, ALU.add)
                    if ins is not None:
                        v.drain()
                    ins = nc.vector.tensor_reduce(nmax[:, c:c + 1], ps[:, 0:n], AX.X, ALU.max, negate=True)
                    if s["sink"]:
                        v.drain()
                        ins = tt(nmax[:, c:c + 1], nmax[:, c:c + 1], nsink[:, h:h + 1], ALU.min)
                    ins.then_inc(S[name + "_max"], 1)
                    if h == 1 and u > 1:
                        rows = rows_of_queries(name)
                        finish(rows[rows.index(qt) - 1])
                    if beside and name == "sw":
                        beside[1](u)
                    elif beside:
                        beside(qt, h)
                finish(rows_of_queries(name)[-1])

            def w_lo(stage, u, g=0):
                v.wait_ge(S["w_hi"], g * UNITS + (BASE_W[stage] + u + 1))
                tt(split_target(wL, stage, u), unit(v, stage, u, g), split_target(wH, stage, u),
                   ALU.subtract).then_inc(S["w_split"], 1)

            def x_lo(name, k, x, hi, lo):
                v.wait_ge(S["act_hi"], BASE_X[name] + k + 1)
                tt(lo[:, k, :], x[:, k, 0:lo.shape[-1]], hi[:, k, :], ALU.subtract).then_inc(S["act_split"], 1)

            def split_linear(stage, evacuate=None, units=KD, before=None, start=0):
                for u in range(units + 2):
                    if start <= u < units:
                        w_lo(stage, u)
                    if u == 1 and before:
                        before()
                    if u >= 2 and evacuate:
                        evacuate(u - 2)

            def layer_norm(i, x, gain, j0, dst, split=None, ahead=()):
                if i % 2:
                    ps, free = get_a(v, f"ln_m{i}", 0)
                else:
                    v.wait_ge(S["sum_ready"], i // 2 + 1)
                    ps, free = psO, S["mean_read"]
                for k in range(KD):
                    ins = tt(x[:, k, 0:LAT], x[:, k, 0:LAT], ps[:, 0:LAT], ALU.subtract)
                    ins.then_inc(S["centered"], 1)
                v.drain().then_inc(free, 1)
                for a in ahead:
                    w_lo(*a)
                emptied(v, f"ln_v{i}", 0)
                for k in range(KD):
                    stt(dst[:, k, 0:LAT], x[:, k, 0:LAT], vec(gain, j0 + k), rstd[:, 0:LAT], ALU.mult,
                        ALU.mult).then_inc(S["norm_set"], 1)
                    if split and k >= 1:
                        x_lo(split, k - 1, dst, sH[LAT], sL[LAT])
                if split:
                    x_lo(split, KD - 1, dst, sH[LAT], sL[LAT])

            def rms(i, layer, norm, first, n, dst, split=None, ahead=(), hi=None, lo=None):
                for k in range(KD):
                    ts(aff[:, k, :], mod[:, layer, (first + 1) * KD + k, :], 1.0, vec(norm, 8 * layer + k),
                       ALU.add, ALU.mult)
                v.drain()
                for a in ahead:
                    w_lo(*a)
                if i % 2 == 0:
                    emptied(v, f"rms{i}", 0)
                else:
                    v.wait_ge(S["sum_read"], (i + 1) // 2)
                hi, lo = (sH[n], sL[n]) if hi is None else (hi, lo)
                spans = [(0, LAT, 0)] + ([(LAT, n, 1)] if n > LAT else [])
                for k in range(KD):
                    for a, b, e in spans:
                        ins = stt(dst[:, k, a:b], xT[:, k, a:b], aff[:, k, e:e + 1], rstd[:, a:b], ALU.mult, ALU.mult)
                    ins.then_inc(S["norm_set"], 1)
                    if split and k >= 1:
                        x_lo(split, k - 1, dst, hi, lo)
                if split:
                    x_lo(split, KD - 1, dst, hi, lo)

            def residual(stage, mix):
                def add(m):
                    ps, free = get_a(v, stage, m)
                    stt(xT[:, m, 0:LAT], xT[:, m, 0:LAT], ALPHA, ps[:, 0:LAT], ALU.mult, ALU.add).then_inc(free, 1)

                split_linear(stage, add, before=lambda: [x_lo(stage, k, mix, sH[LAT], sL[LAT]) for k in range(KD)])

            def gated(stage, layer, n, mix=None):
                spans = [(0, LAT, 0)] + ([(LAT, n, 1)] if n > LAT else [])

                def add(m):
                    ps, free = get_a(v, stage, m)
                    for a, b, e in spans:
                        ins = stt(xT[:, m, a:b], ps[:, a:b], mod[:, layer, 2 * KD + m, e:e + 1], xT[:, m, a:b],
                                  ALU.mult, ALU.add)
                    ins.then_inc(free, 1)

                if mix is None:
                    split_linear(stage, add, start=2)
                else:
                    split_linear(stage, add, before=lambda: [x_lo(stage, k, mix, sH[n], sL[n]) for k in range(KD)])

            def ple(l):
                split_linear(f"ple_g{l}", start=2)
                for j in range(KD):
                    emptied(v, f"ple_g{l}", j)
                    ps, free = get_a(v, f"ple_p{l}", j)
                    tt(gates[:, j, :], gates[:, j, :], ps[:, 0:LAT], ALU.mult).then_inc(free, 1)
                    v.drain()
                    stt(acc[:, j, :], acc[:, j, :], ALPHA, gates[:, j, :], ALU.mult, ALU.add)
                w_lo(f"mlp{l}", 0)
                w_lo(f"mlp{l}", 1)

            def mlp(name, index, n):
                acc = accs[n]

                def part(i, last):
                    more = i * ((GH + KD) // 2)

                    def hidden_lo(m):
                        v.wait_ge(S["g_hi"], i * GH + (index * GH * GROUPS + m + 1))
                        tt(gL[n][:, m, :], hid[n][:, m % 2, :], gH[n][:, m, :], ALU.subtract).then_inc(S["hidden_set"], 1)

                    def add_up(j):
                        ps, free = get_a(v, name, GH + j, more)
                        tt(acc[:, j, :], acc[:, j, :], ps[:, 0:n], ALU.add).then_inc(free, 1)
                        if last and name in RESIDUAL:
                            v.drain()
                            for a, b, e in [(0, LAT, 0)] + ([(LAT, n, 1)] if n > LAT else []):
                                ins = stt(xT[:, j, a:b], acc[:, j, a:b], mod[:, RESIDUAL[name], 5 * KD + j, e:e + 1],
                                          xT[:, j, a:b], ALU.mult, ALU.add)
                            ins.then_inc(S["residual_set"], 1)

                    def modulations(k):
                        if name not in ADA:
                            return
                        l, e, r = ADA[name], k // (KD // 2), k % (KD // 2)
                        if r == 0:
                            v.wait_ge(ada_landed[e], i * 16 + (16 * GROUPS * l + 16))
                        for x in range(2):
                            c = silu[:, 2 * k + x:2 * k + x + 1]
                            if k == 0:
                                ts(adas[:, x, :], adaw[:, e, r, :], c, None, ALU.mult)
                            else:
                                ins = stt(adas[:, x, :], adaw[:, e, r, :], c, adas[:, x, :], ALU.mult, ALU.add)
                        if r == KD // 2 - 1:
                            ins.then_inc(S["ada_used"], 1)
                        if k == KD - 1:
                            v.drain().then_inc(S["ada_sum"], 1)
                        else:
                            v.drain()

                    modulations(0)
                    modulations(1)
                    for m in range(GH):
                        if m < GH - 1:
                            w_lo(name, m + 2, i)
                        hidden_lo(m)
                        modulations(2 + m)
                    w_lo(name, GH + 1, i)
                    for q in range(GH - 1):
                        add_up(2 * q)
                        add_up(2 * q + 1)
                        if q < GH - 2:
                            w_lo(name, GH + 2 + q, i)
                        elif not last:
                            w_lo(name, 0, i + 1)
                        if q < 2:
                            modulations(6 + q)
                    add_up(KD - 2)
                    add_up(KD - 1)
                    if not last:
                        w_lo(name, 1, i + 1)
                    if name in ADA:
                        v.wait_ge(S["row_turned"], i + (GROUPS * ADA[name] + 1))
                        nc.vector.tensor_copy(mod[:, ADA[name], bass.ds(i * (MC // P), MC // P), :],
                                              psB[:, 0, 0:2 * MC // P].rearrange("p (a b) -> p a b", b=2))
                    v.drain()

                if index >= 2:
                    v.wait_ge(S["acc_zero"], index - 1)
                with v.Fori(0, GROUPS - 1) as i:
                    part(i, False)
                part(GROUPS - 1, True)
                if name in ADA:
                    l = ADA[name]
                    b = vecT[:, ROW["ada_b"] + 48 * l:ROW["ada_b"] + 48 * l + 48]
                    for x in range(2):
                        tt(mod[:, l, :, x], mod[:, l, :, x], b, ALU.add)

            for k in range(KD):
                ps, free = get_b(v, "load", k)
                nc.vector.tensor_copy(xT[:, k, 0:LAT], ps).then_inc(free, 1)
            w_lo("hy_xr", 0)
            w_lo("hy_xr", 1)
            meet(v)

            nc.vector.memset(xpad[:, :, 0:3], 0.0)
            hy_units = [(name, m) for name in ("hy_xr", "hy_yr", "hy_q", "hy_ki") for m in range(4)]

            def prepare():
                v.wait_ge(bias_in, BIAS_IN)
                ts(nsink, sink, -1.0, None, ALU.mult)
                ts(bq8, vec("bq", 0), B_D ** -0.5, None, ALU.mult)
                ts(cq8, vec("cq", 0), P ** -0.5, None, ALU.mult)
                v.wait_ge(S["lam_exp"], 1)
                log1p(lz, ls, ls2, lacc)
                ts(ls, vecT[:, ROW["lam"]:ROW["lam"] + 4], -1.0, 0.0, ALU.mult, ALU.max)
                v.drain()
                stt(sp4, lacc, 2.0, ls, ALU.mult, ALU.add)
                v.drain()
                ts(sp8, sp4, -2 * LRU_HALF, None, ALU.mult)
                ts(sp4, sp4, LRU_HALF, None, ALU.mult).then_inc(S["lam_set"], 1)

            def convolve(c):
                emptied(v, "hy_xr", c)
                ts(xc[:, c, :], xpad[:, c, 0:LAT], vec("conv_w", c), vec("conv_b", c), ALU.mult, ALU.add)
                for i in range(1, 4):
                    v.drain()
                    stt(xc[:, c, :], xpad[:, c, i:i + LAT], vec("conv_w", RC * i + c), xc[:, c, :], ALU.mult, ALU.add)
                if c == RC - 1:
                    v.drain().then_inc(S["conv_set"], 1)

            for n, (name, m) in enumerate(hy_units):
                if n >= 2:
                    w_lo(name, m)
                if n == 1:
                    for k in range(KD):
                        x_lo("hy", k, xT, xH, xL)
                if n == 9:
                    ps, free = get_b(v, "load", 8)
                    nc.vector.tensor_copy(vecT[:, :], ps[:, 0:NROW]).then_inc(free, 1)
                    v.drain()
                if 10 <= n < 10 + RC:
                    convolve(n - 10)
                if n == 14:
                    prepare()
            for m in range(3):
                ps, free = get_a(v, "hy_ki", m)
                nc.vector.tensor_copy(kT if m == 0 else iqT[:, m - 1, :], ps[:, 0:LAT]).then_inc(free, 1)
            ps, free = get_a(v, "hy_ki", 3)
            nc.vector.tensor_copy(ikT, ps[:, 0:LAT]).then_inc(free, 1)
            ps, free = get_a(v, "hy_v", 0)
            ps = ps[:, 0:4 * 68].rearrange("p (t c) -> p t c", c=68)
            nc.vector.tensor_copy(vN, ps[:, :, 0:64])
            ts(iw, ps[:, :, 64:68], IDX_H ** -0.5 * IDX_D ** -0.5, None, ALU.mult).then_inc(free, 1)
            for k in range(0, KD, 2):
                ps, free = get_b(v, "load", 9 + k // 2)
                nc.vector.tensor_copy(xT[:, k:k + 2, LAT:TOK], ps.rearrange("p (a b) -> p a b", a=2)).then_inc(free, 1)
            for l in range(2):
                for k in range(2):
                    ps, free = get_b(v, "load", 13 + 2 * l + k)
                    nc.vector.tensor_copy(pT[:, l, k, :], ps).then_inc(free, 1)
            v.wait_ge(const_in, 16)
            for qt in range(1, LT):
                nk = (qt + 1) * P
                s = isc[:, qt, 0:nk]
                for hp in range(2):
                    n = 2 * (qt - 1) + hp
                    emptied(v, "idx", n)
                    for e in range(2):
                        h = 2 * hp + e
                        if h == 0:
                            ts(s, relu[:, n % 2, 0, 0:nk], iw[:, qt, 0:1], None, ALU.mult)
                        else:
                            ins = stt(s, relu[:, n % 2, e, 0:nk], iw[:, qt, h:h + 1], s, ALU.mult, ALU.add)
                            if e == 1:
                                ins.then_inc(S["relu_used"], 1)
                        v.drain()
                tt(s[:, qt * P:nk], s[:, qt * P:nk], C["before"], ALU.add)
            def recur(c):
                if c == 0:
                    v.wait_ge(S["sqrt_set"], 1)
                tt(gi[:, c, :], gi[:, c, :], xc[:, c, :], ALU.mult)
                stt(gr[:, c, :], lru[:, c, :], 1.0, gr[:, c, :], ALU.add, ALU.mult)
                v.drain()
                tt(gi[:, c, :], gi[:, c, :], gr[:, c, :], ALU.mult)
                v.drain()
                nc.vector.tensor_tensor_scan(xc[:, c, :], lru[:, c, :], gi[:, c, :], 0.0, ALU.mult, ALU.add)
                v.drain()
                tt(mixT0[:, c, :], xc[:, c, :], yg[:, c, :], ALU.mult)

            def pick_keys(qt, h):
                if qt + 1 == LT:
                    if h % 2:
                        recur(h // 2)
                    return
                nk = (qt + 2) * P
                s = isc[:, qt + 1, 0:nk]
                for _ in range((3, 3, 3, 3, 2, 2, 0, 0)[h]):
                    nc.vector.max(m8, s)
                    v.drain()
                    nc.vector.match_replace(s, m8, s, TAKEN)
                    v.drain()
                if h == 5:
                    pen = pens[:, qt + 1, 0:nk]
                    ts(pen, s, TAKEN, 1.0, ALU.is_equal, ALU.subtract)
                    v.drain()
                    ts(pen, pen, -NEG, None, ALU.mult).then_inc(S["pens_set"], 1)

            meet(v)
            s16 = silu.rearrange("p (k v) -> p k v", v=2)
            for e, name in enumerate(("c", "c_ctx")):
                tt(s16[:, :, e], s16[:, :, e], vecT[:, ROW[name]:ROW[name] + KD], ALU.mult)
            attention("dsa", pick_keys)
            meet(v)
            residual("hy_out", mixT0)
            layer_norm(0, xT, "ln1_g", 0, acc, "mlp0", ahead=[("ple_g0", 0), ("ple_g0", 1)])
            ple(0)
            meet(v)
            mlp("mlp0", 0, LAT)
            meet(v)
            layer_norm(1, acc, "ln2_g", 0, xT)

            def latent(j, t, n, name, stage):
                emptied(v, stage, 0)
                for k in range(n):
                    stt(t[:, k, :], t[:, k, :], vec(name, k), rs1[:, j, :], ALU.mult,
                        ALU.mult).then_inc(S["latent_set"], 1)

            latent(0, cqT, 4, "q_norm", "mla_sq")
            ps, free = get_a(v, "mla_kr", 0)
            tt(krt[0:32, 0, :], ps[0:32, 0:512], C["cosM"][0:32], ALU.mult)
            tt(krt[0:32, 1, :], ps[0:32, 512:1024], C["sinM"][0:32], ALU.mult).then_inc(free, 1)
            v.drain()
            tt(krt[0:32, 0, :], krt[0:32, 0, :], krt[0:32, 1, :], ALU.add).then_inc(S["kr_set"], 1)
            latent(1, ckvT, 2, "kv_norm", "mla_skv")
            for c in range(4):
                ps, free = get_a(v, "uq", 3 * c + 2)
                if c >= 1:
                    v.wait_ge(S["rot_used"], c)
                tt(rt[:, 0, :], ps[:, 0:512], C["cosM"], ALU.mult)
                tt(rt[:, 1, :], ps[:, 512:1024], C["sinM"], ALU.mult).then_inc(free, 1)
                v.drain()
                tt(rt[:, 0, :], rt[:, 0, :], rt[:, 1, :], ALU.add).then_inc(S["rot_set"], 1)
            for c in range(4):
                for m in range(2):
                    ps, free = get_a(v, "ukv", 4 * c + 2 + m)
                    nc.vector.tensor_copy(vM[:, 2 * m:2 * m + 2, 256 * c:256 * c + 256],
                                          ps[:, 0:512].rearrange("p (e c) -> p e c", e=2)).then_inc(free, 1)
            meet(v)
            attention("mla")
            residual("mla_out", mixT1)
            layer_norm(2, xT, "ln1_g", 8, acc, "mlp1", ahead=[("ple_g1", 0), ("ple_g1", 1)])
            ple(1)
            meet(v)
            mlp("mlp1", 1, LAT)
            meet(v)
            layer_norm(3, acc, "ln2_g", 8, xT)
            rms(0, 0, "norm1", 0, TOK, ab_raw, "ab", ahead=[("ab", 0), ("ab", 1)], lo=abL, hi=abH)

            def ab_read(u):
                if u in AB_TILES["v"]:
                    ps, free = get_a(v, "ab", u)
                    nc.vector.tensor_copy(vaT[u - 8], ps[:, 0:TOK]).then_inc(free, 1)
                elif u in AB_TILES["qb"] or u in AB_TILES["kb"]:
                    ps, free = get_a(v, "ab", u)
                    nc.vector.tensor_copy(qkb[:, u - 16, :], ps[:, 0:TOK]).then_inc(free, 1)
                elif u in AB_TILES["vb"]:
                    ps, free = get_a(v, "ab", u)
                    nc.vector.tensor_copy(vbT[0], ps[:, 0:LAT])
                    nc.vector.tensor_copy(vbT[1], ps[:, LAT:TOK]).then_inc(free, 1)

            split_linear("ab", ab_read, AB_UNITS, start=2)
            meet(v)

            def head_norms(stage, first, n, tile, rs, tmp, gain, cos, sin):
                def normalize(m):
                    x = tile(m)
                    v.wait_ge(S["root_set"], first + m + 1)
                    stt(x, x, gain(m), rs[:, m % 2, 0:x.shape[-1]], ALU.mult, ALU.mult).then_inc(S["rope_raw"], 1)

                normalize(0)
                normalize(1)
                for p in range(0, n, 2):
                    for m in range(p + 2, min(p + 4, n)):
                        normalize(m)
                    for m in (p, p + 1):
                        ps, free = get_a(v, stage, rope_product(n, m))
                        x = tile(m)[:, 0:LAT]
                        tt(tmp[:, m % 2, :], ps[:, 0:LAT], sin, ALU.mult).then_inc(free, 1)
                        tt(x, x, cos, ALU.mult)
                        v.drain()
                        tt(x, x, tmp[:, m % 2, :], ALU.add)
                v.drain()

            nc.vector.memset(vaN[:, :, :, P:P + 1], 1.0)
            for t in range(6):
                ps, free = get_b(v, "va", t)
                nc.vector.tensor_copy(vaN[:, t, :, 0:P], ps.rearrange("p (h c) -> p h c", h=A_H)).then_inc(free, 1)
            for e, n in enumerate((LT, CT)):
                ps, free = get_b(v, "vb", e)
                nc.vector.tensor_copy(vb[:, LT * e:LT * e + n, :],
                                      ps[:, 0:n * P].rearrange("p (t c) -> p t c", c=P)).then_inc(free, 1)
            head_norms("ab_n", 0, 6, lambda m: qkb[:, m, :], rsb, rtb,
                       lambda m: bq8 if m < 4 else vec("bk", 0), C["cosB"], C["sinB"])
            meet(v)
            v.wait_ge(S["log_set"], 1)
            z, s, s2, r = (x[0:4] for x in (R0, R1, R2, R3))
            lf, gi_ = gF[0:4], gI[0:4]
            ts(lf, lf, 0.0, None, ALU.min)
            nc.vector.memset(z, 1.0)
            v.drain()
            tt(lf, lf, r, ALU.subtract)
            nc.vector.memset(z.rearrange("p a (c t) -> p a c t", t=P)[:, :, :, 0:1], 0.0)
            nc.vector.memset(mrow, 0.0)
            v.drain()
            flat = lambda x: x.rearrange("p a b -> p (a b)")
            nc.vector.tensor_tensor_scan(flat(s), flat(z), flat(lf), 0.0, ALU.mult, ALU.add)
            v.drain()
            tt(gi_, gi_, s, ALU.subtract)
            v.drain()
            for j in range(6):
                for dr in range(2):
                    a, b = j * P, j * P + P
                    nc.vector.tensor_tensor_scan(s2[:, dr, a:b], gi_[:, dr, a:b], gi_[:, dr, a:b],
                                                 mrow[:, dr, j:j + 1], ALU.max, ALU.max)
                v.drain()
                for dr in range(2):
                    tt(mrow[:, dr, j + 1:j + 2], s[:, dr, b - 1:b], s2[:, dr, b - 1:b], ALU.add)
                v.drain()
            last = s2.rearrange("p a (c t) -> p a c t", t=P)[:, :, :, P - 1]
            tt(crow, mrow[:, :, 0:6], last, ALU.subtract)
            for j in range(6):
                for dr in range(2):
                    a, b, t = j * P, j * P + P, LSTM_ORDER[dr][j]
                    step = -1 if dr else 1
                    g, m, total = (x[:, dr, a:b][:, ::step] for x in (gi_, s2, s))
                    to = slice(t * P, t * P + P)
                    ts(r[:, dr, to], m, -1.0, mrow[:, dr, j:j + 1], ALU.mult, ALU.add)
                    ts(lf[:, dr, to], g, s2[:, dr, b - 1:b], None, ALU.subtract)
                    stt(z[:, dr, to], total, -1.0, m, ALU.mult, ALU.subtract)
                    ts(peak[0:4, dr, to], m, -1.0, None, ALU.mult)
            v.drain()
            for j in range(6):
                for dr in range(2):
                    t = LSTM_ORDER[dr][j]
                    nc.vector.tensor_copy(s[:, dr, t * P:t * P + P], gi_[:, dr, j * P:j * P + P][:, ::-1 if dr else 1])
            v.drain().then_inc(S["row_arg"], 1)
            meet(v)
            meet(v)
            nc.vector.memset(hs, 0.0)
            nc.vector.memset(Cn, 0.0)
            v.drain().then_inc(S["state_set"], 1)
            pen = (C["after"], C["before"])

            def lstm_score(u):
                j, dr, h = lstm_units[u]
                ps, free = get_a(v, "mix", 2 * u)
                v.wait_ge(S["exp_arg"], u + 1)
                if u >= 2:
                    v.wait_ge(S["lstm_ready"], u - 1)
                tt(lw[:, u % 2, 1, 0:P], ps[:, 0:P], lw[:, u % 2, 0, 0:P], ALU.mult).then_inc(S["score_set"], 1)
                t = LSTM_ORDER[dr][j]
                ts(lw[:, u % 2, 3, :], ps[:, 512:512 + P + 1], gcol[:, 0, 6 * dr + t, h:h + 1], None,
                   ALU.mult).then_inc(free, 1)

            def lstm_out(u):
                j, dr, h = lstm_units[u]
                t = LSTM_ORDER[dr][j]
                v.wait_ge(S["lstm_ready"], u + 1)
                num = lw[:, u % 2, 3, :]
                tt(num, num, psO[:, 512:512 + P + 1], ALU.add)
                stt(Cn[:, dr, h, :], Cn[:, dr, h, :], carry[:, h, 6 * dr + j:6 * dr + j + 1], psO[:, 768:768 + P + 1],
                    ALU.mult, ALU.add).then_inc(S["lstm_free"], 1)
                v.drain().then_inc(S["state_set"], 1)
                stt(den[:, 0:1], num[:, P:P + 1], -1.0, num[:, P:P + 1], ALU.mult, ALU.max)
                v.drain()
                tt(den[:, 0:1], den[:, 0:1], gcol[:, 1, 6 * dr + t, h:h + 1], ALU.max)
                v.drain()
                nc.vector.reciprocal(den[:, 1:2], den[:, 0:1])
                v.drain()
                stt(hs[:, t, h, :], num[:, 0:P], den[:, 1:2], hs[:, t, h, :], ALU.mult, ALU.add).then_inc(S["hs_set"], 1)

            def lstm_first(u):
                j, dr, h = lstm_units[u]
                ps, _ = get_a(v, "mix", 2 * u)
                tt(lw[:, u % 2, 0, 0:P], ps[:, P:2 * P], pen[dr], ALU.add).then_inc(S["lstm_d"], 1)

            def lstm_rest(u):
                lstm_score(u)
                if u >= 1:
                    lstm_out(u - 1)

            attention("sw", (lstm_first, lstm_rest))
            v.drain()
            lstm_out(len(lstm_units) - 1)
            v.drain()
            v.wait_ge(S["hs_sq"], 1)
            for h in range(A_H):
                for t in range(6):
                    ins = ts(hs[:, t, h, :], hs[:, t, h, :], hrs[:, 4 * t + h:4 * t + h + 1], None, ALU.mult)
                ins.then_inc(S["hs_normed"], 1)
            for h in range(A_H):
                for e, (a, b) in enumerate(((0, LAT), (LAT, TOK))):
                    ps, free = get_b(v, "hs", 2 * h + e)
                    stt(mixT2[:, h, a:b], ps[:, 0:b - a], vec("a_norm", h), oaT[:, h, a:b], ALU.mult,
                        ALU.mult).then_inc(free, 1)
            for k in range(A_H):
                x_lo("ab_out", k, mixT2, sH[TOK], sL[TOK])
            w_lo("ab_out", 0)
            w_lo("ab_out", 1)
            for k in range(A_H, KD):
                x_lo("ab_out", k, mixT2, sH[TOK], sL[TOK])
            gated("ab_out", 0, TOK)
            rms(1, 0, "norm2", 3, TOK, hraw, "mlp2", ahead=[("mlp2", 0), ("mlp2", 1)])
            mlp("mlp2", 2, TOK)

            rms(2, 1, "norm1", 0, TOK, hraw, "cin", ahead=[("c_k", 0), ("c_k", 1)])
            for g in range(2):
                n = 4 if g == 0 else 2
                ps, free = get_a(v, "c_v", g)
                nc.vector.tensor_copy(vC[:, 4 * g:4 * g + n, :],
                                      ps[:, 0:256 * n].rearrange("p (t c) -> p t c", c=256)).then_inc(free, 1)
            for u in range(8):
                w_lo("c_q", u)
            meet(v)
            head_norms("c_n", 6, 10, lambda m: qC[:, m, :] if m < 8 else kC[:, m - 8, :], rsc, rtc,
                       lambda m: cq8 if m < 8 else vec("ck", 0), C["cosC"], C["sinC"])
            meet(v)
            attention("cat")
            gated("c_out", 1, LAT, mixT3)
            rms(3, 1, "norm2", 3, LAT, hraw, "mlp3", ahead=[("mlp3", 0), ("mlp3", 1)])
            mlp("mlp3", 3, LAT)
            for t in range(LT):
                for e in range(2):
                    ps, free = get_b(v, "out", 2 * t + e)
                    nc.vector.tensor_copy(xn[:, t, 512 * e:512 * e + 512], ps).then_inc(free, 1)
                v.drain().then_inc(out_set, 1)
            meet(v)

        assert len(set(met.values())) == 1, met


LRU_HALF = 8.0 / 2
PRE_LSTM, BEFORE_MLP3 = 10, 2


def host_constants():
    import numpy as np
    c = np.zeros((P, NCONST), np.float32)

    def put(name, a):
        lo, hi = CONST[name]
        c[:a.shape[0], lo:hi] = a

    i = np.arange(P)
    put("ident", np.eye(P))
    put("mean", np.full((P, P), 1 / D))
    put("mean128", np.full((P, P), 1 / P))
    put("mean64", (i[:, None] // 64 == i[None] // 64) / 64)
    for name, w in (("rot64", 64), ("rot128", 128)):
        r = np.zeros((P, P))
        for o in range(P):
            b, e = o // w * w, o % w
            if e < w // 2:
                r[b + e + w // 2, o] = -1
            else:
                r[b + e - w // 2, o] = 1
        put(name, r)
    put("after", np.where(i[:, None] <= i[None], 0.0, NEG))
    put("before", np.where(i[:, None] >= i[None], 0.0, NEG))
    put("dist", (LAT - P + i[:, None] - np.arange(LAT)[None]) * 1.0)
    pick = np.zeros((4, 4, P))
    for h in range(4):
        pick[h, h] = 1
    put("pick", pick.reshape(4, 4 * P))
    f = np.float32

    def axial(dim):
        rows = LAT // 64
        row = np.repeat(np.arange(rows), 64).astype(f)
        col = np.tile(np.arange(64), rows).astype(f)
        n = dim // 4
        inv = f(10000.0) ** (-np.arange(n, dtype=f) / f(n))
        ang = np.concatenate([row[:, None] * inv, col[:, None] * inv], -1)
        return np.cos(ang).T, np.sin(ang).T

    for name, dim in (("B", 64), ("C", 128)):
        cs, sn = axial(dim)
        put("cos" + name, np.tile(cs, (P // (dim // 2), 1)))
        put("sin" + name, np.tile(sn, (P // (dim // 2), 1)))
    freq = f(10000.0) ** (-np.arange(0, ROPE, 2, dtype=f) / f(ROPE))
    ang = (np.arange(LAT, dtype=f)[:, None] * freq[None]).T
    cs, sn = np.cos(ang), np.sin(ang)
    put("cosM", np.tile(np.concatenate([cs, cs]), (4, 1)))
    put("sinM", np.tile(np.concatenate([-sn, sn]), (4, 1)))
    put("eps", np.tile(np.array([[LN_EPS, RMS_EPS]]), (P, 1)))
    put("pair", np.tile(np.array([[1, 0, 0, 1]]), (P, 1)))
    return c


_INS = ["x", "p", "ln1_g", "ln1_b", "ln2_g", "ln2_b", "mlp_w1", "mlp_w2", "ple_w_proj", "ple_w_gate", "hy_w_in",
        "hy_conv_w", "hy_conv_b", "hy_ga_w", "hy_ga_b", "hy_gx_w", "hy_gx_b", "hy_lambda", "hy_w_out", "mla_w_down",
        "mla_q_norm", "mla_kv_norm", "mla_w_uq", "mla_w_ukv", "mla_w_out", "c_2", "ctx_2", "c_ctx_2", "ada_w_2",
        "ada_b_2", "norm1_g_2", "norm2_g_2", "ab_w_in_2", "ab_gate_b_2", "mlstm_norm_g_2", "swa_q_norm_g_2",
        "swa_k_norm_g_2", "swa_sink_2", "ab_w_out_2", "c_w_in_2", "c_q_norm_g_2", "c_k_norm_g_2", "c_w_out_2",
        "mlp_w1_2", "mlp_w2_2"]


def kernel(**inputs):
    import numpy as _np
    import concourse.bacc as _bacc
    from concourse import mybir as _mybir
    from concourse.bass_utils import run_bass_kernel_spmd as _run

    nc = _bacc.Bacc("TRN2", target_bir_lowering=False, num_devices=1)
    arrays, args = {}, {}
    for name in _INS:
        a = _np.ascontiguousarray(inputs[name])
        arrays[f"in_{name}_dram"] = a
        args[name] = nc.dram_tensor(f"in_{name}_dram", a.shape, _mybir.dt.from_np(a.dtype), kind="ExternalInput").ap()
    c = host_constants()
    arrays["shape_constants_dram"] = c
    consts = nc.dram_tensor("shape_constants_dram", c.shape, _mybir.dt.float32, kind="ExternalInput").ap()
    out = nc.dram_tensor("out_0_dram", (1, LAT, D), _mybir.dt.float32, kind="ExternalOutput").ap()
    build(nc, args, consts, out)
    r = _run(nc, [arrays], core_ids=[0])
    return r.results[0]["out_0_dram"]
```
